# Optimizing a Trainium2 kernel written in Bass

```python
import jax, jax.numpy as jnp
from jax import lax
import numpy as np

D_MODEL = 1024
BATCH = 1
SEQ = 512
DEPTH = 2
DEC_BATCH = 1
DEC_SEQ = 64
PAST_LEN = 128

CHUNK = 64
N_META = 16
N_AB = (DEPTH + 1) // 2
N_POOL = DEPTH // 2
A_HEADS = 4
A_DK = 128
A_DV = 128
A_KW = A_HEADS * A_DK
A_VW = A_HEADS * A_DV
B_HEADS = 4
B_DH = 128
B_QW = B_HEADS * B_DH
IDX_HEADS = 4
IDX_DIM = 64
TOPK_MAX = 256
Q_BLOCK = 128
MIX_W = A_VW + B_QW
IN_SPLITS = (A_KW, A_KW, A_VW, A_VW, B_QW, B_DH, B_DH, IDX_HEADS * IDX_DIM, IDX_DIM, IDX_HEADS)
IN_COLS = sum(IN_SPLITS)
ROPE_THETA = 500000.0
ROT_FRAC = 4
POOL_WINDOWS = (2, 4, 8, 16)
POOL_GROUP = D_MODEL // len(POOL_WINDOWS)
POOL_HIST = max(POOL_WINDOWS) - 1
D_FF = 2816
RMS_EPS = 1e-6
NEG_BIG = -1e30

kernel_name = 'hybrid_streaming_hgrn2_dsa_pool_step'

def rms_norm(x, g):
    xf = x.astype(jnp.float32)
    y = xf * lax.rsqrt(jnp.mean(xf * xf, axis=-1, keepdims=True) + RMS_EPS)
    return (y * g.astype(jnp.float32)).astype(x.dtype)

def swiglu(u, wg, wu, wd):
    return (jax.nn.silu(u @ wg) * (u @ wu)) @ wd

def rope_partial(x, pos):
    d = x.shape[-1]
    r = d // ROT_FRAC
    half = r // 2
    inv = ROPE_THETA ** (-jnp.arange(half, dtype=jnp.float32) / half)
    ang = pos.astype(jnp.float32)[:, None] * inv[None, :]
    cos = jnp.cos(ang)[None, :, None, :]
    sin = jnp.sin(ang)[None, :, None, :]
    xf = x.astype(jnp.float32)
    x1, x2, rest = xf[..., :half], xf[..., half:r], xf[..., r:]
    return jnp.concatenate([x1 * cos - x2 * sin, x2 * cos + x1 * sin, rest], axis=-1).astype(x.dtype)

def hgrn2_recurrence(q, k, v, log_f, s0):
    B, H, T, _ = q.shape
    nc = -(-T // CHUNK)
    pad = nc * CHUNK - T

    def blk(a):
        a = jnp.pad(a, ((0, 0), (0, 0), (0, pad), (0, 0)))
        return a.reshape(B, H, nc, CHUNK, a.shape[-1]).transpose(2, 0, 1, 3, 4)

    causal = jnp.tril(jnp.ones((CHUNK, CHUNK), dtype=bool))[:, :, None]

    def step(s, inp):
        qc, kc, vc, gc = inp
        b = jnp.cumsum(gc, axis=2)
        o_inter = jnp.einsum('bhtk,bhkv->bhtv', qc * jnp.exp(b), s)
        diff = b[:, :, :, None, :] - b[:, :, None, :, :]
        decay = jnp.where(causal, jnp.exp(jnp.where(causal, diff, 0.0)), 0.0)
        att = jnp.einsum('bhtk,bhsk,bhtsk->bhts', qc, kc, decay)
        o = o_inter + jnp.einsum('bhts,bhsv->bhtv', att, vc)
        b_last = b[:, :, -1:, :]
        s_new = jnp.exp(b_last[:, :, 0, :])[..., None] * s + jnp.einsum(
            'bhsk,bhsv->bhkv', kc * jnp.exp(b_last - b), vc)
        return s_new, o

    s_fin, o = lax.scan(step, s0, (blk(q), blk(k), blk(v), blk(log_f)))
    o = o.transpose(1, 2, 0, 3, 4).reshape(B, H, nc * CHUNK, -1)[:, :, :T]
    return o, s_fin

def dsa_attend(q, k, v, qi, ki, wi, q_chunk, k_chunk, topk):
    B, Tq, H, Dh = q.shape
    qb = min(Q_BLOCK, Tq)
    nb = -(-Tq // qb)
    pad = nb * qb - Tq

    def blocks(a):
        a = jnp.pad(a, [(0, 0), (0, pad)] + [(0, 0)] * (a.ndim - 2))
        return a.reshape((B, nb, qb) + a.shape[2:]).swapaxes(0, 1)

    qc_blocks = jnp.pad(q_chunk, (0, pad), mode='edge').reshape(nb, qb)
    kif = ki.astype(jnp.float32)

    def one(args):
        q_b, qi_b, wi_b, qc_b = args
        sc = jnp.einsum('bqhd,bkd->bqhk', qi_b.astype(jnp.float32), kif) * (IDX_DIM ** -0.5)
        score = jnp.einsum('bqhk,bqh->bqk', jax.nn.relu(sc), wi_b.astype(jnp.float32))
        adm = k_chunk[None, :] <= qc_b[:, None]
        score = jnp.where(adm[None], score, NEG_BIG)
        _, top_idx = lax.top_k(score, topk)
        valid = jnp.take_along_axis(jnp.broadcast_to(adm[None], score.shape), top_idx, axis=-1)
        kg = jax.vmap(lambda kb, ib: kb[ib])(k, top_idx)
        vg = jax.vmap(lambda vb, ib: vb[ib])(v, top_idx)
        s = jnp.einsum('bqhd,bqnd->bqhn', q_b.astype(jnp.float32), kg.astype(jnp.float32)) * (Dh ** -0.5)
        s = jnp.where(valid[:, :, None, :], s, NEG_BIG)
        p = jax.nn.softmax(s, axis=-1)
        return jnp.einsum('bqhn,bqnd->bqhd', p, vg.astype(jnp.float32)).astype(q.dtype)

    out = lax.map(one, (blocks(q), blocks(qi), blocks(wi), qc_blocks))
    return out.swapaxes(0, 1).reshape(B, nb * qb, H, Dh)[:, :Tq]

def ab_mixer(u, pos, q_chunk, past_k, past_v, past_ki, past_chunk, s0,
             w_in, w_out, lb, o_gain, q_gain, k_gain, topk):
    B, T, _ = u.shape
    z = u @ w_in
    split_at = [int(c) for c in np.cumsum(IN_SPLITS)[:-1]]
    aq, af, ai, ag, bq, bk, bv, bqi, bki, bw = jnp.split(z, split_at, axis=-1)
    qa = jax.nn.silu(aq.astype(jnp.float32)).reshape(B, T, A_HEADS, A_DK).transpose(0, 2, 1, 3)
    zf = af.astype(jnp.float32).reshape(B, T, A_HEADS, A_DK).transpose(0, 2, 1, 3)
    lb_h = lb.reshape(A_HEADS, 1, A_DK)
    lb_pos = lb_h > 0
    lb_safe = jnp.where(lb_pos, lb_h, 0.5)
    log_f = jnp.where(lb_pos,
                      jnp.logaddexp(jnp.log(lb_safe), jnp.log1p(-lb_safe) + jax.nn.log_sigmoid(zf)),
                      jax.nn.log_sigmoid(zf))
    ka = (1.0 - lb_h) * jax.nn.sigmoid(-zf)
    va = ai.astype(jnp.float32).reshape(B, T, A_HEADS, A_DV).transpose(0, 2, 1, 3)
    oa, s_fin = hgrn2_recurrence(qa, ka, va, log_f, s0.astype(jnp.float32))
    oa = oa.transpose(0, 2, 1, 3)
    oa = oa * lax.rsqrt(jnp.mean(oa * oa, axis=-1, keepdims=True) + RMS_EPS)
    oa = oa.reshape(B, T, A_VW) * o_gain.astype(jnp.float32) * jax.nn.sigmoid(ag.astype(jnp.float32))
    q = rope_partial(rms_norm(bq.reshape(B, T, B_HEADS, B_DH), q_gain), pos)
    k_new = rope_partial(rms_norm(bk.reshape(B, T, 1, B_DH), k_gain), pos)[:, :, 0]
    v_new = bv
    qi = rope_partial(bqi.reshape(B, T, IDX_HEADS, IDX_DIM), pos)
    ki_new = rope_partial(bki.reshape(B, T, 1, IDX_DIM), pos)[:, :, 0]
    wi = bw * (IDX_HEADS ** -0.5)
    k_all = jnp.concatenate([past_k.astype(k_new.dtype), k_new], axis=1)
    v_all = jnp.concatenate([past_v.astype(v_new.dtype), v_new], axis=1)
    ki_all = jnp.concatenate([past_ki.astype(ki_new.dtype), ki_new], axis=1)
    k_chunk = jnp.concatenate([past_chunk, q_chunk])
    ob = dsa_attend(q, k_all, v_all, qi, ki_all, wi, q_chunk, k_chunk, topk)
    merged = jnp.concatenate([oa.astype(u.dtype), ob.reshape(B, T, B_QW)], axis=-1)
    return merged @ w_out, k_new, v_new, ki_new, s_fin.astype(s0.dtype)

def pool_mixer(u, hist, pos, w_grp, scale):
    B, T, D = u.shape
    ue = jnp.concatenate([hist.astype(u.dtype), u], axis=1).astype(jnp.float32)
    cs = jnp.cumsum(ue, axis=1)
    cs = jnp.concatenate([jnp.zeros((B, 1, D), jnp.float32), cs], axis=1)
    end = cs[:, POOL_HIST + 1:]
    uf = ue[:, POOL_HIST:]
    outs = []
    for g, w in enumerate(POOL_WINDOWS):
        sl = slice(g * POOL_GROUP, (g + 1) * POOL_GROUP)
        start = cs[:, POOL_HIST + 1 - w: POOL_HIST + 1 - w + T, sl]
        cnt = jnp.minimum(w, pos + 1).astype(jnp.float32)[None, :, None]
        mean = (end[..., sl] - start) / cnt
        outs.append(jnp.einsum('btc,cd->btd', mean - uf[..., sl], w_grp[g].astype(jnp.float32)))
    y = jnp.concatenate(outs, axis=-1) * scale.astype(jnp.float32)
    return y.astype(u.dtype), ue[:, -POOL_HIST:].astype(u.dtype)

def setup_inputs(seed: int = 0) -> dict:
    key = jax.random.key(seed)
    ks = jax.random.split(key, 25)
    f32 = jnp.float32

    def nrm(k, shape, scale=1.0):
        return jax.random.normal(k, shape, f32) * scale

    def gain(k, shape):
        return 1.0 + 0.05 * jax.random.normal(k, shape, f32)

    return {
        'x_prompt': nrm(ks[0], (BATCH, SEQ, D_MODEL)),
        'x_sample': nrm(ks[1], (DEC_BATCH, DEC_SEQ, D_MODEL)),
        'cache_k': nrm(ks[2], (N_AB, DEC_BATCH, PAST_LEN, B_DH)),
        'cache_v': nrm(ks[3], (N_AB, DEC_BATCH, PAST_LEN, B_DH)),
        'cache_ki': nrm(ks[4], (N_AB, DEC_BATCH, PAST_LEN, IDX_DIM)),
        'state_hgrn': nrm(ks[5], (N_AB, DEC_BATCH, A_HEADS, A_DK, A_DV), 0.5),
        'state_pool': nrm(ks[6], (N_POOL, DEC_BATCH, POOL_HIST, D_MODEL)),
        'meta_tokens': nrm(ks[7], (N_META, D_MODEL)),
        'norm_ffn1': gain(ks[8], (DEPTH, D_MODEL)),
        'ffn1_wg': nrm(ks[9], (DEPTH, D_MODEL, D_FF), D_MODEL ** -0.5),
        'ffn1_wu': nrm(ks[10], (DEPTH, D_MODEL, D_FF), D_MODEL ** -0.5),
        'ffn1_wd': nrm(ks[11], (DEPTH, D_FF, D_MODEL), D_FF ** -0.5),
        'norm_mix': gain(ks[12], (DEPTH, D_MODEL)),
        'norm_ffn2': gain(ks[13], (DEPTH, D_MODEL)),
        'ffn2_wg': nrm(ks[14], (DEPTH, D_MODEL, D_FF), D_MODEL ** -0.5),
        'ffn2_wu': nrm(ks[15], (DEPTH, D_MODEL, D_FF), D_MODEL ** -0.5),
        'ffn2_wd': nrm(ks[16], (DEPTH, D_FF, D_MODEL), D_FF ** -0.5),
        'ab_w_in': nrm(ks[17], (N_AB, D_MODEL, IN_COLS), D_MODEL ** -0.5),
        'ab_w_out': nrm(ks[18], (N_AB, MIX_W, D_MODEL), MIX_W ** -0.5),
        'hgrn_lb_logits': nrm(ks[19], (N_AB, A_KW), 0.5),
        'hgrn_out_norm': gain(ks[20], (N_AB, A_VW)),
        'attn_q_norm': gain(ks[21], (N_AB, B_DH)),
        'attn_k_norm': gain(ks[22], (N_AB, B_DH)),
        'pool_w': nrm(ks[23], (N_POOL, len(POOL_WINDOWS), POOL_GROUP, POOL_GROUP), POOL_GROUP ** -0.5),
        'pool_scale': gain(ks[24], (N_POOL, D_MODEL)),
    }

def reference(x_prompt, x_sample, cache_k, cache_v, cache_ki, state_hgrn, state_pool,
              meta_tokens, norm_ffn1, ffn1_wg, ffn1_wu, ffn1_wd, norm_mix, norm_ffn2,
              ffn2_wg, ffn2_wu, ffn2_wd, ab_w_in, ab_w_out, hgrn_lb_logits, hgrn_out_norm,
              attn_q_norm, attn_k_norm, pool_w, pool_scale):
    Bp, Sp, D = x_prompt.shape
    Bs, Ts, _ = x_sample.shape
    P = cache_k.shape[2]
    hp = jnp.concatenate([jnp.broadcast_to(meta_tokens.astype(x_prompt.dtype)[None], (Bp, N_META, D)), x_prompt], axis=1)
    Tp = hp.shape[1]
    pos_p = jnp.arange(Tp, dtype=jnp.int32)
    chunk_p = jnp.where(pos_p < N_META, -1, (pos_p - N_META) // CHUNK)
    pos_s = P + jnp.arange(Ts, dtype=jnp.int32)
    chunk_s = pos_s // CHUNK
    past_chunk = jnp.arange(P, dtype=jnp.int32) // CHUNK
    topk_p = min(TOPK_MAX, Sp // 4)
    topk_s = min(TOPK_MAX, (P + Ts) // 4)
    empty_kv = jnp.zeros((Bp, 0, B_DH), hp.dtype)
    empty_ki = jnp.zeros((Bp, 0, IDX_DIM), hp.dtype)
    empty_c = jnp.zeros((0,), jnp.int32)
    s0_p = jnp.zeros((Bp, A_HEADS, A_DK, A_DV), jnp.float32)
    hist_p = jnp.zeros((Bp, POOL_HIST, D), hp.dtype)
    lb_soft = jax.nn.softmax(hgrn_lb_logits.astype(jnp.float32), axis=0)
    lb_all = jnp.cumsum(lb_soft, axis=0) - lb_soft[0]

    kp_l, vp_l, kip_l, sp_l, pp_l = [], [], [], [], []
    ks_l, vs_l, kis_l, ss_l, ps_l = [], [], [], [], []
    hs = x_sample
    for l in range(DEPTH):
        hp = hp + 0.5 * swiglu(rms_norm(hp, norm_ffn1[l]), ffn1_wg[l], ffn1_wu[l], ffn1_wd[l])
        hs = hs + 0.5 * swiglu(rms_norm(hs, norm_ffn1[l]), ffn1_wg[l], ffn1_wu[l], ffn1_wd[l])
        up = rms_norm(hp, norm_mix[l])
        us = rms_norm(hs, norm_mix[l])
        j = l // 2
        if l % 2 == 0:
            mp, kp, vp, kip, sp = ab_mixer(up, pos_p, chunk_p, empty_kv, empty_kv, empty_ki, empty_c, s0_p,
                                           ab_w_in[j], ab_w_out[j], lb_all[j], hgrn_out_norm[j],
                                           attn_q_norm[j], attn_k_norm[j], topk_p)
            ms, ks, vs, kis, ss = ab_mixer(us, pos_s, chunk_s, cache_k[j], cache_v[j], cache_ki[j], past_chunk,
                                           state_hgrn[j], ab_w_in[j], ab_w_out[j], lb_all[j], hgrn_out_norm[j],
                                           attn_q_norm[j], attn_k_norm[j], topk_s)
            kp_l.append(kp); vp_l.append(vp); kip_l.append(kip); sp_l.append(sp)
            ks_l.append(ks); vs_l.append(vs); kis_l.append(kis); ss_l.append(ss)
        else:
            mp, pp = pool_mixer(up, hist_p, pos_p, pool_w[j], pool_scale[j])
            ms, ps = pool_mixer(us, state_pool[j], pos_s, pool_w[j], pool_scale[j])
            pp_l.append(pp); ps_l.append(ps)
        hp = hp + mp
        hs = hs + ms
        hp = hp + 0.5 * swiglu(rms_norm(hp, norm_ffn2[l]), ffn2_wg[l], ffn2_wu[l], ffn2_wd[l])
        hs = hs + 0.5 * swiglu(rms_norm(hs, norm_ffn2[l]), ffn2_wg[l], ffn2_wu[l], ffn2_wd[l])

    y_prompt = hp[:, N_META:]
    return (y_prompt, hs,
            jnp.stack(kp_l), jnp.stack(vp_l), jnp.stack(kip_l), jnp.stack(sp_l), jnp.stack(pp_l),
            jnp.stack(ks_l), jnp.stack(vs_l), jnp.stack(kis_l), jnp.stack(ss_l), jnp.stack(ps_l))


_drawn_inputs = setup_inputs


def setup_inputs(seed=0):
    import zlib

    import numpy as np

    out = dict(_drawn_inputs(seed))
    spreads = {}
    factors = {'state_hgrn': 6.342,
     'hgrn_out_norm': 3.187,
     'attn_q_norm': 8.0,
     'norm_ffn2': 3.29,
     'pool_scale': 4.641}
    for name, (base, spread) in spreads.items():
        noise = np.random.default_rng([zlib.crc32(name.encode()), seed]).standard_normal(out[name].shape)
        drawn = base * np.exp(spread * noise) if base else spread * noise
        out[name] = __import__('jax').numpy.asarray(drawn.astype(out[name].dtype))
    for name, factor in factors.items():
        out[name] = (out[name] * factor).astype(out[name].dtype)
    return out
```

```python
from contextlib import ExitStack

import numpy as np

import concourse.bass as bass
from concourse import mybir

F32 = mybir.dt.float32
ACT = mybir.ActivationFunctionType
ALU = mybir.AluOpType

P = 128
D_MODEL, D_FF = 1024, 2816
SEQ, N_META, N_SAMPLE, PAST = 512, 16, 64, 128
N_PROMPT = SEQ + N_META
MAIN = 512
TAIL = N_PROMPT - MAIN
NT = N_PROMPT + N_SAMPLE
HALF = NT // 2
SMP0, TAIL0 = MAIN, MAIN + N_SAMPLE
DC = D_MODEL // P
FC = D_FF // P
HEADS, DH = 4, 128
IDX_HEADS, IDX_DIM = 4, 64
TOPK, TOPK_SAMPLE = SEQ // 4, (PAST + N_SAMPLE) // 4
CHUNK = 64
RMS_EPS = 1e-6
NEG_BIG = -1e30
TAKEN = -3e38
PAD_TOP = 3e38
ROPE_THETA = 500000.0
POOL_WINDOWS = (2, 4, 8, 16)
POOL_HIST = 15
FFN_UNITS = FC + DC
IN_UNITS = 20
OUT_UNITS = DC
WSLOT = FC * P
VW = DH + IDX_HEADS
TILES = 5
ROWS = [P, P, P, P, N_SAMPLE + TAIL]
WIDTH = [144, 272, 400, 528, 528]
LEVELS = [64, 32, 16, 8, 4, 2, 1]
PASSES = [(kind, hp, h) for hp in range(2)
          for kind, h in [("level", h) for h in LEVELS] + [("diag", 0), ("q", 0), ("k", 0)]]
DECAYS = [x for x in PASSES if x[0] != "diag"]
SEGMENTS = [(i * P, P) for i in range(4)] + [(SMP0, N_SAMPLE), (TAIL0, TAIL)]
FFN_OF_STAGE = {0: 0, 2: 1, 3: 2, 5: 3}
UNIT0 = {0: 0, 1: FFN_UNITS, 2: FFN_UNITS + IN_UNITS + OUT_UNITS}
UNIT0[3] = UNIT0[2] + FFN_UNITS
UNIT0[5] = UNIT0[3] + FFN_UNITS


def build(nc, d):
    with ExitStack() as ctx:
        def sb(name, shape, dt=F32):
            return ctx.enter_context(nc.sbuf_tensor(name, shape, dt))

        def sem(name):
            return ctx.enter_context(nc.semaphore(name))

        resid = sb("resid", [P, DC, NT])
        normed = sb("normed", [P, DC, NT])
        wslot = sb("wslot", [P, 2, WSLOT])
        square = sb("square", [P, 2, NT])
        square_sum = sb("square_sum", [P, NT])
        root = sb("root", [P, NT])
        rnorm = sb("rnorm", [P, NT])
        act_out = sb("act_out", [P, 2, NT])
        ones = sb("ones", [P, P])
        ident = sb("ident", [P, P])
        eps = sb("eps", [P, 1])
        gains = sb("gains", [P, 6, DC])
        ARENA = 31900
        arena = sb("arena", [P, ARENA])
        hidden = arena[:, 0:FC * NT].rearrange("p (f n) -> p f n", f=FC)
        top = [0]

        def take(n):
            top[0] += n
            assert top[0] <= ARENA, top[0]
            return arena[:, top[0] - n:top[0]]

        def heads4(ap):
            return ap.rearrange("p (h n) -> p h n", h=HEADS)

        zf = heads4(take(HEADS * NT))
        qa = heads4(take(HEADS * NT))
        ag = heads4(take(HEADS * NT))
        ka = heads4(take(HEADS * NT))
        va = take(TILES * MAIN).rearrange("p (t n) -> p t n", t=TILES)
        kt = take(NT)
        assert top[0] <= FC * NT
        top[0] = FC * NT
        eg = take(8 * NT)
        decay = eg[:, 0:4 * NT].rearrange("p (b h n) -> p b h n", b=2, h=2)
        decayed = eg[:, 4 * NT:8 * NT].rearrange("p (b h n) -> p b h n", b=2, h=2)
        gate_a = heads4(eg[:, 0:4 * NT])
        gate_b = heads4(eg[:, 4 * NT:8 * NT])
        w_ai = eg[:, 0:DC * MAIN].rearrange("p (c n) -> p c n", c=DC)
        kd_tok = eg[:, 0:TILES * MAIN].rearrange("p (t n) -> p t n", t=TILES)
        probs = eg[:, 0:HEADS * 528].rearrange("p (h n) -> p h n", h=HEADS)
        probs_t = eg[:, HEADS * 528:HEADS * 528 + 5 * MAIN].rearrange("p (c h n) -> p c h n", c=5, h=HEADS)
        qt = heads4(take(HEADS * NT))
        small = take(3 * NT)
        kit = small[:, 0:NT]
        qit = small[:, NT:3 * NT].rearrange("p (c n) -> p c n", c=2)
        states_lo = small[:, 0:3 * MAIN].rearrange("p (s n) -> p s n", s=3)
        states_hi = take(4 * MAIN).rearrange("p (s n) -> p s n", s=4)
        att = take(TILES * MAIN).rearrange("p (t h n) -> p t h n", t=TILES, h=HEADS)
        relu_sc = att.rearrange("p t h n -> p (t h n)")[:, 0:2 * 528].rearrange("p (b n) -> p b n", b=2)
        score = take(TILES * 528).rearrange("p (t n) -> p t n", t=TILES)
        w_vw = score.rearrange("p t n -> p (t n)")[:, 0:DC * VW].rearrange("p (c n) -> p c n", c=DC)
        ropes = take(2 * NT).rearrange("p (b n) -> p b n", b=2)
        adm = take(144)
        vb = take(TILES * DH).rearrange("p (t n) -> p t n", t=TILES)
        v_tail = take(DH)
        cache = take(3 * P).rearrange("p (c n) -> p c n", c=3)
        perms = take(2 * P).rearrange("p (c n) -> p c n", c=2)
        mask_bits = sb("mask_bits", [P, 8, P])
        masks = mask_bits[:].bitcast(mybir.dt.uint32)
        smalls = sb("smalls", [P, 256])
        wi = smalls[:, 0:20].rearrange("p (t h) -> p t h", t=TILES)
        rq = smalls[:, 20:40].rearrange("p (t h) -> p t h", t=TILES)
        lb_in, lb, lb_free, lb_ln, lb_on, lb_shift, lb_e = (smalls[:, 40 + 4 * i:44 + 4 * i] for i in range(7))
        cgain = smalls[:, 68:76]
        e_last = smalls[:, 76:100].rearrange("p (h s) -> p h s", h=HEADS)
        max8 = smalls[:, 100:108]
        mx = smalls[:, 108:112]
        nbias = smalls[:, 112:116]
        psumv = smalls[:, 116:120]
        pinv = smalls[:, 120:124]
        rqs = smalls[:, 124:144].rearrange("p (t h) -> p t h", t=TILES)
        pscale = smalls[:, 144:152]
        top[0] = 0
        UE = 2 * POOL_HIST + NT
        PP0, PS0 = POOL_HIST, 2 * POOL_HIST + N_PROMPT
        ue = take(DC * UE).rearrange("p (c n) -> p c n", c=DC)
        sums = take(DC * UE).rearrange("p (c n) -> p c n", c=DC)
        sums2 = take(DC * UE).rearrange("p (c n) -> p c n", c=DC)
        pooled = take(DC * NT).rearrange("p (c n) -> p c n", c=DC)
        w_pool = take(2048).rearrange("p (g k m n) -> p g k m n", g=4, k=2, m=2)
        inv_cnt = take(64).rearrange("p (g n) -> p g n", g=4)

        ps = ctx.enter_context(nc.psum_tensor("ps", [P, 8, 512], F32))
        psf = ps[:, :, :].rearrange("p b n -> p (b n)")

        def state(i):
            return states_lo[:, i] if i < 3 else states_hi[:, i - 3]

        consts_in = sem("consts_in")
        resid_in = sem("resid_in")
        weights_in = [sem("weights_in0"), sem("weights_in1")]
        unit_done = sem("unit_done")
        ones_set = sem("ones_set")
        hid_done = sem("hid_done")
        silu_done = sem("silu_done")
        resid_done = sem("resid_done")
        square_done = sem("square_done")
        sumsq_zero = sem("sumsq_zero")
        sumsq_done = sem("sumsq_done")
        sumall_done = sem("sumall_done")
        root_done = sem("root_done")
        rnorm_done = sem("rnorm_done")
        normed_done = sem("normed_done")
        dve_step = sem("dve_step")
        act_step = sem("act_step")
        pool_step = sem("pool_step")
        names = """vw_in ai_in ab_in rope_in state_in vw_mm vw_evac ai_mm ai_evac raw_evac perm_mm rope_done
            isc_mm relu_done isc_acc topk_done qk_sq qsum_mm ksum_mm kroot_done k_normed qroot_done rq_done
            gate_l1 gate_min gate_a_done gate_ka gate_ln gate_logf scan_done kexp_done lb_done
            diff_done dexp_done mult_done level_mm att_zero att_evac elast_done kdt_mm kdt_evac delta_mm
            state_done sample_state head_mm head_evac osq_done osum_mm oroot_done oa_done
            logit_mm masked_done exp_done p_done pt_mm pt_evac pv_mm pv_evac
            pool_in hist_zero ue_done pwin_done pool_mm out_sem y_out kperm_mm qperm_done ao_free""".split()
        s = {n: sem(n) for n in names}

        block = ctx.enter_context(nc.Block())

        @block.sync
        def _(sync):
            sync.dma_start(resid[:], d["x"]).then_inc(resid_in, 16)
            sync.dma_start(gains[:], d["gains"]).then_inc(resid_in, 16)

            def load_units(src, unit0, n, width):
                with sync.Fori(0, n // 2) as i:
                    for b in range(2):
                        sync.wait_ge(unit_done, 2 * i + unit0 + b + 1)
                        sync.dma_start(wslot[:, b, 0:width], src[bass.ds(2 * i + b, 1)].rearrange("u p n -> (u p) n")) \
                            .then_inc(weights_in[b], 16)

            def load_ffn(f, stage):
                load_units(d["w_up"][f], UNIT0[stage], FC, 2 * DC * P)
                load_units(d["w_dn"][f], UNIT0[stage] + FC, DC, FC * P)

            load_ffn(0, 0)
            load_units(d["w_in"], UNIT0[1], IN_UNITS, DC * P)
            load_units(d["w_out"], UNIT0[1] + IN_UNITS, OUT_UNITS, DC * P)
            load_ffn(1, 2)
            load_ffn(2, 3)
            load_ffn(3, 5)
            with sync.Fori(0, DC) as i:
                sync.wait_ge(resid_done, i + 2 + 5 * DC + 1)
                sync.dma_start(d["y"][:, bass.ds(i, 1), :], resid[:, bass.ds(i, 1), :]).then_inc(s["y_out"], 16)
            sync.wait_ge(s["y_out"], 16 * DC)

        @block.gpsimd
        def _(pool):
            g = nc.gpsimd

            def link(ins):
                nonlocal_step[0] += 1
                ins.then_inc(pool_step, 1)
                pool.wait_ge(pool_step, nonlocal_step[0])

            nonlocal_step = [0]
            pool.dma_start(ident[:], d["ident"]).then_inc(consts_in, 16)
            pool.dma_start(mask_bits[:], d["masks"]).then_inc(consts_in, 16)
            pool.dma_start(smalls[:, 40:44], d["lb_logits"]).then_inc(consts_in, 16)
            pool.dma_start(cgain, d["cgain"]).then_inc(consts_in, 16)
            pool.dma_start(pscale, d["pool_scale"]).then_inc(consts_in, 16)
            pool.dma_start(adm, d["adm"]).then_inc(consts_in, 16)
            pool.dma_start(cache, d["cache"]).then_inc(consts_in, 16)
            pool.dma_start(perms, d["perms"]).then_inc(consts_in, 16)
            pool.dma_start(ropes, d["rope_idx"]).then_inc(s["rope_in"], 16)
            pool.dma_start(w_vw, d["w_vw"]).then_inc(s["vw_in"], 16)
            pool.dma_start(w_ai, d["w_ai"]).then_inc(s["ai_in"], 16)
            pool.wait_ge(s["vw_evac"], TILES)
            pool.dma_start(d["v"][:, 0:4], vb[:, 0:4]).then_inc(s["out_sem"], 16)
            pool.dma_start(d["v"][0:ROWS[4], 4], vb[0:ROWS[4], 4]).then_inc(s["out_sem"], 16)
            pool.wait_ge(s["rope_done"], 3)
            pool.dma_start(ropes, d["rope_head"]).then_inc(s["rope_in"], 16)
            pool.dma_start(d["ki"], kit[0:IDX_DIM]).then_inc(s["out_sem"], 16)
            pool.wait_ge(s["gate_l1"], 1)
            link(g.tensor_scalar(gate_b, zf, 0.0, None, ALU.min))
            g.tensor_tensor(gate_b, gate_b, gate_a, ALU.subtract).then_inc(s["gate_min"], 1)
            pool.wait_ge(s["gate_min"], 1)
            g.tensor_tensor(ka, gate_b, zf, ALU.subtract).then_inc(s["gate_min"], 1)
            pool.wait_ge(s["gate_ln"], 1)
            link(g.tensor_tensor(gate_a, gate_a, gate_b, ALU.subtract))
            pool.wait_ge(s["lb_done"], 1)
            for h in range(HEADS):
                last = g.tensor_scalar(gate_a[:, h], gate_a[:, h], lb_on[:, h:h + 1], None, ALU.mult)
            link(last)
            pool.wait_ge(s["gate_min"], 2)
            g.tensor_tensor(zf, gate_a, gate_b, ALU.add).then_inc(s["gate_logf"], 1)
            pool.wait_ge(s["isc_acc"], 4 * TILES)
            g.memset(att, 0.0).then_inc(s["att_zero"], 1)
            pool.dma_start(states_hi[:, 2], d["state"]).then_inc(s["state_in"], 16)
            pool.wait_ge(s["scan_done"], 1)
            for n, (kind, hp, h) in enumerate(DECAYS):
                if n >= 2:
                    pool.wait_ge(s["mult_done"], n - 1)
                e = decay[:, n % 2]
                b = zf[:, 2 * hp:2 * hp + 2]
                if kind == "level":
                    cols = MAIN if h == 64 else TAIL0 if h >= 16 else NT
                    ev = e[:, :, 0:cols].rearrange("p a (n x) -> p a n x", x=2 * h)
                    bv = b[:, :, 0:cols].rearrange("p a (n x) -> p a n x", x=2 * h)
                    ref = bv[:, :, :, h - 1:h].to_broadcast([P, 2, cols // (2 * h), h])
                    g.tensor_tensor(ev[:, :, :, 0:h], ref, bv[:, :, :, 0:h], ALU.subtract)
                    g.tensor_tensor(ev[:, :, :, h:2 * h], bv[:, :, :, h:2 * h], ref, ALU.subtract) \
                        .then_inc(s["diff_done"], 1)
                elif kind == "k":
                    for lo, w in ((0, P), (SMP0, N_SAMPLE), (TAIL0, TAIL)):
                        cols = MAIN if lo == 0 else w
                        ev = e[:, :, lo:lo + cols].rearrange("p a (n x) -> p a n x", x=w)
                        bv = b[:, :, lo:lo + cols].rearrange("p a (n x) -> p a n x", x=w)
                        last = g.tensor_tensor(ev, bv[:, :, :, w - 1:w].to_broadcast([P, 2, cols // w, w]), bv,
                                               ALU.subtract)
                    last.then_inc(s["diff_done"], 1)
            pool.wait_ge(s["rope_done"], 4)
            pool.dma_start(d["k"], kt).then_inc(s["out_sem"], 16)
            pool.wait_ge(s["state_done"], 5)
            pool.dma_start(d["hgrn_p"], states_hi[:, 1]).then_inc(s["out_sem"], 16)
            pool.wait_ge(s["sample_state"], 1)
            pool.dma_start(d["hgrn_s"], states_hi[:, 3]).then_inc(s["out_sem"], 16)
            pool.wait_ge(unit_done, UNIT0[3] + FFN_UNITS + 2)
            pool.dma_start(w_pool, d["w_pool"]).then_inc(s["pool_in"], 16)
            pool.dma_start(inv_cnt, d["inv_cnt"]).then_inc(s["pool_in"], 16)
            pool.dma_start(ue[:, :, N_PROMPT + POOL_HIST:PS0], d["state_pool"]).then_inc(s["pool_in"], 16)
            g.memset(ue[:, :, 0:POOL_HIST], 0.0).then_inc(s["hist_zero"], 1)
            pool.wait_ge(s["ue_done"], 3 * DC)
            pool.dma_start(d["pool_p"], ue[:, :, N_PROMPT:N_PROMPT + POOL_HIST]).then_inc(s["out_sem"], 16)
            pool.dma_start(d["pool_s"], ue[:, :, UE - POOL_HIST:UE]).then_inc(s["out_sem"], 16)
            pool.wait_ge(s["out_sem"], 16 * 8)

        @block.scalar
        def _(act):
            a = nc.scalar
            steps = [0]

            def link(ins):
                steps[0] += 1
                ins.then_inc(act_step, 1)
                act.wait_ge(act_step, steps[0])

            def halves(bank):
                return ps[:, bank:bank + 2, 0:HALF]

            def split(ap):
                return ap.rearrange("p (b n) -> p b n", b=2)

            def root_of(stage):
                act.wait_ge(sumall_done, stage + 1)
                a.activation(split(root[:]), halves(2), ACT.Sqrt, bias=eps[:, 0:1], scale=1.0 / D_MODEL) \
                    .then_inc(root_done, 1)

            def squares_in_down(stage):
                with act.Fori(0, DC // 2) as i:
                    for b in range(2):
                        act.wait_ge(resid_done, 2 * i + b + 2 + DC * stage + 1)
                        act.wait_ge(sumsq_done, 2 * i + b + DC * (stage + 1) - 1)
                        a.activation(square[:, b, :], resid[:, bass.ds(2 * i + b, 1), :].rearrange("p a n -> p (a n)"),
                                     ACT.Square).then_inc(square_done, 1)
                root_of(stage + 1)

            def ffn(stage, last=False):
                f = FFN_OF_STAGE[stage]
                with act.Fori(0, FC // 2) as i:
                    for b in range(2):
                        act.wait_ge(unit_done, 2 * i + b + UNIT0[stage] + 2 + 1)
                        act.wait_ge(hid_done, 2 * i + b + FC * f + 1)
                        a.activation(split(act_out[:, b, :]), halves(4 * b), ACT.Silu).then_inc(silu_done, 1)
                if not last:
                    squares_in_down(stage)

            act.wait_ge(resid_in, 32)
            act.wait_ge(ones_set, 3)
            for c in range(DC):
                if c >= 2:
                    act.wait_ge(sumsq_done, c - 1)
                a.activation(square[:, c % 2, :], resid[:, c, :], ACT.Square).then_inc(square_done, 1)
            root_of(0)
            ffn(0)

            U = UNIT0[1] + 2
            for t in range(TILES):
                act.wait_ge(s["vw_mm"], t + 1)
                r = ROWS[t]
                a.activation(vb[0:r, t], ps[0:r, 4 + t % 2, 0:DH], ACT.Copy)
                if t == 4:
                    a.activation(v_tail[0:TAIL], ps[N_SAMPLE:r, 4, 0:DH], ACT.Copy)
                a.activation(wi[0:r, t], ps[0:r, 4 + t % 2, DH:VW], ACT.Copy, scale=IDX_HEADS ** -0.5) \
                    .then_inc(s["vw_evac"], 1)
            for n, dst in enumerate((kit, qit[:, 0], qit[:, 1])):
                act.wait_ge(unit_done, U + n + 1)
                a.activation(split(dst), halves(2 * (n % 2)), ACT.Copy).then_inc(s["raw_evac"], 1)
            for t in range(TILES):
                act.wait_ge(s["ai_mm"], t + 1)
                a.activation(va[0:ROWS[t], t], ps[0:ROWS[t], 4 + t % 2, :], ACT.Copy).then_inc(s["ai_evac"], 1)
            n = 0
            for t in range(TILES):
                for h in range(IDX_HEADS):
                    act.wait_ge(s["isc_mm"], n + 1)
                    if n >= 2:
                        act.wait_ge(s["isc_acc"], n - 1)
                    bank = 4 + 2 * (n % 2)
                    a.activation(relu_sc[0:ROWS[t], n % 2, 0:WIDTH[t]],
                                 psf[0:ROWS[t], bank * 512:bank * 512 + WIDTH[t]], ACT.Relu,
                                 scale=IDX_DIM ** -0.5).then_inc(s["relu_done"], 1)
                    n += 1
            act.wait_ge(unit_done, U + 3 + 1)
            a.activation(split(kt), halves(2), ACT.Copy).then_inc(s["raw_evac"], 1)
            a.activation(split(square[:, 0, :]), halves(2), ACT.Square).then_inc(s["qk_sq"], 1)
            for h in range(HEADS):
                b = 2 * ((4 + h) % 2)
                act.wait_ge(unit_done, U + 4 + h + 1)
                a.activation(split(qt[:, h]), halves(b), ACT.Copy, scale=cgain[:, 0:1])
                if h >= 1:
                    act.wait_ge(s["ksum_mm" if h == 1 else "qsum_mm"], 1 if h == 1 else h - 1)
                a.activation(split(square[:, (h + 1) % 2, :]), halves(b), ACT.Square).then_inc(s["qk_sq"], 1)
            for h in range(HEADS):
                act.wait_ge(unit_done, U + 8 + h + 1)
                a.activation(split(zf[:, h]), halves(2 * (h % 2)), ACT.Copy).then_inc(s["raw_evac"], 1)
            act.wait_ge(s["raw_evac"], 8)
            act.wait_ge(s["ai_mm"], TILES)
            link(a.activation(gate_a, zf, ACT.Abs))
            link(a.activation(gate_a, gate_a, ACT.Exp, scale=-1.0))
            a.activation(gate_a, gate_a, ACT.Ln, bias=ones[:, 0:1]).then_inc(s["gate_l1"], 1)

            def proj(n, dst, h, func):
                act.wait_ge(unit_done, U + n + 1)
                a.activation(split(dst[:, h]), halves(2 * (n % 2)), func).then_inc(s["raw_evac"], 1)

            for h in range(HEADS):
                proj(12 + h, qa, h, ACT.Silu)
            act.wait_ge(s["qsum_mm"], 4)
            a.activation(rqs[:, 0:4], ps[:, 4, 0:16].rearrange("p (t h) -> p t h", t=4), ACT.Sqrt, bias=eps[:, 0:1],
                         scale=1.0 / DH)
            a.activation(rqs[0:ROWS[4], 4], ps[0:ROWS[4], 4, 16:20], ACT.Sqrt, bias=eps[0:ROWS[4], 0:1],
                         scale=1.0 / DH).then_inc(s["qroot_done"], 1)
            act.wait_ge(s["ksum_mm"], 1)
            a.activation(split(root[:]), halves(6), ACT.Sqrt, bias=eps[:, 0:1], scale=1.0 / DH) \
                .then_inc(s["kroot_done"], 1)
            for h in range(HEADS):
                proj(16 + h, ag, h, ACT.Sigmoid)
            act.wait_ge(s["gate_min"], 2)
            act.wait_ge(s["lb_done"], 1)
            link(a.activation(lb_ln, lb_free, ACT.Ln))
            for h in range(HEADS):
                last = a.activation(gate_a[:, h], gate_b[:, h], ACT.Exp, bias=lb_ln[:, h:h + 1])
            link(last)
            for h in range(HEADS):
                last = a.activation(gate_a[:, h], gate_a[:, h], ACT.Ln, bias=lb_shift[:, h:h + 1])
            last.then_inc(s["gate_ln"], 1)
            for h in range(HEADS):
                last = a.activation(ka[:, h], ka[:, h], ACT.Exp, bias=lb_ln[:, h:h + 1])
            last.then_inc(s["gate_ka"], 1)
            act.wait_ge(s["scan_done"], 1)
            diffs = 0
            for n, (kind, hp, h) in enumerate(DECAYS):
                cols = NT if kind != "level" else MAIN if h == 64 else TAIL0 if h >= 16 else NT
                e = decay[:, n % 2, :, 0:cols]
                if kind == "q":
                    act.wait_ge(s["mult_done"], n - 1)
                    a.activation(e, zf[:, 2 * hp:2 * hp + 2], ACT.Exp).then_inc(s["dexp_done"], 1)
                else:
                    diffs += 1
                    act.wait_ge(s["diff_done"], diffs)
                    a.activation(e, e, ACT.Exp).then_inc(s["dexp_done"], 1)
            a.activation(e_last[:, :, 0:4], zf[:, :, P - 1:MAIN:P], ACT.Exp)
            a.activation(e_last[:, :, 4:5], zf[:, :, TAIL0 - 1:TAIL0], ACT.Exp)
            a.activation(e_last[:, :, 5:6], zf[:, :, NT - 1:NT], ACT.Exp).then_inc(s["elast_done"], 1)
            act.wait_ge(s["mult_done"], len(DECAYS))
            for t in range(TILES):
                act.wait_ge(s["kdt_mm"], t + 1)
                if t == 0:
                    act.wait_ge(s["level_mm"], 16)
                a.activation(kd_tok[0:ROWS[t], t], ps[0:ROWS[t], 6 + t % 2, :], ACT.Copy).then_inc(s["kdt_evac"], 1)
            for t in range(TILES):
                act.wait_ge(s["head_mm"], t + 1)
                if t == 0:
                    act.wait_ge(s["elast_done"], 1)
                r = ROWS[t]
                a.activation(zf[:, :, t * P:t * P + r],
                             ps[:, 6 + t % 2, :].rearrange("p (h n) -> p h n", h=HEADS)[:, :, 0:r], ACT.Copy) \
                    .then_inc(s["head_evac"], 1)
            act.wait_ge(s["head_evac"], TILES)
            for h in range(HEADS):
                if h >= 2:
                    act.wait_ge(s["osum_mm"], h - 1)
                a.activation(square[:, h % 2, :], zf[:, h], ACT.Square).then_inc(s["osq_done"], 1)
            for h in range(HEADS):
                act.wait_ge(s["osum_mm"], h + 1)
                act.wait_ge(s["k_normed"], 1)
                if h >= 1:
                    act.wait_ge(s["oa_done"], h)
                a.activation(split(root[:]), halves(2 * (h % 2)), ACT.Sqrt, bias=eps[:, 0:1], scale=1.0 / DH) \
                    .then_inc(s["oroot_done"], 1)
            ev = 0
            for t in range(TILES):
                r = ROWS[t]
                for h in range(HEADS):
                    act.wait_ge(s["masked_done"], t * HEADS + h + 1)
                    a.activation(probs[0:r, h, 0:WIDTH[t]], probs[0:r, h, 0:WIDTH[t]], ACT.Exp,
                                 bias=nbias[0:r, h:h + 1], scale=rq[0:r, t, h:h + 1],
                                 accum_out=psumv[0:r, h:h + 1]).then_inc(s["exp_done"], 1)
                for c, (kw, kc, parts) in enumerate(key_chunks(t)):
                    act.wait_ge(s["pt_mm"], ev + 1)
                    if c == 0 and t > 0:
                        act.wait_ge(s["pv_mm"], t)
                    for lo, n in parts:
                        last = a.activation(probs_t[0:kw, c, :, lo:lo + n],
                                            ps[0:kw, 4 + ev % 2, :].rearrange("p (h n) -> p h n", h=HEADS)[:, :, lo:lo + n],
                                            ACT.Copy)
                    last.then_inc(s["pt_evac"], 1)
                    ev += 1
                act.wait_ge(s["pv_mm"], t + 1)
                a.activation(normed[:, 4:8, t * P:t * P + r],
                             ps[:, 6 + t % 2, :].rearrange("p (h n) -> p h n", h=HEADS)[:, :, 0:r], ACT.Copy) \
                    .then_inc(s["pv_evac"], 1)
            squares_in_down(1)
            ffn(2)
            ffn(3)
            squares_in_down(4)
            ffn(5, last=True)

        @block.vector
        def _(dve):
            v = nc.vector
            steps = [0]

            def link(ins):
                steps[0] += 1
                ins.then_inc(dve_step, 1)
                dve.wait_ge(dve_step, steps[0])

            def halves(bank):
                return ps[:, bank:bank + 2, 0:HALF]

            def split(ap):
                return ap.rearrange("p (b n) -> p b n", b=2)

            def norm(stage, write=None):
                dve.wait_ge(root_done, stage + 1)
                v.reciprocal(rnorm[:], root[:]).then_inc(rnorm_done, 1)
                dve.wait_ge(rnorm_done, stage + 1)
                v.memset(square_sum[:], 0.0).then_inc(sumsq_zero, 1)
                for c in range(DC):
                    if write:
                        write(c)
                    else:
                        v.scalar_tensor_tensor(normed[:, c, :], resid[:, c, :], gains[:, stage, c:c + 1], rnorm[:],
                                               ALU.mult, ALU.mult).then_inc(normed_done, 1)

            def add_squares(base, i, b):
                dve.wait_ge(square_done, i + b + base + 1)
                dve.wait_ge(sumsq_done, i + b + base)
                v.tensor_tensor(square_sum[:], square_sum[:], square[:, b, :], ALU.add).then_inc(sumsq_done, 1)

            def update_residual(stage, unit0, factor, last=False):
                dve.wait_ge(sumsq_zero, stage + 1)
                with dve.Fori(0, DC // 2) as i:
                    for b in range(2):
                        dve.wait_ge(unit_done, 2 * i + b + unit0 + 2 + 1)
                        r = split(resid[:, bass.ds(2 * i + b, 1), :].rearrange("p a n -> p (a n)"))
                        v.scalar_tensor_tensor(r, halves(4 * b), factor, r, ALU.mult, ALU.add).then_inc(resid_done, 1)
                    if not last:
                        for b in range(2):
                            add_squares(DC * (stage + 1), 2 * i, b)

            def ffn(stage, last=False):
                f = FFN_OF_STAGE[stage]
                with dve.Fori(0, FC // 2) as i:
                    for b in range(2):
                        dve.wait_ge(silu_done, 2 * i + b + FC * f + 1)
                        v.tensor_tensor(split(hidden[:, bass.ds(2 * i + b, 1), :].rearrange("p a n -> p (a n)")),
                                        split(act_out[:, b, :]), halves(4 * b + 2), ALU.mult).then_inc(hid_done, 1)
                update_residual(stage, UNIT0[stage] + FC, 0.5, last)

            v.memset(ones[:], 1.0).then_inc(ones_set, 1)
            v.memset(eps[:], RMS_EPS).then_inc(ones_set, 1)
            v.memset(square_sum[:], 0.0).then_inc(ones_set, 1)
            v.memset(act_out[:, 0, 0:1], 0.0).then_inc(hid_done, 2)
            v.memset(act_out[:, 0, 1:2], 0.0).then_inc(resid_done, 2)
            dve.wait_ge(ones_set, 3)
            for c in range(DC):
                dve.wait_ge(square_done, c + 1)
                if c:
                    dve.wait_ge(sumsq_done, c)
                v.tensor_tensor(square_sum[:], square_sum[:], square[:, c % 2, :], ALU.add).then_inc(sumsq_done, 1)
            norm(0)
            dve.wait_ge(consts_in, 16 * 8)
            link(v.tensor_tensor(lb_e, lb_in, lb_in, ALU.subtract))
            link(v.tensor_scalar(lb_e, lb_e, 1.0, None, ALU.add))
            link(v.reciprocal(lb_shift, lb_e))
            link(v.tensor_tensor(lb_e, lb_e, lb_shift, ALU.mult))
            link(v.tensor_tensor(lb, lb_e, lb_e, ALU.subtract))
            link(v.tensor_scalar(lb_free, lb, -1.0, 1.0, ALU.mult, ALU.add))
            link(v.tensor_scalar(lb_on, lb, 0.0, None, ALU.is_gt))
            link(v.tensor_scalar(lb_e, lb_on, -1.0, 1.0, ALU.mult, ALU.add))
            v.tensor_tensor(lb_shift, lb, lb_e, ALU.add).then_inc(s["lb_done"], 1)
            ffn(0)
            norm(1)

            def rope(x, table, bank):
                link(v.tensor_tensor(x, x, ropes[:, 0], ALU.mult))
                link(v.tensor_tensor(split(act_out[:, 0, :]), halves(bank), split(ropes[:, 1]), ALU.mult))
                v.tensor_tensor(x, x, act_out[:, 0, :], ALU.add).then_inc(s["rope_done"], 1)

            dve.wait_ge(s["rope_in"], 16)
            for n, x in enumerate((kit, qit[:, 0], qit[:, 1])):
                dve.wait_ge(s["perm_mm"], n + 1)
                rope(x, 0, 6)
            n = 0
            for t in range(TILES):
                r, w = ROWS[t], WIDTH[t]
                for h in range(IDX_HEADS):
                    dve.wait_ge(s["relu_done"], n + 1)
                    if h == 0:
                        if t == 0:
                            dve.wait_ge(s["vw_evac"], TILES)
                        ins = v.tensor_scalar(score[0:r, t, 0:w], relu_sc[0:r, n % 2, 0:w], wi[0:r, t, 0:1], None,
                                              ALU.mult)
                    else:
                        ins = v.scalar_tensor_tensor(score[0:r, t, 0:w], relu_sc[0:r, n % 2, 0:w],
                                                     wi[0:r, t, h:h + 1], score[0:r, t, 0:w], ALU.mult, ALU.add)
                    ins.then_inc(s["isc_acc"], 1)
                    n += 1
                    dve.wait_ge(s["isc_acc"], n)
                if t < 4:
                    link(v.tensor_tensor(score[:, t, t * P:t * P + 144], score[:, t, t * P:t * P + 144], adm, ALU.add))
                else:
                    last = PAST + N_SAMPLE
                    link(v.memset(score[0:N_SAMPLE, t, last:last + TOPK - TOPK_SAMPLE], PAD_TOP))
                    link(v.memset(score[0:N_SAMPLE, t, last + TOPK - TOPK_SAMPLE:528], NEG_BIG))
            for t in range(TILES):
                sc = score[0:ROWS[t], t, 0:WIDTH[t]]
                for _ in range(TOPK // 8):
                    link(v.max(max8[0:ROWS[t]], sc))
                    link(v.match_replace(sc, max8[0:ROWS[t]], sc, TAKEN))
                link(v.tensor_scalar(sc, sc, -2e38, NEG_BIG, ALU.is_gt, ALU.mult))
                if t < 4:
                    link(v.tensor_tensor(score[:, t, t * P:t * P + 144], score[:, t, t * P:t * P + 144], adm, ALU.min))
                else:
                    link(v.memset(score[0:N_SAMPLE, t, PAST + N_SAMPLE:528], NEG_BIG))
            dve.wait_ge(s["kroot_done"], 1)
            link(v.reciprocal(rnorm[:], root[:]))
            v.scalar_tensor_tensor(kt, kt, cgain[:, 1:2], rnorm[:], ALU.mult, ALU.mult).then_inc(s["k_normed"], 1)
            dve.wait_ge(s["k_normed"], 1)
            dve.wait_ge(s["rope_in"], 32)
            dve.wait_ge(s["qroot_done"], 1)
            link(v.reciprocal(rq[:, 0:4], rqs[:, 0:4]))
            link(v.reciprocal(rq[0:ROWS[4], 4], rqs[0:ROWS[4], 4]))
            link(v.tensor_scalar(rq[:, 0:4], rq[:, 0:4], DH ** -0.5, None, ALU.mult))
            link(v.tensor_scalar(rq[0:ROWS[4], 4], rq[0:ROWS[4], 4], DH ** -0.5, None, ALU.mult))
            for n in range(5):
                dve.wait_ge(s["kperm_mm"], n + 1)
                rope(kt if n == 0 else qt[:, n - 1], 1, 2 * (n % 2))
                dve.wait_ge(s["rope_done"], 3 + n + 1)
            dve.wait_ge(s["gate_logf"], 1)
            for h in range(HEADS):
                for lo, w in SEGMENTS:
                    last = v.tensor_tensor_scan(zf[:, h, lo:lo + w], ones[:, 0:w], zf[:, h, lo:lo + w], 0.0, ALU.mult,
                                                ALU.add)
            last.then_inc(s["scan_done"], 1)
            dve.wait_ge(s["gate_ka"], 1)
            dve.wait_ge(s["raw_evac"], 16)
            dve.wait_ge(s["att_zero"], 1)
            nd = lv = 0

            def collect(n):
                kind, hp, h = LEVEL_PASSES[n]
                m = LEVELS.index(h) if kind == "level" else len(LEVELS)
                dve.wait_ge(s["level_mm"], n + 1)
                if n:
                    dve.wait_ge(s["att_evac"], n)
                for pair in range(2):
                    last = v.copy_predicated(
                        att[:, 2 * pair:2 * pair + 2, 2 * hp:2 * hp + 2, :],
                        masks[:, m:m + 1, :].rearrange("p (a b) n -> p a b n", b=1).to_broadcast([P, 2, 2, P]),
                        ps[:, 3 * (n % 2) + pair, :].rearrange("p (a b n) -> p a b n", a=2, b=2))
                if not (kind == "level" and h == 64):
                    r = N_SAMPLE if kind == "level" and h >= 16 else ROWS[4]
                    last = v.copy_predicated(
                        att[0:r, 4, 2 * hp:2 * hp + 2, 0:r],
                        masks[0:r, m:m + 1, 0:r].to_broadcast([r, 2, r]),
                        ps[0:r, 3 * (n % 2) + 2, 0:256].rearrange("p (b n) -> p b n", b=2)[:, :, 0:r])
                last.then_inc(s["att_evac"], 1)

            lv = 0
            for kind, hp, h in PASSES:
                if kind == "diag":
                    lv += 1
                    collect(lv - 2)
                    continue
                dve.wait_ge(s["dexp_done"], nd + 1)
                e, gd = decay[:, nd % 2], decayed[:, lv % 2]
                k2, q2 = ka[:, 2 * hp:2 * hp + 2], qa[:, 2 * hp:2 * hp + 2]
                if kind == "level":
                    if lv >= 2:
                        dve.wait_ge(s["level_mm"], lv - 1)
                    cols = MAIN if h == 64 else TAIL0 if h >= 16 else NT

                    def blocks(ap):
                        return ap[:, :, 0:cols].rearrange("p a (n x) -> p a n x", x=2 * h)
                    v.tensor_tensor(blocks(gd)[:, :, :, 0:h], blocks(e)[:, :, :, 0:h], blocks(k2)[:, :, :, 0:h], ALU.mult)
                    v.tensor_tensor(blocks(gd)[:, :, :, h:2 * h], blocks(e)[:, :, :, h:2 * h],
                                    blocks(q2)[:, :, :, h:2 * h], ALU.mult).then_inc(s["mult_done"], 1)
                    lv += 1
                    if h != LEVELS[0]:
                        collect(lv - 2)
                else:
                    if kind == "q":
                        collect(lv - 1)
                        v.tensor_tensor(q2, q2, e, ALU.mult).then_inc(s["mult_done"], 1)
                    else:
                        v.tensor_tensor(k2, k2, e, ALU.mult).then_inc(s["mult_done"], 1)
                nd += 1
            dve.wait_ge(s["elast_done"], 1)
            dve.wait_ge(s["state_in"], 16)
            dve.wait_ge(s["out_sem"], 16 * 4)
            for i in range(6):
                dve.wait_ge(s["delta_mm"], i + 1)
                src = states_hi[:, 2] if i == 5 else state(max(i - 1, 0))
                dst = states_hi[:, 3] if i == 5 else state(i)
                seg = (0, 1, 2, 3, 5, 4)[i]
                if i == 0:
                    last = v.tensor_copy(dst, ps[:, 0, :])
                else:
                    if i < 5:
                        dve.wait_ge(s["state_done"], i)
                    for h in range(HEADS):
                        c = slice(h * DH, (h + 1) * DH)
                        last = v.scalar_tensor_tensor(dst[:, c], src[:, c], e_last[:, h, seg:seg + 1], ps[:, i, c],
                                                      ALU.mult, ALU.add)
                last.then_inc(s["state_done"] if i < 5 else s["sample_state"], 1)
            for h in range(HEADS):
                dve.wait_ge(s["oroot_done"], h + 1)
                link(v.reciprocal(rnorm[:], root[:]))
                link(v.scalar_tensor_tensor(rnorm[:], rnorm[:], cgain[:, 4 + h:5 + h], ag[:, h], ALU.mult, ALU.mult))
                v.tensor_tensor(normed[:, h, :], zf[:, h], rnorm[:], ALU.mult).then_inc(s["oa_done"], 1)
                dve.wait_ge(s["oa_done"], h + 1)
            for t in range(TILES):
                r, w = ROWS[t], WIDTH[t]
                for h in range(HEADS):
                    dve.wait_ge(s["logit_mm"], t * HEADS + h + 1)
                    if h == 0 and t:
                        dve.wait_ge(s["pt_mm"], sum(len(key_chunks(x)) for x in range(t)))
                    bank = 2 * (h % 2)
                    link(v.tensor_tensor_reduce(out=probs[0:r, h, 0:w], in0=psf[0:r, bank * 512:bank * 512 + w],
                                                in1=score[0:r, t, 0:w], scale=1.0, scalar=TAKEN, op0=ALU.add,
                                                op1=ALU.max, accum_out=mx[0:r, h:h + 1]))
                    v.tensor_scalar(nbias[0:r, h:h + 1], mx[0:r, h:h + 1], rq[0:r, t, h:h + 1], -1.0, ALU.mult,
                                    ALU.mult).then_inc(s["masked_done"], 1)
                    dve.wait_ge(s["masked_done"], t * HEADS + h + 1)
                for h in range(HEADS):
                    dve.wait_ge(s["exp_done"], t * HEADS + h + 1)
                    link(v.reciprocal(pinv[0:r, h:h + 1], psumv[0:r, h:h + 1]))
                    v.tensor_scalar(probs[0:r, h, 0:w], probs[0:r, h, 0:w], pinv[0:r, h:h + 1], None, ALU.mult) \
                        .then_inc(s["p_done"], 1)
            update_residual(1, UNIT0[1] + IN_UNITS, 1.0)
            norm(2)
            dve.wait_ge(s["out_sem"], 16 * 6)
            ffn(2)
            norm(3)
            ffn(3)

            def to_ue(c):
                if c == 0:
                    dve.wait_ge(unit_done, UNIT0[3] + FFN_UNITS + 2)
                    dve.wait_ge(resid_done, 2 + DC * 4)
                for lo, n, dst in ((0, MAIN, PP0), (TAIL0, TAIL, PP0 + MAIN), (SMP0, N_SAMPLE, PS0)):
                    v.scalar_tensor_tensor(ue[:, c, dst:dst + n], resid[:, c, lo:lo + n], gains[:, 4, c:c + 1],
                                           rnorm[:, lo:lo + n], ALU.mult, ALU.mult).then_inc(s["ue_done"], 1)
            norm(4, to_ue)
            dve.wait_ge(s["ue_done"], 3 * DC)
            dve.wait_ge(s["pool_in"], 48)
            dve.wait_ge(s["hist_zero"], 1)
            bufs = (sums, sums2)
            for gi, w in enumerate(POOL_WINDOWS):
                cs = slice(2 * gi, 2 * gi + 2)
                src, step, k = ue[:, cs], 1, 0
                while step < w:
                    dst = bufs[k % 2][:, cs]
                    lo = 2 * step - 1
                    link(v.tensor_tensor(dst[:, :, lo:UE], src[:, :, lo:UE], src[:, :, lo - step:UE - step], ALU.add))
                    src, step, k = dst, 2 * step, k + 1
                dst = bufs[k % 2][:, cs]
                link(v.tensor_tensor(dst[:, :, PP0:PP0 + 16], src[:, :, PP0:PP0 + 16],
                                     inv_cnt[:, gi:gi + 1, :].to_broadcast([P, 2, 16]), ALU.mult))
                link(v.tensor_scalar(dst[:, :, PP0 + 16:UE], src[:, :, PP0 + 16:UE], 1.0 / w, None, ALU.mult))
                for lo, n, at in ((0, MAIN, PP0), (TAIL0, TAIL, PP0 + MAIN), (SMP0, N_SAMPLE, PS0)):
                    last = v.tensor_tensor(pooled[:, cs, lo:lo + n], dst[:, :, at:at + n], ue[:, cs, at:at + n],
                                           ALU.subtract)
                last.then_inc(s["pwin_done"], 1)
            dve.wait_ge(sumsq_zero, 5)
            for c in range(DC):
                dve.wait_ge(s["pool_mm"], c + 1)
                r = split(resid[:, c, :])
                v.scalar_tensor_tensor(r, halves(4 * (c % 2)), pscale[:, c:c + 1], r, ALU.mult, ALU.add) \
                    .then_inc(resid_done, 1)
                if c % 2:
                    for b in range(2):
                        add_squares(DC * 5, c - 1, b)
            norm(5)
            dve.wait_ge(s["out_sem"], 16 * 8)
            ffn(5, last=True)

        @block.tensor
        def _(pe):
            mm = nc.tensor.matmul

            def arrived(unit, b, i=0):
                pe.wait_ge(weights_in[b], 16 * (i + unit // 2 + 1))

            def sum_squares(stage):
                pe.wait_ge(sumsq_done, DC * (stage + 1))
                for hf in range(2):
                    last = mm(ps[:, 2 + hf, 0:HALF], ones[:], square_sum[:, hf * HALF:(hf + 1) * HALF], start=True,
                              stop=True)
                last.then_inc(sumall_done, 1)

            def product(bank, w, x, k, n):
                for hf in range(2):
                    last = mm(ps[:, bank + hf, 0:HALF], w, x[:, hf * HALF:(hf + 1) * HALF], start=(k == 0),
                              stop=(k == n - 1))
                return last

            def ffn(stage, last_stage=False):
                f = FFN_OF_STAGE[stage]
                with pe.Fori(0, FC // 2) as i:
                    for b in range(2):
                        arrived(UNIT0[stage], b, i)
                        pe.wait_ge(hid_done, 2 * i + b + FC * f + 1)
                        w = wslot[:, b, 0:2 * DC * P].rearrange("p (g c n) -> p g c n", g=2, c=DC)
                        for c in range(DC):
                            if b == 0:
                                pe.wait_ge(normed_done, DC * NORMED[stage] + c + 1)
                            for gu in range(2):
                                last = product(4 * b + 2 * gu, w[:, gu, c, :], normed[:, c, :], c, DC)
                        last.then_inc(unit_done, 1)
                with pe.Fori(0, DC // 2) as i:
                    for b in range(2):
                        arrived(UNIT0[stage] + FC, b, i)
                        pe.wait_ge(resid_done, 2 * i + b + DC * stage + 1)
                        pe.wait_ge(hid_done, 2 + FC * f + FC - 1 + b)
                        w = wslot[:, b, :].rearrange("p (c n) -> p c n", c=FC)
                        for c in range(FC):
                            if c == FC - 1 and b == 0:
                                pe.wait_ge(hid_done, 2 + FC * f + c + 1)
                            last = product(4 * b, w[:, c, :], hidden[:, c, :], c, FC)
                        last.then_inc(unit_done, 1)
                if not last_stage:
                    sum_squares(stage + 1)

            pe.wait_ge(ones_set, 3)
            mm(ps[:, 7, 0:2], ones[:], ones[:, 0:2], start=True, stop=True).then_inc(unit_done, 2)
            sum_squares(0)
            ffn(0)

            U = UNIT0[1]
            x = normed

            def cols(t):
                return slice(t * P, t * P + ROWS[t])

            pe.wait_ge(normed_done, 2 * DC)
            pe.wait_ge(s["vw_in"], 16)
            for t in range(TILES):
                if t >= 2:
                    pe.wait_ge(s["vw_evac"], t - 1)
                for c in range(DC):
                    last = mm(ps[0:ROWS[t], 4 + t % 2, 0:VW], x[:, c, cols(t)], w_vw[:, c, :], start=(c == 0),
                              stop=(c == DC - 1))
                last.then_inc(s["vw_mm"], 1)

            def in_unit(n):
                arrived(U + n, n % 2)
                if 2 <= n < 8:
                    pe.wait_ge(s["qk_sq" if 5 <= n else "raw_evac"], n - 4 if 5 <= n else n - 1 if n < 5 else 0)
                w = wslot[:, n % 2, 0:DC * P].rearrange("p (c n) -> p c n", c=DC)
                for c in range(DC):
                    last = product(2 * (n % 2), w[:, c, :], x[:, c, :], c, DC)
                last.then_inc(unit_done, 1)

            def exchange(table, src, bank, signal):
                last = product(bank, perms[:, table, :], src, 0, 1)
                last.then_inc(signal, 1)

            pe.wait_ge(consts_in, 16 * 8)
            for n, src in enumerate((kit, qit[:, 0], qit[:, 1])):
                in_unit(n)
                if n:
                    pe.wait_ge(s["raw_evac"], n)
                    if n >= 2:
                        pe.wait_ge(s["rope_done"], n - 1)
                    exchange(0, (kit, qit[:, 0])[n - 1], 6, s["perm_mm"])
            pe.wait_ge(s["ai_in"], 16)
            for t in range(TILES):
                pe.wait_ge(s["vw_evac"], TILES)
                if t >= 2:
                    pe.wait_ge(s["ai_evac"], t - 1)
                for c in range(DC):
                    last = mm(ps[0:ROWS[t], 4 + t % 2, :], x[:, c, cols(t)], w_ai[:, c, :], start=(c == 0),
                              stop=(c == DC - 1))
                last.then_inc(s["ai_mm"], 1)
                if t == 0:
                    pe.wait_ge(s["raw_evac"], 3)
                    pe.wait_ge(s["rope_done"], 2)
                    exchange(0, qit[:, 1], 6, s["perm_mm"])
            pe.wait_ge(s["rope_done"], 3)
            pe.wait_ge(s["ai_evac"], TILES)
            n = 0
            for t in range(TILES):
                for h in range(IDX_HEADS):
                    if n >= 2:
                        pe.wait_ge(s["relu_done"], n - 1)
                    bank = 4 + 2 * (n % 2)
                    rows = slice(IDX_DIM * (h % 2), IDX_DIM * (h % 2) + IDX_DIM)
                    w = min(WIDTH[t], MAIN)
                    q = qit[rows, h // 2, cols(t)]
                    last = mm(ps[0:ROWS[t], bank, 0:w], q, kit[rows, 0:w], start=True, stop=True)
                    if WIDTH[t] > MAIN:
                        last = mm(ps[0:ROWS[t], bank + 1, 0:TAIL], q, kit[rows, TAIL0:NT], start=True, stop=True)
                    if t == 4:
                        q = qit[rows, h // 2, SMP0:TAIL0]
                        mm(ps[0:N_SAMPLE, bank, 0:PAST], q, cache[rows, 1, :], start=True, stop=True)
                        last = mm(ps[0:N_SAMPLE, bank, PAST:PAST + N_SAMPLE], q, kit[rows, SMP0:TAIL0], start=True,
                                  stop=True)
                    last.then_inc(s["isc_mm"], 1)
                    n += 1
            in_unit(3)
            for n in range(4, 8):
                if n == 4:
                    pe.wait_ge(s["raw_evac"], 3)
                in_unit(n)
                pe.wait_ge(s["qk_sq"], n - 3)
                pe.wait_ge(s["relu_done"], 4 * TILES)
                if n == 4:
                    product(6, ones[:], square[:, 0, :], 0, 1).then_inc(s["ksum_mm"], 1)
                else:
                    head_square_sums(mm, ps, square, ones, n - 5, s)
            pe.wait_ge(s["qk_sq"], 5)
            for n in range(8, IN_UNITS):
                if n < 10:
                    pass
                else:
                    pe.wait_ge(s["raw_evac"], n - 5)
                in_unit(n)
                if n == 8:
                    head_square_sums(mm, ps, square, ones, 3, s)
            for n in range(5):
                if n == 0:
                    pe.wait_ge(s["k_normed"], 1)
                    pe.wait_ge(s["raw_evac"], 16)
                if n >= 2:
                    pe.wait_ge(s["rope_done"], 3 + n - 1)
                exchange(1, kt if n == 0 else qt[:, n - 1], 2 * (n % 2), s["kperm_mm"])
            pe.wait_ge(s["rope_done"], 8)
            pe.wait_ge(s["kroot_done"], 1)
            pe.wait_ge(s["qroot_done"], 1)
            for n, (kind, hp, h) in enumerate(LEVEL_PASSES):
                if n >= 2:
                    pe.wait_ge(s["att_evac"], n - 1)
                if kind == "level":
                    pe.wait_ge(s["mult_done"], n + 1 if hp == 0 else n + 2)
                else:
                    pe.wait_ge(s["gate_ka"], 1)
                for t in range(TILES):
                    r = ROWS[t]
                    if t == 4 and kind == "level":
                        if h == 64:
                            continue
                        if h >= 16:
                            r = N_SAMPLE
                    for a in range(2):
                        if kind == "level":
                            left = right = decayed[:, n % 2, a, t * P:t * P + r]
                        else:
                            left, right = ka[:, 2 * hp + a, t * P:t * P + r], qa[:, 2 * hp + a, t * P:t * P + r]
                        at = (t % 2) * 256 + a * P if t < 4 else a * P
                        last = mm(ps[0:r, 3 * (n % 2) + t // 2, at:at + r], left, right, start=True, stop=True)
                last.then_inc(s["level_mm"], 1)
            pe.wait_ge(s["mult_done"], len(DECAYS))
            for t in range(TILES):
                if t >= 2:
                    pe.wait_ge(s["kdt_evac"], t - 1)
                for h in range(HEADS):
                    last = nc.tensor.transpose(ps[0:ROWS[t], 6 + t % 2, h * DH:(h + 1) * DH], ka[:, h, cols(t)],
                                               ident[:])
                last.then_inc(s["kdt_mm"], 1)
            pe.wait_ge(s["att_evac"], 16)
            pe.wait_ge(s["kdt_evac"], TILES)
            pe.wait_ge(s["ai_evac"], TILES)
            for i in range(6):
                t, rows = (i, slice(0, P)) if i < 4 else (4, slice(N_SAMPLE, ROWS[4])) if i == 4 else (4, slice(0, N_SAMPLE))
                for h in range(HEADS):
                    c = slice(h * DH, (h + 1) * DH)
                    last = mm(ps[:, i, c], kd_tok[rows, t, c], va[rows, t, c], start=True, stop=True)
                last.then_inc(s["delta_mm"], 1)
            for t in range(TILES):
                if t >= 2:
                    pe.wait_ge(s["head_evac"], t - 1)
                if t:
                    pe.wait_ge(s["state_done"], t)
                if t == 4:
                    pe.wait_ge(s["state_in"], 16)
                o = ps[:, 6 + t % 2, :].rearrange("p (h n) -> p h n", h=HEADS)
                for h in range(HEADS):
                    c = slice(h * DH, (h + 1) * DH)
                    if t < 4:
                        last = mm(o[:, h, :], va[:, t, c], att[:, t, h, :], start=True, stop=(t == 0))
                        if t:
                            last = mm(o[:, h, :], state(t - 1)[:, c], qa[:, h, cols(t)], start=False, stop=True)
                    else:
                        for rows, st, lo, n in ((slice(0, N_SAMPLE), states_hi[:, 2], SMP0, N_SAMPLE),
                                                (slice(N_SAMPLE, ROWS[4]), state(3), TAIL0, TAIL)):
                            mm(o[:, h, rows], va[rows, 4, c], att[rows, 4, h, rows], start=True, stop=False)
                            last = mm(o[:, h, rows], st[:, c], qa[:, h, lo:lo + n], start=False, stop=True)
                last.then_inc(s["head_mm"], 1)
            for h in range(HEADS):
                pe.wait_ge(s["osq_done"], h + 1)
                if h == 0:
                    pe.wait_ge(s["sample_state"], 1)
                    pe.wait_ge(s["state_done"], 5)
                if h >= 2:
                    pe.wait_ge(s["oroot_done"], h - 1)
                product(2 * (h % 2), ones[:], square[:, h % 2, :], 0, 1).then_inc(s["osum_mm"], 1)
            ev = 0
            for t in range(TILES):
                r = ROWS[t]
                for h in range(HEADS):
                    n = t * HEADS + h
                    if n >= 2:
                        pe.wait_ge(s["masked_done"], n - 1)
                    elif n == 0:
                        pe.wait_ge(s["oroot_done"], HEADS)
                    bank = 2 * (h % 2)
                    q = qt[:, h, cols(t)]
                    w = min(WIDTH[t], MAIN)
                    last = mm(ps[0:r, bank, 0:w], q, kt[:, 0:w], start=True, stop=True)
                    if WIDTH[t] > MAIN:
                        last = mm(ps[0:r, bank + 1, 0:TAIL], q, kt[:, TAIL0:NT], start=True, stop=True)
                    if t == 4:
                        q = qt[:, h, SMP0:TAIL0]
                        mm(ps[0:N_SAMPLE, bank, 0:PAST], q, cache[:, 0, :], start=True, stop=True)
                        last = mm(ps[0:N_SAMPLE, bank, PAST:PAST + N_SAMPLE], q, kt[:, SMP0:TAIL0], start=True,
                                  stop=True)
                    last.then_inc(s["logit_mm"], 1)
                for kw, kc, parts in key_chunks(t):
                    if ev >= 2:
                        pe.wait_ge(s["pt_evac"], ev - 1)
                    for h in range(HEADS):
                        pe.wait_ge(s["p_done"], t * HEADS + h + 1)
                        last = nc.tensor.transpose(ps[0:kw, 4 + ev % 2, h * P:h * P + r], probs[0:r, h, kc:kc + kw],
                                                   ident[0:r, 0:r])
                    last.then_inc(s["pt_mm"], 1)
                    ev += 1
                pe.wait_ge(s["pt_evac"], ev)
                if t == 0:
                    pe.wait_ge(s["head_evac"], TILES)
                if t >= 2:
                    pe.wait_ge(s["pv_evac"], t - 1)
                out = ps[:, 6 + t % 2, :].rearrange("p (h n) -> p h n", h=HEADS)
                chunks = key_chunks(t)
                if t < 4:
                    for c, (kw, kc, parts) in enumerate(chunks):
                        vk = v_tail[0:TAIL] if kc == MAIN else vb[0:kw, c]
                        last = mm(out, vk, probs_t[0:kw, c], start=(c == 0), stop=(c == len(chunks) - 1))
                else:
                    tail = slice(N_SAMPLE, ROWS[4])
                    for c in range(5):
                        kw = P if c < 4 else TAIL
                        last = mm(out[:, :, tail], vb[0:kw, c] if c < 4 else v_tail[0:TAIL], probs_t[0:kw, c, :, tail],
                                  start=(c == 0), stop=(c == 4))
                    smp = slice(0, N_SAMPLE)
                    mm(out[:, :, smp], cache[:, 2, :], probs_t[:, 0, :, smp], start=True, stop=False)
                    last = mm(out[:, :, smp], vb[0:N_SAMPLE, 4], probs_t[0:N_SAMPLE, 1, :, smp], start=False, stop=True)
                last.then_inc(s["pv_mm"], 1)
            pe.wait_ge(s["pv_evac"], TILES)
            pe.wait_ge(s["oa_done"], HEADS)
            pe.wait_ge(s["masked_done"], TILES * HEADS)
            pe.wait_ge(s["pt_evac"], ev)
            with pe.Fori(0, DC // 2) as i:
                for b in range(2):
                    arrived(U + IN_UNITS, b, i)
                    pe.wait_ge(resid_done, 2 * i + b + DC + 1)
                    w = wslot[:, b, 0:DC * P].rearrange("p (c n) -> p c n", c=DC)
                    for c in range(DC):
                        last = product(4 * b, w[:, c, :], normed[:, c, :], c, DC)
                    last.then_inc(unit_done, 1)
            sum_squares(2)
            ffn(2)
            ffn(3)
            pe.wait_ge(s["pool_in"], 48)
            for c in range(DC):
                gi, m = c // 2, c % 2
                pe.wait_ge(s["pwin_done"], gi + 1)
                pe.wait_ge(resid_done, DC * 4 + c + 1)
                for k in range(2):
                    last = product(4 * (c % 2), w_pool[:, gi, k, m, :], pooled[:, 2 * gi + k, :], k, 2)
                last.then_inc(s["pool_mm"], 1)
            sum_squares(5)
            ffn(5, last_stage=True)



NORMED = {0: 0, 1: 1, 2: 2, 3: 3, 5: 4}
LEVEL_PASSES = [x for x in PASSES if x[0] in ("level", "diag")]


def key_chunks(t):
    if t < 4:
        w = WIDTH[t]
        return [(min(P, w - k), k, [(0, P)]) for k in range(0, w, P)]
    return [(P, k, [(0, ROWS[4])]) for k in range(0, MAIN, P)] + [(TAIL, MAIN, [(0, ROWS[4])])]


def head_square_sums(mm, ps, square, ones, h, s):
    for t in range(TILES):
        last = mm(ps[0:ROWS[t], 4, 4 * t + h:4 * t + h + 1], square[:, (h + 1) % 2, t * P:t * P + ROWS[t]],
                  ones[:, 0:1], start=True, stop=True)
    last.then_inc(s["qsum_mm"], 1)


def token_order():
    return np.r_[0:MAIN, TAIL0:NT], np.arange(SMP0, TAIL0)


def rope_tables(dim, heads_in_chunk):
    half = dim // 8
    inv = (np.float32(ROPE_THETA) ** (-np.arange(half, dtype=np.float32) / np.float32(half))).astype(np.float32)
    pos = np.zeros(NT, np.float32)
    prompt, sample = token_order()
    pos[prompt] = np.arange(N_PROMPT)
    pos[sample] = PAST + np.arange(N_SAMPLE)
    ang = (pos[None, :] * inv[:, None]).astype(np.float32).astype(np.float64)
    cos, sin = np.ones((dim, NT)), np.zeros((dim, NT))
    cos[:half] = cos[half:2 * half] = np.cos(ang)
    sin[:half], sin[half:2 * half] = -np.sin(ang), np.sin(ang)
    table = np.stack([np.tile(cos, (heads_in_chunk, 1)), np.tile(sin, (heads_in_chunk, 1))], 1)
    perm = np.arange(P)
    for k in range(heads_in_chunk):
        o = k * dim
        perm[o:o + 2 * half] = o + np.r_[half:2 * half, 0:half]
    return table.astype(np.float32), np.eye(P, dtype=np.float32)[perm]


def shape_constants():
    rope_idx, perm_idx = rope_tables(IDX_DIM, 2)
    rope_head, perm_head = rope_tables(DH, 1)
    i = np.arange(P)
    src, dst = i[:, None], i[None, :]
    masks = [(src // (2 * h) == dst // (2 * h)) & (src % (2 * h) < h) & (dst % (2 * h) >= h) for h in LEVELS]
    masks.append(src == dst)
    bound = np.where(i < 16, 16, np.where(i < 80, 80, 144))
    adm = np.where(np.arange(144)[None, :] < bound[:, None], 0.0, NEG_BIG).astype(np.float32)
    pos = np.arange(16)
    inv_cnt = np.stack([1.0 / np.minimum(w, pos + 1) for w in POOL_WINDOWS]).astype(np.float32)
    return {
        "ident": np.eye(P, dtype=np.float32), "masks": np.stack(masks, 1).astype(np.float32), "adm": adm,
        "rope_idx": rope_idx, "rope_head": rope_head, "perms": np.stack([perm_idx, perm_head], 1),
        "inv_cnt": np.ascontiguousarray(np.broadcast_to(inv_cnt, (P, 4, 16))),
    }


def chunked(a):
    return a.reshape(-1, P, *a.shape[1:]).swapaxes(0, 1)


def units(w):
    k, n = w.shape
    return w.reshape(k // P, P, n // P, P).transpose(2, 1, 0, 3).reshape(n // P, P, k)


_OUTS = {"y": (P, DC, NT), "k": (P, NT), "v": (P, TILES, DH), "ki": (IDX_DIM, NT), "hgrn_p": (P, HEADS * DH),
         "hgrn_s": (P, HEADS * DH), "pool_p": (P, DC, POOL_HIST), "pool_s": (P, DC, POOL_HIST)}


def kernel(**inputs):
    import concourse.bacc as _bacc
    from concourse.bass_utils import run_bass_kernel_spmd as _run

    i = {k: np.asarray(v) for k, v in inputs.items()}
    prompt, sample = token_order()
    x = np.empty((NT, D_MODEL), np.float32)
    x[prompt] = np.concatenate([i["meta_tokens"], i["x_prompt"][0]])
    x[sample] = i["x_sample"][0]
    w_in = i["ab_w_in"][0]
    c = np.cumsum((0, 512, 512, 512, 512, 512, 128, 128, 256, 64, 4))
    aq, af, ai, ag, bq, bk, bv, bqi, bki, bw = (w_in[:, c[n]:c[n + 1]] for n in range(10))
    gains = np.stack([i["norm_ffn1"][0], i["norm_mix"][0], i["norm_ffn2"][0],
                      i["norm_ffn1"][1], i["norm_mix"][1], i["norm_ffn2"][1]])
    cki = i["cache_ki"][0, 0].T
    arrays = {
        "x": chunked(x.T), "gains": gains.reshape(6, DC, P).transpose(2, 0, 1),
        "w_up": np.stack([np.stack([units(i[n + "_wg"][l]), units(i[n + "_wu"][l])], 2).reshape(FC, P, 2 * DC * P)
                          for l in range(2) for n in ("ffn1", "ffn2")]),
        "w_dn": np.stack([units(i[n + "_wd"][l]) for l in range(2) for n in ("ffn1", "ffn2")]),
        "w_in": units(np.concatenate([bki, bki, bqi, bk, bq, af, aq, ag], 1)),
        "w_vw": chunked(np.concatenate([bv, bw], 1)), "w_ai": chunked(ai), "w_out": units(i["ab_w_out"][0]),
        "lb_logits": i["hgrn_lb_logits"].reshape(HEADS, P).T,
        "cgain": np.concatenate([i["attn_q_norm"], i["attn_k_norm"], i["attn_q_norm"], i["attn_k_norm"],
                                 i["hgrn_out_norm"].reshape(HEADS, P)]).T,
        "pool_scale": i["pool_scale"].reshape(DC, P).T,
        "cache": np.stack([i["cache_k"][0, 0].T, np.concatenate([cki, cki]), i["cache_v"][0, 0]], 1),
        "state": i["state_hgrn"][0, 0].transpose(1, 0, 2).reshape(P, HEADS * DH),
        "state_pool": chunked(i["state_pool"][0, 0].T),
        "w_pool": i["pool_w"][0].reshape(4, 2, P, 2, P).transpose(2, 0, 1, 3, 4).reshape(P, 4, 2, 2, P),
        **shape_constants(),
    }
    arrays = {k: np.ascontiguousarray(v) for k, v in arrays.items()}
    nc = _bacc.Bacc("TRN2", target_bir_lowering=False, num_devices=1)
    d = {k: nc.dram_tensor("in_" + k, v.shape, mybir.dt.from_np(v.dtype), kind="ExternalInput").ap()
         for k, v in arrays.items()}
    d |= {k: nc.dram_tensor("out_" + k, v, F32, kind="ExternalOutput").ap() for k, v in _OUTS.items()}
    build(nc, d)
    r = _run(nc, [{"in_" + k: v for k, v in arrays.items()}], core_ids=[0]).results[0]
    o = {k: r["out_" + k] for k in _OUTS}

    def tokens(a):
        a = a.transpose(2, 1, 0).reshape(NT, -1)
        return a[prompt], a[sample]

    y_p, y_s = tokens(o["y"])
    k_p, k_s = tokens(o["k"][:, None])
    ki_p, ki_s = tokens(o["ki"][:, None])
    v_rows = o["v"].transpose(1, 0, 2)
    v_all = np.concatenate([v_rows[:4].reshape(MAIN, DH), v_rows[4, :ROWS[4]]])
    v_p, v_s = v_all[prompt], v_all[sample]

    def states(a):
        return a.reshape(P, HEADS, DH).transpose(1, 0, 2)[None, None]

    def hist(a):
        return a.transpose(2, 1, 0).reshape(POOL_HIST, D_MODEL)[None, None]

    out = (y_p[N_META:][None], y_s[None], k_p[None, None], v_p[None, None], ki_p[None, None], states(o["hgrn_p"]),
           hist(o["pool_p"]), k_s[None, None], v_s[None, None], ki_s[None, None], states(o["hgrn_s"]),
           hist(o["pool_s"]))
    return tuple(np.ascontiguousarray(a) for a in out)
```

```python
from contextlib import ExitStack

import numpy as np

import concourse.bass as bass
from concourse import mybir

F32 = mybir.dt.float32
F16 = mybir.dt.float16
U32 = mybir.dt.uint32
AXIS_X = mybir.AxisListType.X
ALL_MAX = bass.bass_isa.ReduceOp.max
ACT = mybir.ActivationFunctionType
ALU = mybir.AluOpType

P = 128
D_MODEL, D_FF = 1024, 2816
SEQ, N_META, N_SAMPLE, PAST = 512, 16, 64, 128
N_PROMPT = SEQ + N_META
MAIN = 512
TAIL = N_PROMPT - MAIN
NT = N_PROMPT + N_SAMPLE
HALF = NT // 2
SMP0, TAIL0 = MAIN, MAIN + N_SAMPLE
DC = D_MODEL // P
FC = D_FF // P
HEADS, DH = 4, 128
IDX_HEADS, IDX_DIM = 4, 64
TOPK, TOPK_SAMPLE = SEQ // 4, (PAST + N_SAMPLE) // 4
CHUNK = 64
RMS_EPS = 1e-6
NEG_BIG = -1e30
TAKEN = -3e38
PAD_TOP = 3e38
ROPE_THETA = 500000.0
POOL_WINDOWS = (2, 4, 8, 16)
POOL_HIST = 15
FFN_UNITS = FC + DC
IN_UNITS = 20
OUT_UNITS = DC
UP_W, DN_W = 2 * DC * P, FC * P
WSLOT = DN_W
EXPONENT = 0x7F800000
TINY = 2.0 ** -100
VW = DH + IDX_HEADS
TILES = 5
ROWS = [P, P, P, P, N_SAMPLE + TAIL]
WIDTH = [144, 272, 400, 528, 528]
LEVELS = [64, 32, 16, 8, 4, 2, 1]
PASSES = [(kind, hp, h) for hp in range(2)
          for kind, h in [("level", h) for h in LEVELS] + [("diag", 0), ("q", 0), ("k", 0)]]
DECAYS = [x for x in PASSES if x[0] != "diag"]
SEGMENTS = [(i * P, P) for i in range(4)] + [(SMP0, N_SAMPLE), (TAIL0, TAIL)]
FFN_OF_STAGE = {0: 0, 2: 1, 3: 2, 5: 3}
UNIT0 = {0: 0, 1: FFN_UNITS, 2: FFN_UNITS + IN_UNITS + OUT_UNITS}
UNIT0[3] = UNIT0[2] + FFN_UNITS
UNIT0[5] = UNIT0[3] + FFN_UNITS


def build(nc, d):
    with ExitStack() as ctx:
        def sb(name, shape, dt=F32):
            return ctx.enter_context(nc.sbuf_tensor(name, shape, dt))

        def sem(name):
            return ctx.enter_context(nc.semaphore(name))

        resid = sb("resid", [P, DC, NT])
        normed = sb("normed", [P, DC, NT])
        normed16 = normed[:, :, :].rearrange("p c n -> p (c n)").bitcast(F16) \
            .rearrange("p (a c n) -> p a c n", a=2, c=DC)
        wslot = sb("wslot", [P, 2, WSLOT])
        scales = sb("scales", [P, 160])
        gmax, gall, gexp, inv_x = (scales[:, 6 * i:6 * i + 6] for i in range(4))
        gains16 = scales[:, 24:72].rearrange("p (s c) -> p s c", s=6)
        wmax, wall, wexp, wdown, wscale, wback = (scales[:, 72 + 2 * i:74 + 2 * i] for i in range(6))
        hmax = scales[:, 84:84 + FC]
        hmax1, hall, hexp, hdown, hscale, inv_h = (scales[:, 106 + i:107 + i] for i in range(6))
        gscale = scales[:, 112:118]
        square = sb("square", [P, 2, NT])
        square_sum = sb("square_sum", [P, NT])
        root = sb("root", [P, NT])
        rnorm = sb("rnorm", [P, NT])
        act_out = sb("act_out", [P, 2, NT])
        ones = sb("ones", [P, P])
        ident = sb("ident", [P, P])
        eps = sb("eps", [P, 1])
        gains = sb("gains", [P, 6, DC])
        ARENA = 31900
        arena = sb("arena", [P, ARENA])
        HN = FC * NT
        hidden16 = arena[:, 0:HN].bitcast(F16).rearrange("p (a f n) -> p a f n", a=2, f=FC)
        hidden = arena[:, HN:2 * HN].rearrange("p (f n) -> p f n", f=FC)
        w16 = arena[:, 2 * HN:2 * HN + 2 * WSLOT].bitcast(F16).rearrange("p (b a n) -> p b a n", b=2, a=2)
        top = [0]

        def take(n):
            top[0] += n
            assert top[0] <= ARENA, top[0]
            return arena[:, top[0] - n:top[0]]

        def heads4(ap):
            return ap.rearrange("p (h n) -> p h n", h=HEADS)

        zf = heads4(take(HEADS * NT))
        qa = heads4(take(HEADS * NT))
        ag = heads4(take(HEADS * NT))
        ka = heads4(take(HEADS * NT))
        va = take(TILES * MAIN).rearrange("p (t n) -> p t n", t=TILES)
        kt = take(NT)
        assert top[0] <= FC * NT
        top[0] = FC * NT
        eg = take(8 * NT)
        decay = eg[:, 0:4 * NT].rearrange("p (b h n) -> p b h n", b=2, h=2)
        decayed = eg[:, 4 * NT:8 * NT].rearrange("p (b h n) -> p b h n", b=2, h=2)
        gate_a = heads4(eg[:, 0:4 * NT])
        gate_b = heads4(eg[:, 4 * NT:8 * NT])
        w_ai = eg[:, 0:DC * MAIN].rearrange("p (c n) -> p c n", c=DC)
        kd_tok = eg[:, 0:TILES * MAIN].rearrange("p (t n) -> p t n", t=TILES)
        probs = eg[:, 0:HEADS * 528].rearrange("p (h n) -> p h n", h=HEADS)
        probs_t = eg[:, HEADS * 528:HEADS * 528 + 5 * MAIN].rearrange("p (c h n) -> p c h n", c=5, h=HEADS)
        qt = heads4(take(HEADS * NT))
        small = take(3 * NT)
        kit = small[:, 0:NT]
        qit = small[:, NT:3 * NT].rearrange("p (c n) -> p c n", c=2)
        states_lo = small[:, 0:3 * MAIN].rearrange("p (s n) -> p s n", s=3)
        states_hi = take(4 * MAIN).rearrange("p (s n) -> p s n", s=4)
        att = take(TILES * MAIN).rearrange("p (t h n) -> p t h n", t=TILES, h=HEADS)
        relu_sc = att.rearrange("p t h n -> p (t h n)")[:, 0:2 * 528].rearrange("p (b n) -> p b n", b=2)
        score = take(TILES * 528).rearrange("p (t n) -> p t n", t=TILES)
        w_vw = score.rearrange("p t n -> p (t n)")[:, 0:DC * VW].rearrange("p (c n) -> p c n", c=DC)
        ropes = take(2 * NT).rearrange("p (b n) -> p b n", b=2)
        adm = take(144)
        vb = take(TILES * DH).rearrange("p (t n) -> p t n", t=TILES)
        v_tail = take(DH)
        cache = take(3 * P).rearrange("p (c n) -> p c n", c=3)
        perms = take(2 * P).rearrange("p (c n) -> p c n", c=2)
        mask_bits = sb("mask_bits", [P, 8, P])
        masks = mask_bits[:].bitcast(mybir.dt.uint32)
        smalls = sb("smalls", [P, 256])
        wi = smalls[:, 0:20].rearrange("p (t h) -> p t h", t=TILES)
        rq = smalls[:, 20:40].rearrange("p (t h) -> p t h", t=TILES)
        lb_in, lb, lb_free, lb_ln, lb_on, lb_shift, lb_e = (smalls[:, 40 + 4 * i:44 + 4 * i] for i in range(7))
        cgain = smalls[:, 68:76]
        e_last = smalls[:, 76:100].rearrange("p (h s) -> p h s", h=HEADS)
        max8 = smalls[:, 100:108]
        mx = smalls[:, 108:112]
        nbias = smalls[:, 112:116]
        psumv = smalls[:, 116:120]
        pinv = smalls[:, 120:124]
        rqs = smalls[:, 124:144].rearrange("p (t h) -> p t h", t=TILES)
        pscale = smalls[:, 144:152]
        top[0] = 0
        UE = 2 * POOL_HIST + NT
        PP0, PS0 = POOL_HIST, 2 * POOL_HIST + N_PROMPT
        ue = take(DC * UE).rearrange("p (c n) -> p c n", c=DC)
        sums = take(DC * UE).rearrange("p (c n) -> p c n", c=DC)
        sums2 = take(DC * UE).rearrange("p (c n) -> p c n", c=DC)
        pooled = take(DC * NT).rearrange("p (c n) -> p c n", c=DC)
        w_pool = take(2048).rearrange("p (g k m n) -> p g k m n", g=4, k=2, m=2)
        inv_cnt = take(64).rearrange("p (g n) -> p g n", g=4)

        ps = ctx.enter_context(nc.psum_tensor("ps", [P, 8, 512], F32))
        psf = ps[:, :, :].rearrange("p b n -> p (b n)")

        def state(i):
            return states_lo[:, i] if i < 3 else states_hi[:, i - 3]

        consts_in = sem("consts_in")
        resid_in = sem("resid_in")
        gains_in = sem("gains_in")
        weights_in = [sem("weights_in0"), sem("weights_in1")]
        unit_done = sem("unit_done")
        gmax_done, gall_done, gscale_done = sem("gmax_done"), sem("gall_done"), sem("gscale_done")
        wmax_done = sem("wmax_done")
        wall_done = sem("wall_done")
        wexp_done, wdown_done = sem("wexp_done"), sem("wdown_done")
        wscale_done = sem("wscale_done")
        wback_done = sem("wback_done")
        whigh_done = sem("whigh_done")
        wlow_done = sem("wlow_done")
        hpart_done, hmax_done, hall_done, hscale_done = sem("hpart_done"), sem("hmax_done"), sem("hall_done"), sem("hscale_done")
        hhigh_done, hlow_done = sem("hhigh_done"), sem("hlow_done")
        scaled_done, nhigh_done = sem("scaled_done"), sem("nhigh_done")
        ones_set = sem("ones_set")
        hid_done = sem("hid_done")
        silu_done = sem("silu_done")
        resid_done = sem("resid_done")
        square_done = sem("square_done")
        sumsq_zero = sem("sumsq_zero")
        sumsq_done = sem("sumsq_done")
        sumall_done = sem("sumall_done")
        root_done = sem("root_done")
        rnorm_done = sem("rnorm_done")
        normed_done = sem("normed_done")
        dve_step = sem("dve_step")
        act_step = sem("act_step")
        pool_step = sem("pool_step")
        names = """vw_in ai_in ab_in rope_in state_in vw_mm vw_evac ai_mm ai_evac raw_evac perm_mm rope_done
            isc_mm relu_done isc_acc topk_done qk_sq qsum_mm ksum_mm kroot_done k_normed qroot_done rq_done
            gate_l1 gate_min gate_a_done gate_ka gate_ln gate_logf scan_done kexp_done lb_done
            diff_done dexp_done mult_done level_mm att_zero att_evac elast_done kdt_mm kdt_evac delta_mm
            state_done sample_state head_mm head_evac osq_done osum_mm oroot_done oa_done
            logit_mm masked_done exp_done p_done pt_mm pt_evac pv_mm pv_evac
            pool_in hist_zero ue_done pwin_done pool_mm out_sem y_out kperm_mm qperm_done ao_free""".split()
        s = {n: sem(n) for n in names}

        block = ctx.enter_context(nc.Block())

        @block.sync
        def _(sync):
            sync.dma_start(gains[:], d["gains"]).then_inc(gains_in, 16)
            sync.dma_start(resid[:], d["x"]).then_inc(resid_in, 16)

            def load(src, u, b, width):
                sync.dma_start(wslot[:, b, 0:width], src[bass.ds(u, 1)].rearrange("u p n -> (u p) n")) \
                    .then_inc(weights_in[b], 16)

            def load_units(src, unit0, n, width, first=0):
                with sync.Fori(first // 2, n // 2) as i:
                    for b in range(2):
                        sync.wait_ge(unit_done, 2 * i + unit0 + b + 1)
                        load(src, 2 * i + b, b, width)

            def load_split(src, ffn_unit0, n, width, first=0):
                with sync.Fori(first // 2, n // 2) as i:
                    for b in range(2):
                        sync.wait_ge(wlow_done, 2 * i + ffn_unit0 + b + 1)
                        load(src, 2 * i + b, b, width)

            def load_ffn(f, first=0):
                load_split(d["w_up"][f], f * FFN_UNITS, FC, 2 * DC * P, first)
                load_split(d["w_dn"][f], f * FFN_UNITS + FC, DC, FC * P)

            load_ffn(0)
            for b in range(2):
                sync.wait_ge(wlow_done, FFN_UNITS + b + 1)
                load(d["w_in"], b, b, DC * P)
            load_units(d["w_in"], UNIT0[1], IN_UNITS, DC * P, first=2)
            load_units(d["w_out"], UNIT0[1] + IN_UNITS, OUT_UNITS, DC * P)
            for b in range(2):
                sync.wait_ge(unit_done, UNIT0[2] + b + 1)
                load(d["w_up"][1], b, b, 2 * DC * P)
            load_ffn(1, first=2)
            load_ffn(2)
            load_ffn(3)
            with sync.Fori(0, DC) as i:
                sync.wait_ge(resid_done, i + 2 + 5 * DC + 1)
                sync.dma_start(d["y"][:, bass.ds(i, 1), :], resid[:, bass.ds(i, 1), :]).then_inc(s["y_out"], 16)
            sync.wait_ge(s["y_out"], 16 * DC)

        @block.gpsimd
        def _(pool):
            g = nc.gpsimd

            def link(ins):
                nonlocal_step[0] += 1
                ins.then_inc(pool_step, 1)
                pool.wait_ge(pool_step, nonlocal_step[0])

            nonlocal_step = [0]
            pool.dma_start(ident[:], d["ident"]).then_inc(consts_in, 16)
            pool.dma_start(mask_bits[:], d["masks"]).then_inc(consts_in, 16)
            pool.dma_start(smalls[:, 40:44], d["lb_logits"]).then_inc(consts_in, 16)
            pool.dma_start(cgain, d["cgain"]).then_inc(consts_in, 16)
            pool.dma_start(pscale, d["pool_scale"]).then_inc(consts_in, 16)

            def all_max(n, done):
                b = done
                pool.wait_ge(wmax_done, n + 1)
                g.partition_all_reduce(wall[:, b:b + 1], wmax[:, b:b + 1], P, ALL_MAX).then_inc(wall_done, 1)

            def ffn(f, ahead):
                n0 = f * FFN_UNITS
                for u in range(2, FC + 2):
                    all_max(n0 + u, u % 2)
                pool.wait_ge(hmax_done, f + 1)
                g.partition_all_reduce(hall, hmax1, P, ALL_MAX).then_inc(hall_done, 1)
                for u in range(FC + 2, FFN_UNITS + 2 * ahead):
                    all_max(n0 + u, u % 2)

            def first_two(f):
                for b in range(2):
                    all_max(f * FFN_UNITS + b, b)

            pool.wait_ge(gmax_done, 1)
            g.partition_all_reduce(gall, gmax, P, ALL_MAX).then_inc(gall_done, 1)
            first_two(0)
            ffn(0, 0)
            pool.wait_ge(unit_done, FFN_UNITS + 2)
            pool.dma_start(adm, d["adm"]).then_inc(consts_in, 16)
            pool.dma_start(cache, d["cache"]).then_inc(consts_in, 16)
            pool.dma_start(perms, d["perms"]).then_inc(consts_in, 16)
            pool.dma_start(ropes, d["rope_idx"]).then_inc(s["rope_in"], 16)
            pool.dma_start(w_vw, d["w_vw"]).then_inc(s["vw_in"], 16)
            pool.dma_start(w_ai, d["w_ai"]).then_inc(s["ai_in"], 16)
            pool.wait_ge(s["vw_evac"], TILES)
            pool.dma_start(d["v"][:, 0:4], vb[:, 0:4]).then_inc(s["out_sem"], 16)
            pool.dma_start(d["v"][0:ROWS[4], 4], vb[0:ROWS[4], 4]).then_inc(s["out_sem"], 16)
            pool.wait_ge(s["rope_done"], 3)
            pool.dma_start(ropes, d["rope_head"]).then_inc(s["rope_in"], 16)
            pool.dma_start(d["ki"], kit[0:IDX_DIM]).then_inc(s["out_sem"], 16)
            pool.wait_ge(s["gate_l1"], 1)
            link(g.tensor_scalar(gate_b, zf, 0.0, None, ALU.min))
            g.tensor_tensor(gate_b, gate_b, gate_a, ALU.subtract).then_inc(s["gate_min"], 1)
            pool.wait_ge(s["gate_min"], 1)
            g.tensor_tensor(ka, gate_b, zf, ALU.subtract).then_inc(s["gate_min"], 1)
            pool.wait_ge(s["gate_ln"], 1)
            link(g.tensor_tensor(gate_a, gate_a, gate_b, ALU.subtract))
            pool.wait_ge(s["lb_done"], 1)
            for h in range(HEADS):
                last = g.tensor_scalar(gate_a[:, h], gate_a[:, h], lb_on[:, h:h + 1], None, ALU.mult)
            link(last)
            pool.wait_ge(s["gate_min"], 2)
            g.tensor_tensor(zf, gate_a, gate_b, ALU.add).then_inc(s["gate_logf"], 1)
            pool.wait_ge(s["isc_acc"], 4 * TILES)
            g.memset(att, 0.0).then_inc(s["att_zero"], 1)
            pool.dma_start(states_hi[:, 2], d["state"]).then_inc(s["state_in"], 16)
            pool.wait_ge(s["scan_done"], 1)
            for n, (kind, hp, h) in enumerate(DECAYS):
                if n >= 2:
                    pool.wait_ge(s["mult_done"], n - 1)
                e = decay[:, n % 2]
                b = zf[:, 2 * hp:2 * hp + 2]
                if kind == "level":
                    cols = MAIN if h == 64 else TAIL0 if h >= 16 else NT
                    ev = e[:, :, 0:cols].rearrange("p a (n x) -> p a n x", x=2 * h)
                    bv = b[:, :, 0:cols].rearrange("p a (n x) -> p a n x", x=2 * h)
                    ref = bv[:, :, :, h - 1:h].to_broadcast([P, 2, cols // (2 * h), h])
                    g.tensor_tensor(ev[:, :, :, 0:h], ref, bv[:, :, :, 0:h], ALU.subtract)
                    g.tensor_tensor(ev[:, :, :, h:2 * h], bv[:, :, :, h:2 * h], ref, ALU.subtract) \
                        .then_inc(s["diff_done"], 1)
                elif kind == "k":
                    for lo, w in ((0, P), (SMP0, N_SAMPLE), (TAIL0, TAIL)):
                        cols = MAIN if lo == 0 else w
                        ev = e[:, :, lo:lo + cols].rearrange("p a (n x) -> p a n x", x=w)
                        bv = b[:, :, lo:lo + cols].rearrange("p a (n x) -> p a n x", x=w)
                        last = g.tensor_tensor(ev, bv[:, :, :, w - 1:w].to_broadcast([P, 2, cols // w, w]), bv,
                                               ALU.subtract)
                    last.then_inc(s["diff_done"], 1)
            pool.wait_ge(s["rope_done"], 4)
            pool.dma_start(d["k"], kt).then_inc(s["out_sem"], 16)
            pool.wait_ge(s["state_done"], 5)
            pool.dma_start(d["hgrn_p"], states_hi[:, 1]).then_inc(s["out_sem"], 16)
            pool.wait_ge(s["sample_state"], 1)
            pool.dma_start(d["hgrn_s"], states_hi[:, 3]).then_inc(s["out_sem"], 16)
            first_two(1)
            ffn(1, 1)
            ffn(2, 0)
            pool.wait_ge(unit_done, UNIT0[3] + FFN_UNITS + 2)
            pool.dma_start(w_pool, d["w_pool"]).then_inc(s["pool_in"], 16)
            pool.dma_start(inv_cnt, d["inv_cnt"]).then_inc(s["pool_in"], 16)
            pool.dma_start(ue[:, :, N_PROMPT + POOL_HIST:PS0], d["state_pool"]).then_inc(s["pool_in"], 16)
            g.memset(ue[:, :, 0:POOL_HIST], 0.0).then_inc(s["hist_zero"], 1)
            pool.wait_ge(s["ue_done"], 3 * DC)
            pool.dma_start(d["pool_p"], ue[:, :, N_PROMPT:N_PROMPT + POOL_HIST]).then_inc(s["out_sem"], 16)
            pool.dma_start(d["pool_s"], ue[:, :, UE - POOL_HIST:UE]).then_inc(s["out_sem"], 16)
            first_two(3)
            ffn(3, 0)
            pool.wait_ge(s["out_sem"], 16 * 8)

        @block.scalar
        def _(act):
            a = nc.scalar
            steps = [0]

            def link(ins):
                steps[0] += 1
                ins.then_inc(act_step, 1)
                act.wait_ge(act_step, steps[0])

            def halves(bank):
                return ps[:, bank:bank + 2, 0:HALF]

            def split(ap):
                return ap.rearrange("p (b n) -> p b n", b=2)

            def root_of(stage):
                act.wait_ge(sumall_done, stage + 1)
                a.activation(split(root[:]), halves(2), ACT.Sqrt, bias=eps[:, 0:1], scale=1.0 / D_MODEL) \
                    .then_inc(root_done, 1)

            def square_chunk(stage, c, b):
                act.wait_ge(resid_done, c + 2 + DC * stage + 1)
                act.wait_ge(sumsq_done, c + DC * (stage + 1) - 1)
                a.activation(square[:, b, :], resid[:, bass.ds(c, 1), :].rearrange("p a n -> p (a n)"),
                             ACT.Square).then_inc(square_done, 1)

            def squares(stage):
                with act.Fori(0, DC // 2) as i:
                    for b in range(2):
                        square_chunk(stage, 2 * i + b, b)
                root_of(stage + 1)

            def weight_high(stage, u, b, width):
                act.wait_ge(wscale_done, u + FFN_OF_STAGE[stage] * FFN_UNITS + 1)
                act.wait_ge(unit_done, u + UNIT0[stage] + 1)
                a.activation(w16[:, b, 0, 0:width], wslot[:, b, 0:width], ACT.Copy, scale=wscale[:, b:b + 1]) \
                    .then_inc(whigh_done, 1)

            def silu(stage, u, b):
                f = FFN_OF_STAGE[stage]
                act.wait_ge(unit_done, u + UNIT0[stage] + 2 + 1)
                act.wait_ge(hid_done, u + FC * f + 1)
                act.wait_ge(wback_done, u + f * FFN_UNITS + 1)
                a.activation(split(act_out[:, b, :]), halves(4 * b), ACT.Silu, scale=wback[:, b:b + 1]) \
                    .then_inc(silu_done, 1)

            def normed_high(f):
                for c in range(DC):
                    act.wait_ge(scaled_done, DC * f + c + 1)
                    a.activation(normed16[:, 0, c, :], square[:, c % 2, :], ACT.Copy).then_inc(nhigh_done, 1)

            def ffn(stage, next_stage=None, last=False):
                f = FFN_OF_STAGE[stage]
                normed_high(f)
                weight_high(stage, 1, 1, UP_W)
                with act.Fori(0, FC // 2 - 1) as i:
                    for b in range(2):
                        silu(stage, 2 * i + b, b)
                        weight_high(stage, 2 * i + b + 2, b, UP_W)
                silu(stage, FC - 2, 0)
                weight_high(stage, FC, 0, DN_W)
                silu(stage, FC - 1, 1)
                act.wait_ge(hscale_done, f + 1)
                with act.Fori(0, FC) as i:
                    a.activation(hidden16[:, 0, bass.ds(i, 1), :].rearrange("p a n -> p (a n)"),
                                 hidden[:, bass.ds(i, 1), :].rearrange("p a n -> p (a n)"), ACT.Copy,
                                 scale=hscale).then_inc(hhigh_done, 1)
                weight_high(stage, FC + 1, 1, DN_W)
                with act.Fori(0, DC // 2 - 1) as i:
                    for b in range(2):
                        weight_high(stage, 2 * i + b + FC + 2, b, DN_W)
                        if not last:
                            square_chunk(stage, 2 * i + b, b)
                if next_stage:
                    weight_high(next_stage, 0, 0, UP_W)
                if not last:
                    for c in range(DC - 2, DC):
                        square_chunk(stage, c, c % 2)
                    root_of(stage + 1)

            weight_high(0, 0, 0, UP_W)
            act.wait_ge(resid_in, 16)
            act.wait_ge(ones_set, 3)
            for c in range(DC):
                if c >= 2:
                    act.wait_ge(sumsq_done, c - 1)
                a.activation(square[:, c % 2, :], resid[:, c, :], ACT.Square).then_inc(square_done, 1)
            root_of(0)
            ffn(0)

            U = UNIT0[1] + 2
            for t in range(TILES):
                act.wait_ge(s["vw_mm"], t + 1)
                r = ROWS[t]
                a.activation(vb[0:r, t], ps[0:r, 4 + t % 2, 0:DH], ACT.Copy)
                if t == 4:
                    a.activation(v_tail[0:TAIL], ps[N_SAMPLE:r, 4, 0:DH], ACT.Copy)
                a.activation(wi[0:r, t], ps[0:r, 4 + t % 2, DH:VW], ACT.Copy, scale=IDX_HEADS ** -0.5) \
                    .then_inc(s["vw_evac"], 1)
            for n, dst in enumerate((kit, qit[:, 0], qit[:, 1])):
                act.wait_ge(unit_done, U + n + 1)
                a.activation(split(dst), halves(2 * (n % 2)), ACT.Copy).then_inc(s["raw_evac"], 1)
            for t in range(TILES):
                act.wait_ge(s["ai_mm"], t + 1)
                a.activation(va[0:ROWS[t], t], ps[0:ROWS[t], 4 + t % 2, :], ACT.Copy).then_inc(s["ai_evac"], 1)
            n = 0
            for t in range(TILES):
                for h in range(IDX_HEADS):
                    act.wait_ge(s["isc_mm"], n + 1)
                    if n >= 2:
                        act.wait_ge(s["isc_acc"], n - 1)
                    bank = 4 + 2 * (n % 2)
                    a.activation(relu_sc[0:ROWS[t], n % 2, 0:WIDTH[t]],
                                 psf[0:ROWS[t], bank * 512:bank * 512 + WIDTH[t]], ACT.Relu,
                                 scale=IDX_DIM ** -0.5).then_inc(s["relu_done"], 1)
                    n += 1
            act.wait_ge(unit_done, U + 3 + 1)
            a.activation(split(kt), halves(2), ACT.Copy).then_inc(s["raw_evac"], 1)
            a.activation(split(square[:, 0, :]), halves(2), ACT.Square).then_inc(s["qk_sq"], 1)
            for h in range(HEADS):
                b = 2 * ((4 + h) % 2)
                act.wait_ge(unit_done, U + 4 + h + 1)
                a.activation(split(qt[:, h]), halves(b), ACT.Copy, scale=cgain[:, 0:1])
                if h >= 1:
                    act.wait_ge(s["ksum_mm" if h == 1 else "qsum_mm"], 1 if h == 1 else h - 1)
                a.activation(split(square[:, (h + 1) % 2, :]), halves(b), ACT.Square).then_inc(s["qk_sq"], 1)
            for h in range(HEADS):
                act.wait_ge(unit_done, U + 8 + h + 1)
                a.activation(split(zf[:, h]), halves(2 * (h % 2)), ACT.Copy).then_inc(s["raw_evac"], 1)
            act.wait_ge(s["raw_evac"], 8)
            act.wait_ge(s["ai_mm"], TILES)
            link(a.activation(gate_a, zf, ACT.Abs))
            link(a.activation(gate_a, gate_a, ACT.Exp, scale=-1.0))
            a.activation(gate_a, gate_a, ACT.Ln, bias=ones[:, 0:1]).then_inc(s["gate_l1"], 1)

            def proj(n, dst, h, func):
                act.wait_ge(unit_done, U + n + 1)
                a.activation(split(dst[:, h]), halves(2 * (n % 2)), func).then_inc(s["raw_evac"], 1)

            for h in range(HEADS):
                proj(12 + h, qa, h, ACT.Silu)
            act.wait_ge(s["qsum_mm"], 4)
            a.activation(rqs[:, 0:4], ps[:, 4, 0:16].rearrange("p (t h) -> p t h", t=4), ACT.Sqrt, bias=eps[:, 0:1],
                         scale=1.0 / DH)
            a.activation(rqs[0:ROWS[4], 4], ps[0:ROWS[4], 4, 16:20], ACT.Sqrt, bias=eps[0:ROWS[4], 0:1],
                         scale=1.0 / DH).then_inc(s["qroot_done"], 1)
            act.wait_ge(s["ksum_mm"], 1)
            a.activation(split(root[:]), halves(6), ACT.Sqrt, bias=eps[:, 0:1], scale=1.0 / DH) \
                .then_inc(s["kroot_done"], 1)
            for h in range(HEADS):
                proj(16 + h, ag, h, ACT.Sigmoid)
            act.wait_ge(s["gate_min"], 2)
            act.wait_ge(s["lb_done"], 1)
            link(a.activation(lb_ln, lb_free, ACT.Ln))
            for h in range(HEADS):
                last = a.activation(gate_a[:, h], gate_b[:, h], ACT.Exp, bias=lb_ln[:, h:h + 1])
            link(last)
            for h in range(HEADS):
                last = a.activation(gate_a[:, h], gate_a[:, h], ACT.Ln, bias=lb_shift[:, h:h + 1])
            last.then_inc(s["gate_ln"], 1)
            for h in range(HEADS):
                last = a.activation(ka[:, h], ka[:, h], ACT.Exp, bias=lb_ln[:, h:h + 1])
            last.then_inc(s["gate_ka"], 1)
            act.wait_ge(s["scan_done"], 1)
            diffs = 0
            for n, (kind, hp, h) in enumerate(DECAYS):
                cols = NT if kind != "level" else MAIN if h == 64 else TAIL0 if h >= 16 else NT
                e = decay[:, n % 2, :, 0:cols]
                if kind == "q":
                    act.wait_ge(s["mult_done"], n - 1)
                    a.activation(e, zf[:, 2 * hp:2 * hp + 2], ACT.Exp).then_inc(s["dexp_done"], 1)
                else:
                    diffs += 1
                    act.wait_ge(s["diff_done"], diffs)
                    a.activation(e, e, ACT.Exp).then_inc(s["dexp_done"], 1)
            a.activation(e_last[:, :, 0:4], zf[:, :, P - 1:MAIN:P], ACT.Exp)
            a.activation(e_last[:, :, 4:5], zf[:, :, TAIL0 - 1:TAIL0], ACT.Exp)
            a.activation(e_last[:, :, 5:6], zf[:, :, NT - 1:NT], ACT.Exp).then_inc(s["elast_done"], 1)
            act.wait_ge(s["mult_done"], len(DECAYS))
            for t in range(TILES):
                act.wait_ge(s["kdt_mm"], t + 1)
                if t == 0:
                    act.wait_ge(s["level_mm"], 16)
                a.activation(kd_tok[0:ROWS[t], t], ps[0:ROWS[t], 6 + t % 2, :], ACT.Copy).then_inc(s["kdt_evac"], 1)
            for t in range(TILES):
                act.wait_ge(s["head_mm"], t + 1)
                if t == 0:
                    act.wait_ge(s["elast_done"], 1)
                r = ROWS[t]
                a.activation(zf[:, :, t * P:t * P + r],
                             ps[:, 6 + t % 2, :].rearrange("p (h n) -> p h n", h=HEADS)[:, :, 0:r], ACT.Copy) \
                    .then_inc(s["head_evac"], 1)
            act.wait_ge(s["head_evac"], TILES)
            for h in range(HEADS):
                if h >= 2:
                    act.wait_ge(s["osum_mm"], h - 1)
                a.activation(square[:, h % 2, :], zf[:, h], ACT.Square).then_inc(s["osq_done"], 1)
            for h in range(HEADS):
                act.wait_ge(s["osum_mm"], h + 1)
                act.wait_ge(s["k_normed"], 1)
                if h >= 1:
                    act.wait_ge(s["oa_done"], h)
                a.activation(split(root[:]), halves(2 * (h % 2)), ACT.Sqrt, bias=eps[:, 0:1], scale=1.0 / DH) \
                    .then_inc(s["oroot_done"], 1)
            ev = 0
            for t in range(TILES):
                r = ROWS[t]
                for h in range(HEADS):
                    act.wait_ge(s["masked_done"], t * HEADS + h + 1)
                    a.activation(probs[0:r, h, 0:WIDTH[t]], probs[0:r, h, 0:WIDTH[t]], ACT.Exp,
                                 bias=nbias[0:r, h:h + 1], scale=rq[0:r, t, h:h + 1],
                                 accum_out=psumv[0:r, h:h + 1]).then_inc(s["exp_done"], 1)
                for c, (kw, kc, parts) in enumerate(key_chunks(t)):
                    act.wait_ge(s["pt_mm"], ev + 1)
                    if c == 0 and t > 0:
                        act.wait_ge(s["pv_mm"], t)
                    for lo, n in parts:
                        last = a.activation(probs_t[0:kw, c, :, lo:lo + n],
                                            ps[0:kw, 4 + ev % 2, :].rearrange("p (h n) -> p h n", h=HEADS)[:, :, lo:lo + n],
                                            ACT.Copy)
                    last.then_inc(s["pt_evac"], 1)
                    ev += 1
                act.wait_ge(s["pv_mm"], t + 1)
                a.activation(normed[:, 4:8, t * P:t * P + r],
                             ps[:, 6 + t % 2, :].rearrange("p (h n) -> p h n", h=HEADS)[:, :, 0:r], ACT.Copy) \
                    .then_inc(s["pv_evac"], 1)
            squares(1)
            weight_high(2, 0, 0, UP_W)
            ffn(2, next_stage=3)
            ffn(3)
            weight_high(5, 0, 0, UP_W)
            squares(4)
            ffn(5, last=True)

        @block.vector
        def _(dve):
            v = nc.vector
            steps = [0]

            def link(ins):
                steps[0] += 1
                ins.then_inc(dve_step, 1)
                dve.wait_ge(dve_step, steps[0])

            def halves(bank):
                return ps[:, bank:bank + 2, 0:HALF]

            def split(ap):
                return ap.rearrange("p (b n) -> p b n", b=2)

            def norm(stage, write=None):
                dve.wait_ge(root_done, stage + 1)
                v.reciprocal(rnorm[:], root[:]).then_inc(rnorm_done, 1)
                dve.wait_ge(rnorm_done, stage + 1)
                v.memset(square_sum[:], 0.0).then_inc(sumsq_zero, 1)
                if stage in FFN_OF_STAGE:
                    f = FFN_OF_STAGE[stage]
                    for c in range(DC + 1):
                        if 2 <= c < DC:
                            dve.wait_ge(normed_done, DC * NORMED[stage] + c - 1)
                        if c < DC:
                            v.scalar_tensor_tensor(square[:, c % 2, :], resid[:, c, :], gains16[:, stage, c:c + 1],
                                                   rnorm[:], ALU.mult, ALU.mult).then_inc(scaled_done, 1)
                        if c:
                            dve.wait_ge(scaled_done, DC * f + c)
                            dve.wait_ge(nhigh_done, DC * f + c)
                            v.tensor_tensor(normed16[:, 1, c - 1, :], square[:, (c - 1) % 2, :],
                                            normed16[:, 0, c - 1, :], ALU.subtract).then_inc(normed_done, 1)
                    return
                for c in range(DC):
                    if write:
                        write(c)
                    else:
                        v.scalar_tensor_tensor(normed[:, c, :], resid[:, c, :], gains[:, stage, c:c + 1], rnorm[:],
                                               ALU.mult, ALU.mult).then_inc(normed_done, 1)

            def add_one(base, c, b):
                dve.wait_ge(square_done, c + base + 1)
                dve.wait_ge(sumsq_done, c + base)
                v.tensor_tensor(square_sum[:], square_sum[:], square[:, b, :], ALU.add).then_inc(sumsq_done, 1)

            def add_squares(base, i, b):
                add_one(base, i + b, b)

            def update_chunk(stage, unit, c, b, factor):
                dve.wait_ge(unit_done, unit + 2 + 1)
                r = split(resid[:, bass.ds(c, 1), :].rearrange("p a n -> p (a n)"))
                v.scalar_tensor_tensor(r, halves(4 * b), factor, r, ALU.mult, ALU.add).then_inc(resid_done, 1)

            def update_residual(stage, unit0, factor):
                dve.wait_ge(sumsq_zero, stage + 1)
                with dve.Fori(0, DC // 2) as i:
                    for b in range(2):
                        update_chunk(stage, 2 * i + b + unit0, 2 * i + b, b, factor)
                    for b in range(2):
                        add_squares(DC * (stage + 1), 2 * i, b)

            def weight_max(stage, u, b, width):
                n = u + UNIT0[stage]
                slot_loads = (n - b) // 2 if isinstance(n, int) else None
                dve.wait_ge(weights_in[b], 16 * (slot_loads + 1) if slot_loads is not None else n * 8 + 16 - 8 * b)
                v.tensor_reduce(wmax[:, b:b + 1], wslot[:, b, 0:width], AXIS_X, ALU.max, apply_absolute_value=True) \
                    .then_inc(wmax_done, 1)

            def weight_scale(stage, u, b):
                n = u + FFN_OF_STAGE[stage] * FFN_UNITS + 1
                dve.wait_ge(wall_done, n)
                v.tensor_scalar(wexp[:, b:b + 1].bitcast(U32), wall[:, b:b + 1].bitcast(U32), EXPONENT, None,
                                ALU.bitwise_and).then_inc(wexp_done, 1)
                dve.wait_ge(wexp_done, n)
                v.tensor_scalar(wdown[:, b:b + 1], wexp[:, b:b + 1], 2.0 ** -13, TINY, ALU.mult, ALU.max) \
                    .then_inc(wdown_done, 1)
                dve.wait_ge(wdown_done, n)
                v.reciprocal(wscale[:, b:b + 1], wdown[:, b:b + 1]).then_inc(wscale_done, 1)

            def weight_back(stage, u, b, inv):
                v.tensor_scalar(wback[:, b:b + 1], wdown[:, b:b + 1], inv, None, ALU.mult).then_inc(wback_done, 1)

            def weight_low(stage, u, b, width):
                dve.wait_ge(whigh_done, u + FFN_OF_STAGE[stage] * FFN_UNITS + 1)
                v.scalar_tensor_tensor(w16[:, b, 1, 0:width], wslot[:, b, 0:width], wscale[:, b:b + 1],
                                       w16[:, b, 0, 0:width], ALU.mult, ALU.subtract).then_inc(wlow_done, 1)

            def first_unit(stage):
                weight_max(stage, 0, 0, UP_W)
                weight_scale(stage, 0, 0)
                weight_back(stage, 0, 0, inv_x[:, stage:stage + 1])
                weight_low(stage, 0, 0, UP_W)
                weight_max(stage, 1, 1, UP_W)

            def hidden_chunk(stage, u, b):
                f = FFN_OF_STAGE[stage]
                dve.wait_ge(silu_done, u + FC * f + 1)
                dve.wait_ge(wback_done, u + f * FFN_UNITS + 1)
                h = hidden[:, bass.ds(u, 1), :].rearrange("p a n -> p (a n)")
                v.scalar_tensor_tensor(split(h), halves(4 * b + 2), wback[:, b:b + 1], split(act_out[:, b, :]),
                                       ALU.mult, ALU.mult).then_inc(hid_done, 1)
                dve.wait_ge(hid_done, u + FC * f + 2 + 1)
                v.tensor_reduce(hmax[:, bass.ds(u, 1)], h, AXIS_X, ALU.max, apply_absolute_value=True) \
                    .then_inc(hpart_done, 1)

            def ffn(stage, next_stage=None, last=False):
                f = FFN_OF_STAGE[stage]
                ix = inv_x[:, stage:stage + 1]
                weight_scale(stage, 1, 1)
                weight_back(stage, 1, 1, ix)
                weight_low(stage, 1, 1, UP_W)
                weight_max(stage, 2, 0, UP_W)

                def up_turn(u, b, next_w, after_w):
                    weight_scale(stage, u + 1, 1 - b)
                    hidden_chunk(stage, u - 1, 1 - b)
                    if next_w == UP_W:
                        weight_back(stage, u + 1, 1 - b, ix)
                    weight_low(stage, u + 1, 1 - b, next_w)
                    weight_max(stage, u + 2, b, after_w)

                with dve.Fori(0, FC // 2 - 2) as i:
                    up_turn(2 * i + 1, 1, UP_W, UP_W)
                    up_turn(2 * i + 2, 0, UP_W, UP_W)
                up_turn(FC - 3, 1, UP_W, UP_W)
                up_turn(FC - 2, 0, UP_W, DN_W)
                up_turn(FC - 1, 1, DN_W, DN_W)
                hidden_chunk(stage, FC - 1, 1)
                dve.wait_ge(hpart_done, FC * (f + 1))
                v.tensor_reduce(hmax1, hmax, AXIS_X, ALU.max).then_inc(hmax_done, 1)
                dve.wait_ge(hall_done, f + 1)
                link(v.tensor_scalar(hexp.bitcast(U32), hall.bitcast(U32), EXPONENT, None, ALU.bitwise_and))
                link(v.tensor_scalar(hdown, hexp, 2.0 ** -13, TINY, ALU.mult, ALU.max))
                v.reciprocal(hscale, hdown).then_inc(hscale_done, 1)
                link(v.tensor_scalar(inv_h, hdown, 0.5, None, ALU.mult))
                weight_back(stage, FC, 0, inv_h)
                dve.wait_ge(hscale_done, f + 1)
                with dve.Fori(0, FC) as i:
                    dve.wait_ge(hhigh_done, i + FC * f + 1)
                    v.scalar_tensor_tensor(hidden16[:, 1, bass.ds(i, 1), :].rearrange("p a n -> p (a n)"),
                                           hidden[:, bass.ds(i, 1), :].rearrange("p a n -> p (a n)"), hscale,
                                           hidden16[:, 0, bass.ds(i, 1), :].rearrange("p a n -> p (a n)"),
                                           ALU.mult, ALU.subtract).then_inc(hlow_done, 1)
                dve.wait_ge(sumsq_zero, stage + 1)

                def down_turn(u, c, b, back=True, split_next=True, after=None, add=True):
                    if split_next:
                        weight_scale(stage, u + 1, 1 - b)
                    if c is not None:
                        dve.wait_ge(wback_done, u - 1 + f * FFN_UNITS + 1)
                        update_chunk(stage, u - 1 + UNIT0[stage], c, 1 - b, wback[:, 1 - b:2 - b])
                    if split_next:
                        if c is not None:
                            dve.wait_ge(resid_done, c + 2 + DC * stage + 1)
                        weight_back(stage, u + 1, 1 - b, inv_h)
                        weight_low(stage, u + 1, 1 - b, DN_W)
                    if after:
                        weight_max(stage, u + 2, b, after)
                    if add and not last:
                        add_one(DC * (stage + 1), c - 1, b)

                down_turn(FC, None, 0, after=DN_W, add=False)
                down_turn(FC + 1, 0, 1, after=DN_W, add=False)
                with dve.Fori(0, DC // 2 - 2) as i:
                    down_turn(2 * i + FC + 2, 2 * i + 1, 0, after=DN_W)
                    down_turn(2 * i + FC + 3, 2 * i + 2, 1, after=DN_W)
                down_turn(FFN_UNITS - 2, DC - 3, 0)
                if next_stage:
                    weight_max(next_stage, 0, 0, UP_W)
                    weight_scale(next_stage, 0, 0)
                down_turn(FFN_UNITS - 1, DC - 2, 1, split_next=False)
                if next_stage:
                    dve.wait_ge(resid_done, DC * stage + DC + 1)
                    weight_back(next_stage, 0, 0, inv_x[:, next_stage:next_stage + 1])
                    weight_low(next_stage, 0, 0, UP_W)
                    weight_max(next_stage, 1, 1, UP_W)
                dve.wait_ge(wback_done, FFN_UNITS * (f + 1))
                update_chunk(stage, UNIT0[stage] + FFN_UNITS - 1, DC - 1, 1, wback[:, 1:2])
                if not last:
                    for c in range(DC - 2, DC):
                        add_one(DC * (stage + 1), c, c % 2)

            v.memset(ones[:], 1.0).then_inc(ones_set, 1)
            v.memset(eps[:], RMS_EPS).then_inc(ones_set, 1)
            v.memset(square_sum[:], 0.0).then_inc(ones_set, 1)
            v.memset(act_out[:, 0, 0:1], 0.0).then_inc(hid_done, 2)
            v.memset(act_out[:, 0, 1:2], 0.0).then_inc(resid_done, 2)
            v.memset(act_out[:, 0, 2:3], 0.0).then_inc(wlow_done, 2)
            dve.wait_ge(gains_in, 16)
            v.tensor_reduce(gmax, gains[:], AXIS_X, ALU.max, apply_absolute_value=True).then_inc(gmax_done, 1)
            dve.wait_ge(gall_done, 1)
            link(v.tensor_scalar(gexp.bitcast(U32), gall.bitcast(U32), EXPONENT, None, ALU.bitwise_and))
            link(v.tensor_scalar(inv_x, gexp, 2.0 ** -9, TINY, ALU.mult, ALU.max))
            link(v.reciprocal(gscale, inv_x))
            link(v.tensor_tensor(gains16, gains[:], gscale.rearrange("p (s a) -> p s a", a=1).to_broadcast([P, 6, DC]),
                                 ALU.mult))
            first_unit(0)
            dve.wait_ge(ones_set, 3)
            for c in range(DC):
                dve.wait_ge(square_done, c + 1)
                if c:
                    dve.wait_ge(sumsq_done, c)
                v.tensor_tensor(square_sum[:], square_sum[:], square[:, c % 2, :], ALU.add).then_inc(sumsq_done, 1)
            norm(0)
            ffn(0)
            norm(1)

            dve.wait_ge(consts_in, 16 * 8)
            link(v.tensor_tensor(lb_e, lb_in, lb_in, ALU.subtract))
            link(v.tensor_scalar(lb_e, lb_e, 1.0, None, ALU.add))
            link(v.reciprocal(lb_shift, lb_e))
            link(v.tensor_tensor(lb_e, lb_e, lb_shift, ALU.mult))
            link(v.tensor_tensor(lb, lb_e, lb_e, ALU.subtract))
            link(v.tensor_scalar(lb_free, lb, -1.0, 1.0, ALU.mult, ALU.add))
            link(v.tensor_scalar(lb_on, lb, 0.0, None, ALU.is_gt))
            link(v.tensor_scalar(lb_e, lb_on, -1.0, 1.0, ALU.mult, ALU.add))
            v.tensor_tensor(lb_shift, lb, lb_e, ALU.add).then_inc(s["lb_done"], 1)
            def rope(x, table, bank):
                link(v.tensor_tensor(x, x, ropes[:, 0], ALU.mult))
                link(v.tensor_tensor(split(act_out[:, 0, :]), halves(bank), split(ropes[:, 1]), ALU.mult))
                v.tensor_tensor(x, x, act_out[:, 0, :], ALU.add).then_inc(s["rope_done"], 1)

            dve.wait_ge(s["rope_in"], 16)
            for n, x in enumerate((kit, qit[:, 0], qit[:, 1])):
                dve.wait_ge(s["perm_mm"], n + 1)
                rope(x, 0, 6)
            n = 0
            for t in range(TILES):
                r, w = ROWS[t], WIDTH[t]
                for h in range(IDX_HEADS):
                    dve.wait_ge(s["relu_done"], n + 1)
                    if h == 0:
                        if t == 0:
                            dve.wait_ge(s["vw_evac"], TILES)
                        ins = v.tensor_scalar(score[0:r, t, 0:w], relu_sc[0:r, n % 2, 0:w], wi[0:r, t, 0:1], None,
                                              ALU.mult)
                    else:
                        ins = v.scalar_tensor_tensor(score[0:r, t, 0:w], relu_sc[0:r, n % 2, 0:w],
                                                     wi[0:r, t, h:h + 1], score[0:r, t, 0:w], ALU.mult, ALU.add)
                    ins.then_inc(s["isc_acc"], 1)
                    n += 1
                    dve.wait_ge(s["isc_acc"], n)
                if t < 4:
                    link(v.tensor_tensor(score[:, t, t * P:t * P + 144], score[:, t, t * P:t * P + 144], adm, ALU.add))
                else:
                    last = PAST + N_SAMPLE
                    link(v.memset(score[0:N_SAMPLE, t, last:last + TOPK - TOPK_SAMPLE], PAD_TOP))
                    link(v.memset(score[0:N_SAMPLE, t, last + TOPK - TOPK_SAMPLE:528], NEG_BIG))
            for t in range(TILES):
                sc = score[0:ROWS[t], t, 0:WIDTH[t]]
                for _ in range(TOPK // 8):
                    link(v.max(max8[0:ROWS[t]], sc))
                    link(v.match_replace(sc, max8[0:ROWS[t]], sc, TAKEN))
                link(v.tensor_scalar(sc, sc, -2e38, NEG_BIG, ALU.is_gt, ALU.mult))
                if t < 4:
                    link(v.tensor_tensor(score[:, t, t * P:t * P + 144], score[:, t, t * P:t * P + 144], adm, ALU.min))
                else:
                    link(v.memset(score[0:N_SAMPLE, t, PAST + N_SAMPLE:528], NEG_BIG))
            dve.wait_ge(s["kroot_done"], 1)
            link(v.reciprocal(rnorm[:], root[:]))
            v.scalar_tensor_tensor(kt, kt, cgain[:, 1:2], rnorm[:], ALU.mult, ALU.mult).then_inc(s["k_normed"], 1)
            dve.wait_ge(s["k_normed"], 1)
            dve.wait_ge(s["rope_in"], 32)
            dve.wait_ge(s["qroot_done"], 1)
            link(v.reciprocal(rq[:, 0:4], rqs[:, 0:4]))
            link(v.reciprocal(rq[0:ROWS[4], 4], rqs[0:ROWS[4], 4]))
            link(v.tensor_scalar(rq[:, 0:4], rq[:, 0:4], DH ** -0.5, None, ALU.mult))
            link(v.tensor_scalar(rq[0:ROWS[4], 4], rq[0:ROWS[4], 4], DH ** -0.5, None, ALU.mult))
            for n in range(5):
                dve.wait_ge(s["kperm_mm"], n + 1)
                rope(kt if n == 0 else qt[:, n - 1], 1, 2 * (n % 2))
                dve.wait_ge(s["rope_done"], 3 + n + 1)
            dve.wait_ge(s["gate_logf"], 1)
            for h in range(HEADS):
                for lo, w in SEGMENTS:
                    last = v.tensor_tensor_scan(zf[:, h, lo:lo + w], ones[:, 0:w], zf[:, h, lo:lo + w], 0.0, ALU.mult,
                                                ALU.add)
            last.then_inc(s["scan_done"], 1)
            dve.wait_ge(s["gate_ka"], 1)
            dve.wait_ge(s["raw_evac"], 16)
            dve.wait_ge(s["att_zero"], 1)
            nd = lv = 0

            def collect(n):
                kind, hp, h = LEVEL_PASSES[n]
                m = LEVELS.index(h) if kind == "level" else len(LEVELS)
                dve.wait_ge(s["level_mm"], n + 1)
                if n:
                    dve.wait_ge(s["att_evac"], n)
                for pair in range(2):
                    last = v.copy_predicated(
                        att[:, 2 * pair:2 * pair + 2, 2 * hp:2 * hp + 2, :],
                        masks[:, m:m + 1, :].rearrange("p (a b) n -> p a b n", b=1).to_broadcast([P, 2, 2, P]),
                        ps[:, 3 * (n % 2) + pair, :].rearrange("p (a b n) -> p a b n", a=2, b=2))
                if not (kind == "level" and h == 64):
                    r = N_SAMPLE if kind == "level" and h >= 16 else ROWS[4]
                    last = v.copy_predicated(
                        att[0:r, 4, 2 * hp:2 * hp + 2, 0:r],
                        masks[0:r, m:m + 1, 0:r].to_broadcast([r, 2, r]),
                        ps[0:r, 3 * (n % 2) + 2, 0:256].rearrange("p (b n) -> p b n", b=2)[:, :, 0:r])
                last.then_inc(s["att_evac"], 1)

            lv = 0
            for kind, hp, h in PASSES:
                if kind == "diag":
                    lv += 1
                    collect(lv - 2)
                    continue
                dve.wait_ge(s["dexp_done"], nd + 1)
                e, gd = decay[:, nd % 2], decayed[:, lv % 2]
                k2, q2 = ka[:, 2 * hp:2 * hp + 2], qa[:, 2 * hp:2 * hp + 2]
                if kind == "level":
                    if lv >= 2:
                        dve.wait_ge(s["level_mm"], lv - 1)
                    cols = MAIN if h == 64 else TAIL0 if h >= 16 else NT

                    def blocks(ap):
                        return ap[:, :, 0:cols].rearrange("p a (n x) -> p a n x", x=2 * h)
                    v.tensor_tensor(blocks(gd)[:, :, :, 0:h], blocks(e)[:, :, :, 0:h], blocks(k2)[:, :, :, 0:h], ALU.mult)
                    v.tensor_tensor(blocks(gd)[:, :, :, h:2 * h], blocks(e)[:, :, :, h:2 * h],
                                    blocks(q2)[:, :, :, h:2 * h], ALU.mult).then_inc(s["mult_done"], 1)
                    lv += 1
                    if h != LEVELS[0]:
                        collect(lv - 2)
                else:
                    if kind == "q":
                        collect(lv - 1)
                        v.tensor_tensor(q2, q2, e, ALU.mult).then_inc(s["mult_done"], 1)
                    else:
                        v.tensor_tensor(k2, k2, e, ALU.mult).then_inc(s["mult_done"], 1)
                nd += 1
            dve.wait_ge(s["elast_done"], 1)
            dve.wait_ge(s["state_in"], 16)
            dve.wait_ge(s["out_sem"], 16 * 4)
            for i in range(6):
                dve.wait_ge(s["delta_mm"], i + 1)
                src = states_hi[:, 2] if i == 5 else state(max(i - 1, 0))
                dst = states_hi[:, 3] if i == 5 else state(i)
                seg = (0, 1, 2, 3, 5, 4)[i]
                if i == 0:
                    last = v.tensor_copy(dst, ps[:, 0, :])
                else:
                    if i < 5:
                        dve.wait_ge(s["state_done"], i)
                    for h in range(HEADS):
                        c = slice(h * DH, (h + 1) * DH)
                        last = v.scalar_tensor_tensor(dst[:, c], src[:, c], e_last[:, h, seg:seg + 1], ps[:, i, c],
                                                      ALU.mult, ALU.add)
                last.then_inc(s["state_done"] if i < 5 else s["sample_state"], 1)
            for h in range(HEADS):
                dve.wait_ge(s["oroot_done"], h + 1)
                link(v.reciprocal(rnorm[:], root[:]))
                link(v.scalar_tensor_tensor(rnorm[:], rnorm[:], cgain[:, 4 + h:5 + h], ag[:, h], ALU.mult, ALU.mult))
                v.tensor_tensor(normed[:, h, :], zf[:, h], rnorm[:], ALU.mult).then_inc(s["oa_done"], 1)
                dve.wait_ge(s["oa_done"], h + 1)
            for t in range(TILES):
                r, w = ROWS[t], WIDTH[t]
                for h in range(HEADS):
                    dve.wait_ge(s["logit_mm"], t * HEADS + h + 1)
                    if h == 0 and t:
                        dve.wait_ge(s["pt_mm"], sum(len(key_chunks(x)) for x in range(t)))
                    bank = 2 * (h % 2)
                    link(v.tensor_tensor_reduce(out=probs[0:r, h, 0:w], in0=psf[0:r, bank * 512:bank * 512 + w],
                                                in1=score[0:r, t, 0:w], scale=1.0, scalar=TAKEN, op0=ALU.add,
                                                op1=ALU.max, accum_out=mx[0:r, h:h + 1]))
                    v.tensor_scalar(nbias[0:r, h:h + 1], mx[0:r, h:h + 1], rq[0:r, t, h:h + 1], -1.0, ALU.mult,
                                    ALU.mult).then_inc(s["masked_done"], 1)
                    dve.wait_ge(s["masked_done"], t * HEADS + h + 1)
                for h in range(HEADS):
                    dve.wait_ge(s["exp_done"], t * HEADS + h + 1)
                    link(v.reciprocal(pinv[0:r, h:h + 1], psumv[0:r, h:h + 1]))
                    v.tensor_scalar(probs[0:r, h, 0:w], probs[0:r, h, 0:w], pinv[0:r, h:h + 1], None, ALU.mult) \
                        .then_inc(s["p_done"], 1)
            dve.wait_ge(s["out_sem"], 16 * 6)
            update_residual(1, UNIT0[1] + IN_UNITS, 1.0)
            first_unit(2)
            norm(2)
            ffn(2, next_stage=3)
            norm(3)
            ffn(3)

            def to_ue(c):
                if c == 0:
                    dve.wait_ge(unit_done, UNIT0[3] + FFN_UNITS + 2)
                    dve.wait_ge(resid_done, 2 + DC * 4)
                for lo, n, dst in ((0, MAIN, PP0), (TAIL0, TAIL, PP0 + MAIN), (SMP0, N_SAMPLE, PS0)):
                    v.scalar_tensor_tensor(ue[:, c, dst:dst + n], resid[:, c, lo:lo + n], gains[:, 4, c:c + 1],
                                           rnorm[:, lo:lo + n], ALU.mult, ALU.mult).then_inc(s["ue_done"], 1)
            norm(4, to_ue)
            dve.wait_ge(s["ue_done"], 3 * DC)
            dve.wait_ge(s["pool_in"], 48)
            dve.wait_ge(s["hist_zero"], 1)
            bufs = (sums, sums2)
            for gi, w in enumerate(POOL_WINDOWS):
                cs = slice(2 * gi, 2 * gi + 2)
                src, step, k = ue[:, cs], 1, 0
                while step < w:
                    dst = bufs[k % 2][:, cs]
                    lo = 2 * step - 1
                    link(v.tensor_tensor(dst[:, :, lo:UE], src[:, :, lo:UE], src[:, :, lo - step:UE - step], ALU.add))
                    src, step, k = dst, 2 * step, k + 1
                dst = bufs[k % 2][:, cs]
                link(v.tensor_tensor(dst[:, :, PP0:PP0 + 16], src[:, :, PP0:PP0 + 16],
                                     inv_cnt[:, gi:gi + 1, :].to_broadcast([P, 2, 16]), ALU.mult))
                link(v.tensor_scalar(dst[:, :, PP0 + 16:UE], src[:, :, PP0 + 16:UE], 1.0 / w, None, ALU.mult))
                for lo, n, at in ((0, MAIN, PP0), (TAIL0, TAIL, PP0 + MAIN), (SMP0, N_SAMPLE, PS0)):
                    last = v.tensor_tensor(pooled[:, cs, lo:lo + n], dst[:, :, at:at + n], ue[:, cs, at:at + n],
                                           ALU.subtract)
                last.then_inc(s["pwin_done"], 1)
            first_unit(5)
            dve.wait_ge(sumsq_zero, 5)
            for c in range(DC):
                dve.wait_ge(s["pool_mm"], c + 1)
                r = split(resid[:, c, :])
                v.scalar_tensor_tensor(r, halves(4 * (c % 2)), pscale[:, c:c + 1], r, ALU.mult, ALU.add) \
                    .then_inc(resid_done, 1)
                if c % 2:
                    for b in range(2):
                        add_squares(DC * 5, c - 1, b)
            norm(5)
            dve.wait_ge(s["out_sem"], 16 * 8)
            ffn(5, last=True)

        @block.tensor
        def _(pe):
            mm = nc.tensor.matmul

            def arrived(unit, b, i=0):
                pe.wait_ge(weights_in[b], 16 * (i + unit // 2 + 1))

            def sum_squares(stage):
                pe.wait_ge(sumsq_done, DC * (stage + 1))
                for hf in range(2):
                    last = mm(ps[:, 2 + hf, 0:HALF], ones[:], square_sum[:, hf * HALF:(hf + 1) * HALF], start=True,
                              stop=True)
                last.then_inc(sumall_done, 1)

            def product(bank, w, x, k, n):
                for hf in range(2):
                    last = mm(ps[:, bank + hf, 0:HALF], w, x[:, hf * HALF:(hf + 1) * HALF], start=(k == 0),
                              stop=(k == n - 1))
                return last

            def product16(bank, w_high, w_low, x_high, x_low, k, n):
                for w, x, first, final in ((w_high, x_high, True, False), (w_high, x_low, False, False),
                                           (w_low, x_high, False, True)):
                    for hf in range(2):
                        last = mm(ps[:, bank + hf, 0:HALF], w, x[:, hf * HALF:(hf + 1) * HALF],
                                  start=(first and k == 0), stop=(final and k == n - 1))
                return last

            def ffn(stage, last_stage=False):
                f = FFN_OF_STAGE[stage]
                n0 = f * FFN_UNITS
                with pe.Fori(0, FC // 2) as i:
                    for b in range(2):
                        pe.wait_ge(wlow_done, 2 * i + b + n0 + 2 + 1)
                        pe.wait_ge(hid_done, 2 * i + b + FC * f + 1)
                        w = w16[:, b, :, 0:UP_W].rearrange("p a (g c n) -> p a g c n", g=2, c=DC)
                        for c in range(DC):
                            if b == 0:
                                pe.wait_ge(normed_done, DC * NORMED[stage] + c + 1)
                            for gu in range(2):
                                last = product16(4 * b + 2 * gu, w[:, 0, gu, c, :], w[:, 1, gu, c, :],
                                                 normed16[:, 0, c, :], normed16[:, 1, c, :], c, DC)
                        last.then_inc(unit_done, 1)

                def down(i, b, follow):
                    pe.wait_ge(wlow_done, 2 * i + b + n0 + FC + 2 + 1)
                    pe.wait_ge(resid_done, 2 * i + b + DC * stage + 1)
                    w = w16[:, b, :, 0:DN_W].rearrange("p a (c n) -> p a c n", c=FC)
                    for c in range(FC):
                        if follow:
                            pe.wait_ge(hlow_done, FC * f + c + 1)
                        last = product16(4 * b, w[:, 0, c, :], w[:, 1, c, :], hidden16[:, 0, c, :],
                                         hidden16[:, 1, c, :], c, FC)
                    last.then_inc(unit_done, 1)

                down(0, 0, True)
                down(0, 1, False)
                with pe.Fori(1, DC // 2) as i:
                    for b in range(2):
                        down(i, b, False)
                if not last_stage:
                    sum_squares(stage + 1)

            pe.wait_ge(ones_set, 3)
            mm(ps[:, 7, 0:2], ones[:], ones[:, 0:2], start=True, stop=True).then_inc(unit_done, 2)
            sum_squares(0)
            ffn(0)

            U = UNIT0[1]
            x = normed

            def cols(t):
                return slice(t * P, t * P + ROWS[t])

            pe.wait_ge(normed_done, 2 * DC)
            pe.wait_ge(s["vw_in"], 16)
            for t in range(TILES):
                if t >= 2:
                    pe.wait_ge(s["vw_evac"], t - 1)
                for c in range(DC):
                    last = mm(ps[0:ROWS[t], 4 + t % 2, 0:VW], x[:, c, cols(t)], w_vw[:, c, :], start=(c == 0),
                              stop=(c == DC - 1))
                last.then_inc(s["vw_mm"], 1)

            def in_unit(n):
                arrived(U + n, n % 2)
                if 2 <= n < 8:
                    pe.wait_ge(s["qk_sq" if 5 <= n else "raw_evac"], n - 4 if 5 <= n else n - 1 if n < 5 else 0)
                w = wslot[:, n % 2, 0:DC * P].rearrange("p (c n) -> p c n", c=DC)
                for c in range(DC):
                    last = product(2 * (n % 2), w[:, c, :], x[:, c, :], c, DC)
                last.then_inc(unit_done, 1)

            def exchange(table, src, bank, signal):
                last = product(bank, perms[:, table, :], src, 0, 1)
                last.then_inc(signal, 1)

            pe.wait_ge(consts_in, 16 * 8)
            for n, src in enumerate((kit, qit[:, 0], qit[:, 1])):
                in_unit(n)
                if n:
                    pe.wait_ge(s["raw_evac"], n)
                    if n >= 2:
                        pe.wait_ge(s["rope_done"], n - 1)
                    exchange(0, (kit, qit[:, 0])[n - 1], 6, s["perm_mm"])
            pe.wait_ge(s["ai_in"], 16)
            for t in range(TILES):
                pe.wait_ge(s["vw_evac"], TILES)
                if t >= 2:
                    pe.wait_ge(s["ai_evac"], t - 1)
                for c in range(DC):
                    last = mm(ps[0:ROWS[t], 4 + t % 2, :], x[:, c, cols(t)], w_ai[:, c, :], start=(c == 0),
                              stop=(c == DC - 1))
                last.then_inc(s["ai_mm"], 1)
                if t == 0:
                    pe.wait_ge(s["raw_evac"], 3)
                    pe.wait_ge(s["rope_done"], 2)
                    exchange(0, qit[:, 1], 6, s["perm_mm"])
            pe.wait_ge(s["rope_done"], 3)
            pe.wait_ge(s["ai_evac"], TILES)
            n = 0
            for t in range(TILES):
                for h in range(IDX_HEADS):
                    if n >= 2:
                        pe.wait_ge(s["relu_done"], n - 1)
                    bank = 4 + 2 * (n % 2)
                    rows = slice(IDX_DIM * (h % 2), IDX_DIM * (h % 2) + IDX_DIM)
                    w = min(WIDTH[t], MAIN)
                    q = qit[rows, h // 2, cols(t)]
                    last = mm(ps[0:ROWS[t], bank, 0:w], q, kit[rows, 0:w], start=True, stop=True)
                    if WIDTH[t] > MAIN:
                        last = mm(ps[0:ROWS[t], bank + 1, 0:TAIL], q, kit[rows, TAIL0:NT], start=True, stop=True)
                    if t == 4:
                        q = qit[rows, h // 2, SMP0:TAIL0]
                        mm(ps[0:N_SAMPLE, bank, 0:PAST], q, cache[rows, 1, :], start=True, stop=True)
                        last = mm(ps[0:N_SAMPLE, bank, PAST:PAST + N_SAMPLE], q, kit[rows, SMP0:TAIL0], start=True,
                                  stop=True)
                    last.then_inc(s["isc_mm"], 1)
                    n += 1
            in_unit(3)
            for n in range(4, 8):
                if n == 4:
                    pe.wait_ge(s["raw_evac"], 3)
                in_unit(n)
                pe.wait_ge(s["qk_sq"], n - 3)
                pe.wait_ge(s["relu_done"], 4 * TILES)
                if n == 4:
                    product(6, ones[:], square[:, 0, :], 0, 1).then_inc(s["ksum_mm"], 1)
                else:
                    head_square_sums(mm, ps, square, ones, n - 5, s)
            pe.wait_ge(s["qk_sq"], 5)
            for n in range(8, IN_UNITS):
                if n < 10:
                    pass
                else:
                    pe.wait_ge(s["raw_evac"], n - 5)
                in_unit(n)
                if n == 8:
                    head_square_sums(mm, ps, square, ones, 3, s)
            for n in range(5):
                if n == 0:
                    pe.wait_ge(s["k_normed"], 1)
                    pe.wait_ge(s["raw_evac"], 16)
                if n >= 2:
                    pe.wait_ge(s["rope_done"], 3 + n - 1)
                exchange(1, kt if n == 0 else qt[:, n - 1], 2 * (n % 2), s["kperm_mm"])
            pe.wait_ge(s["rope_done"], 8)
            pe.wait_ge(s["kroot_done"], 1)
            pe.wait_ge(s["qroot_done"], 1)
            for n, (kind, hp, h) in enumerate(LEVEL_PASSES):
                if n >= 2:
                    pe.wait_ge(s["att_evac"], n - 1)
                if kind == "level":
                    pe.wait_ge(s["mult_done"], n + 1 if hp == 0 else n + 2)
                else:
                    pe.wait_ge(s["gate_ka"], 1)
                for t in range(TILES):
                    r = ROWS[t]
                    if t == 4 and kind == "level":
                        if h == 64:
                            continue
                        if h >= 16:
                            r = N_SAMPLE
                    for a in range(2):
                        if kind == "level":
                            left = right = decayed[:, n % 2, a, t * P:t * P + r]
                        else:
                            left, right = ka[:, 2 * hp + a, t * P:t * P + r], qa[:, 2 * hp + a, t * P:t * P + r]
                        at = (t % 2) * 256 + a * P if t < 4 else a * P
                        last = mm(ps[0:r, 3 * (n % 2) + t // 2, at:at + r], left, right, start=True, stop=True)
                last.then_inc(s["level_mm"], 1)
            pe.wait_ge(s["mult_done"], len(DECAYS))
            for t in range(TILES):
                if t >= 2:
                    pe.wait_ge(s["kdt_evac"], t - 1)
                for h in range(HEADS):
                    last = nc.tensor.transpose(ps[0:ROWS[t], 6 + t % 2, h * DH:(h + 1) * DH], ka[:, h, cols(t)],
                                               ident[:])
                last.then_inc(s["kdt_mm"], 1)
            pe.wait_ge(s["att_evac"], 16)
            pe.wait_ge(s["kdt_evac"], TILES)
            pe.wait_ge(s["ai_evac"], TILES)
            for i in range(6):
                t, rows = (i, slice(0, P)) if i < 4 else (4, slice(N_SAMPLE, ROWS[4])) if i == 4 else (4, slice(0, N_SAMPLE))
                for h in range(HEADS):
                    c = slice(h * DH, (h + 1) * DH)
                    last = mm(ps[:, i, c], kd_tok[rows, t, c], va[rows, t, c], start=True, stop=True)
                last.then_inc(s["delta_mm"], 1)
            for t in range(TILES):
                if t >= 2:
                    pe.wait_ge(s["head_evac"], t - 1)
                if t:
                    pe.wait_ge(s["state_done"], t)
                if t == 4:
                    pe.wait_ge(s["state_in"], 16)
                o = ps[:, 6 + t % 2, :].rearrange("p (h n) -> p h n", h=HEADS)
                for h in range(HEADS):
                    c = slice(h * DH, (h + 1) * DH)
                    if t < 4:
                        last = mm(o[:, h, :], va[:, t, c], att[:, t, h, :], start=True, stop=(t == 0))
                        if t:
                            last = mm(o[:, h, :], state(t - 1)[:, c], qa[:, h, cols(t)], start=False, stop=True)
                    else:
                        for rows, st, lo, n in ((slice(0, N_SAMPLE), states_hi[:, 2], SMP0, N_SAMPLE),
                                                (slice(N_SAMPLE, ROWS[4]), state(3), TAIL0, TAIL)):
                            mm(o[:, h, rows], va[rows, 4, c], att[rows, 4, h, rows], start=True, stop=False)
                            last = mm(o[:, h, rows], st[:, c], qa[:, h, lo:lo + n], start=False, stop=True)
                last.then_inc(s["head_mm"], 1)
            for h in range(HEADS):
                pe.wait_ge(s["osq_done"], h + 1)
                if h == 0:
                    pe.wait_ge(s["sample_state"], 1)
                    pe.wait_ge(s["state_done"], 5)
                if h >= 2:
                    pe.wait_ge(s["oroot_done"], h - 1)
                product(2 * (h % 2), ones[:], square[:, h % 2, :], 0, 1).then_inc(s["osum_mm"], 1)
            ev = 0
            for t in range(TILES):
                r = ROWS[t]
                for h in range(HEADS):
                    n = t * HEADS + h
                    if n >= 2:
                        pe.wait_ge(s["masked_done"], n - 1)
                    elif n == 0:
                        pe.wait_ge(s["oroot_done"], HEADS)
                    bank = 2 * (h % 2)
                    q = qt[:, h, cols(t)]
                    w = min(WIDTH[t], MAIN)
                    last = mm(ps[0:r, bank, 0:w], q, kt[:, 0:w], start=True, stop=True)
                    if WIDTH[t] > MAIN:
                        last = mm(ps[0:r, bank + 1, 0:TAIL], q, kt[:, TAIL0:NT], start=True, stop=True)
                    if t == 4:
                        q = qt[:, h, SMP0:TAIL0]
                        mm(ps[0:N_SAMPLE, bank, 0:PAST], q, cache[:, 0, :], start=True, stop=True)
                        last = mm(ps[0:N_SAMPLE, bank, PAST:PAST + N_SAMPLE], q, kt[:, SMP0:TAIL0], start=True,
                                  stop=True)
                    last.then_inc(s["logit_mm"], 1)
                for kw, kc, parts in key_chunks(t):
                    if ev >= 2:
                        pe.wait_ge(s["pt_evac"], ev - 1)
                    for h in range(HEADS):
                        pe.wait_ge(s["p_done"], t * HEADS + h + 1)
                        last = nc.tensor.transpose(ps[0:kw, 4 + ev % 2, h * P:h * P + r], probs[0:r, h, kc:kc + kw],
                                                   ident[0:r, 0:r])
                    last.then_inc(s["pt_mm"], 1)
                    ev += 1
                pe.wait_ge(s["pt_evac"], ev)
                if t == 0:
                    pe.wait_ge(s["head_evac"], TILES)
                if t >= 2:
                    pe.wait_ge(s["pv_evac"], t - 1)
                out = ps[:, 6 + t % 2, :].rearrange("p (h n) -> p h n", h=HEADS)
                chunks = key_chunks(t)
                if t < 4:
                    for c, (kw, kc, parts) in enumerate(chunks):
                        vk = v_tail[0:TAIL] if kc == MAIN else vb[0:kw, c]
                        last = mm(out, vk, probs_t[0:kw, c], start=(c == 0), stop=(c == len(chunks) - 1))
                else:
                    tail = slice(N_SAMPLE, ROWS[4])
                    for c in range(5):
                        kw = P if c < 4 else TAIL
                        last = mm(out[:, :, tail], vb[0:kw, c] if c < 4 else v_tail[0:TAIL], probs_t[0:kw, c, :, tail],
                                  start=(c == 0), stop=(c == 4))
                    smp = slice(0, N_SAMPLE)
                    mm(out[:, :, smp], cache[:, 2, :], probs_t[:, 0, :, smp], start=True, stop=False)
                    last = mm(out[:, :, smp], vb[0:N_SAMPLE, 4], probs_t[0:N_SAMPLE, 1, :, smp], start=False, stop=True)
                last.then_inc(s["pv_mm"], 1)
            pe.wait_ge(s["pv_evac"], TILES)
            pe.wait_ge(s["oa_done"], HEADS)
            pe.wait_ge(s["masked_done"], TILES * HEADS)
            pe.wait_ge(s["pt_evac"], ev)
            with pe.Fori(0, DC // 2) as i:
                for b in range(2):
                    arrived(U + IN_UNITS, b, i)
                    pe.wait_ge(resid_done, 2 * i + b + DC + 1)
                    w = wslot[:, b, 0:DC * P].rearrange("p (c n) -> p c n", c=DC)
                    for c in range(DC):
                        last = product(4 * b, w[:, c, :], normed[:, c, :], c, DC)
                    last.then_inc(unit_done, 1)
            sum_squares(2)
            ffn(2)
            ffn(3)
            pe.wait_ge(s["pool_in"], 48)
            for c in range(DC):
                gi, m = c // 2, c % 2
                pe.wait_ge(s["pwin_done"], gi + 1)
                pe.wait_ge(resid_done, DC * 4 + c + 1)
                for k in range(2):
                    last = product(4 * (c % 2), w_pool[:, gi, k, m, :], pooled[:, 2 * gi + k, :], k, 2)
                last.then_inc(s["pool_mm"], 1)
            sum_squares(5)
            ffn(5, last_stage=True)



NORMED = {0: 0, 1: 1, 2: 2, 3: 3, 5: 4}
LEVEL_PASSES = [x for x in PASSES if x[0] in ("level", "diag")]


def key_chunks(t):
    if t < 4:
        w = WIDTH[t]
        return [(min(P, w - k), k, [(0, P)]) for k in range(0, w, P)]
    return [(P, k, [(0, ROWS[4])]) for k in range(0, MAIN, P)] + [(TAIL, MAIN, [(0, ROWS[4])])]


def head_square_sums(mm, ps, square, ones, h, s):
    for t in range(TILES):
        last = mm(ps[0:ROWS[t], 4, 4 * t + h:4 * t + h + 1], square[:, (h + 1) % 2, t * P:t * P + ROWS[t]],
                  ones[:, 0:1], start=True, stop=True)
    last.then_inc(s["qsum_mm"], 1)


def token_order():
    return np.r_[0:MAIN, TAIL0:NT], np.arange(SMP0, TAIL0)


def rope_tables(dim, heads_in_chunk):
    half = dim // 8
    inv = (np.float32(ROPE_THETA) ** (-np.arange(half, dtype=np.float32) / np.float32(half))).astype(np.float32)
    pos = np.zeros(NT, np.float32)
    prompt, sample = token_order()
    pos[prompt] = np.arange(N_PROMPT)
    pos[sample] = PAST + np.arange(N_SAMPLE)
    ang = (pos[None, :] * inv[:, None]).astype(np.float32).astype(np.float64)
    cos, sin = np.ones((dim, NT)), np.zeros((dim, NT))
    cos[:half] = cos[half:2 * half] = np.cos(ang)
    sin[:half], sin[half:2 * half] = -np.sin(ang), np.sin(ang)
    table = np.stack([np.tile(cos, (heads_in_chunk, 1)), np.tile(sin, (heads_in_chunk, 1))], 1)
    perm = np.arange(P)
    for k in range(heads_in_chunk):
        o = k * dim
        perm[o:o + 2 * half] = o + np.r_[half:2 * half, 0:half]
    return table.astype(np.float32), np.eye(P, dtype=np.float32)[perm]


def shape_constants():
    rope_idx, perm_idx = rope_tables(IDX_DIM, 2)
    rope_head, perm_head = rope_tables(DH, 1)
    i = np.arange(P)
    src, dst = i[:, None], i[None, :]
    masks = [(src // (2 * h) == dst // (2 * h)) & (src % (2 * h) < h) & (dst % (2 * h) >= h) for h in LEVELS]
    masks.append(src == dst)
    bound = np.where(i < 16, 16, np.where(i < 80, 80, 144))
    adm = np.where(np.arange(144)[None, :] < bound[:, None], 0.0, NEG_BIG).astype(np.float32)
    pos = np.arange(16)
    inv_cnt = np.stack([1.0 / np.minimum(w, pos + 1) for w in POOL_WINDOWS]).astype(np.float32)
    return {
        "ident": np.eye(P, dtype=np.float32), "masks": np.stack(masks, 1).astype(np.float32), "adm": adm,
        "rope_idx": rope_idx, "rope_head": rope_head, "perms": np.stack([perm_idx, perm_head], 1),
        "inv_cnt": np.ascontiguousarray(np.broadcast_to(inv_cnt, (P, 4, 16))),
    }


def chunked(a):
    return a.reshape(-1, P, *a.shape[1:]).swapaxes(0, 1)


def units(w):
    k, n = w.shape
    return w.reshape(k // P, P, n // P, P).transpose(2, 1, 0, 3).reshape(n // P, P, k)


_OUTS = {"y": (P, DC, NT), "k": (P, NT), "v": (P, TILES, DH), "ki": (IDX_DIM, NT), "hgrn_p": (P, HEADS * DH),
         "hgrn_s": (P, HEADS * DH), "pool_p": (P, DC, POOL_HIST), "pool_s": (P, DC, POOL_HIST)}


def kernel(**inputs):
    import concourse.bacc as _bacc
    from concourse.bass_utils import run_bass_kernel_spmd as _run

    i = {k: np.asarray(v) for k, v in inputs.items()}
    prompt, sample = token_order()
    x = np.empty((NT, D_MODEL), np.float32)
    x[prompt] = np.concatenate([i["meta_tokens"], i["x_prompt"][0]])
    x[sample] = i["x_sample"][0]
    w_in = i["ab_w_in"][0]
    c = np.cumsum((0, 512, 512, 512, 512, 512, 128, 128, 256, 64, 4))
    aq, af, ai, ag, bq, bk, bv, bqi, bki, bw = (w_in[:, c[n]:c[n + 1]] for n in range(10))
    gains = np.stack([i["norm_ffn1"][0], i["norm_mix"][0], i["norm_ffn2"][0],
                      i["norm_ffn1"][1], i["norm_mix"][1], i["norm_ffn2"][1]])
    cki = i["cache_ki"][0, 0].T
    arrays = {
        "x": chunked(x.T), "gains": gains.reshape(6, DC, P).transpose(2, 0, 1),
        "w_up": np.stack([np.stack([units(i[n + "_wg"][l]), units(i[n + "_wu"][l])], 2).reshape(FC, P, 2 * DC * P)
                          for l in range(2) for n in ("ffn1", "ffn2")]),
        "w_dn": np.stack([units(i[n + "_wd"][l]) for l in range(2) for n in ("ffn1", "ffn2")]),
        "w_in": units(np.concatenate([bki, bki, bqi, bk, bq, af, aq, ag], 1)),
        "w_vw": chunked(np.concatenate([bv, bw], 1)), "w_ai": chunked(ai), "w_out": units(i["ab_w_out"][0]),
        "lb_logits": i["hgrn_lb_logits"].reshape(HEADS, P).T,
        "cgain": np.concatenate([i["attn_q_norm"], i["attn_k_norm"], i["attn_q_norm"], i["attn_k_norm"],
                                 i["hgrn_out_norm"].reshape(HEADS, P)]).T,
        "pool_scale": i["pool_scale"].reshape(DC, P).T,
        "cache": np.stack([i["cache_k"][0, 0].T, np.concatenate([cki, cki]), i["cache_v"][0, 0]], 1),
        "state": i["state_hgrn"][0, 0].transpose(1, 0, 2).reshape(P, HEADS * DH),
        "state_pool": chunked(i["state_pool"][0, 0].T),
        "w_pool": i["pool_w"][0].reshape(4, 2, P, 2, P).transpose(2, 0, 1, 3, 4).reshape(P, 4, 2, 2, P),
        **shape_constants(),
    }
    arrays = {k: np.ascontiguousarray(v) for k, v in arrays.items()}
    nc = _bacc.Bacc("TRN2", target_bir_lowering=False, num_devices=1)
    d = {k: nc.dram_tensor("in_" + k, v.shape, mybir.dt.from_np(v.dtype), kind="ExternalInput").ap()
         for k, v in arrays.items()}
    d |= {k: nc.dram_tensor("out_" + k, v, F32, kind="ExternalOutput").ap() for k, v in _OUTS.items()}
    build(nc, d)
    r = _run(nc, [{"in_" + k: v for k, v in arrays.items()}], core_ids=[0]).results[0]
    o = {k: r["out_" + k] for k in _OUTS}

    def tokens(a):
        a = a.transpose(2, 1, 0).reshape(NT, -1)
        return a[prompt], a[sample]

    y_p, y_s = tokens(o["y"])
    k_p, k_s = tokens(o["k"][:, None])
    ki_p, ki_s = tokens(o["ki"][:, None])
    v_rows = o["v"].transpose(1, 0, 2)
    v_all = np.concatenate([v_rows[:4].reshape(MAIN, DH), v_rows[4, :ROWS[4]]])
    v_p, v_s = v_all[prompt], v_all[sample]

    def states(a):
        return a.reshape(P, HEADS, DH).transpose(1, 0, 2)[None, None]

    def hist(a):
        return a.transpose(2, 1, 0).reshape(POOL_HIST, D_MODEL)[None, None]

    out = (y_p[N_META:][None], y_s[None], k_p[None, None], v_p[None, None], ki_p[None, None], states(o["hgrn_p"]),
           hist(o["pool_p"]), k_s[None, None], v_s[None, None], ki_s[None, None], states(o["hgrn_s"]),
           hist(o["pool_s"]))
    return tuple(np.ascontiguousarray(a) for a in out)
```

```python
from contextlib import ExitStack

import numpy as np

import concourse.bass as bass
from concourse import mybir

F32 = mybir.dt.float32
F16 = mybir.dt.float16
U32 = mybir.dt.uint32
AXIS_X = mybir.AxisListType.X
ALL_MAX = bass.bass_isa.ReduceOp.max
ACT = mybir.ActivationFunctionType
ALU = mybir.AluOpType

P = 128
D_MODEL, D_FF = 1024, 2816
SEQ, N_META, N_SAMPLE, PAST = 512, 16, 64, 128
N_PROMPT = SEQ + N_META
MAIN = 512
TAIL = N_PROMPT - MAIN
NT = N_PROMPT + N_SAMPLE
HALF = NT // 2
SMP0, TAIL0 = MAIN, MAIN + N_SAMPLE
DC = D_MODEL // P
FC = D_FF // P
HEADS, DH = 4, 128
IDX_HEADS, IDX_DIM = 4, 64
TOPK, TOPK_SAMPLE = SEQ // 4, (PAST + N_SAMPLE) // 4
CHUNK = 64
RMS_EPS = 1e-6
NEG_BIG = -1e30
TAKEN = -3e38
PAD_TOP = 3e38
ROPE_THETA = 500000.0
POOL_WINDOWS = (2, 4, 8, 16)
POOL_HIST = 15
FFN_UNITS = FC + DC
IN_UNITS = 20
OUT_UNITS = DC
UP_W, DN_W = 2 * DC * P, FC * P
WSLOT = DN_W
EARLY = 10
EXPONENT = 0x7F800000
TINY = 2.0 ** -100
VW = DH + IDX_HEADS
TILES = 5
ROWS = [P, P, P, P, N_SAMPLE + TAIL]
WIDTH = [144, 272, 400, 528, 528]
LEVELS = [64, 32, 16, 8, 4, 2, 1]
PASSES = [(kind, hp, h) for hp in range(2) for kind, h in [("level", h) for h in LEVELS] + [("diag", 0)]] + \
         [(kind, hp, 0) for kind in ("k", "q") for hp in range(2)]
DECAYS = [x for x in PASSES if x[0] != "diag"]
SEGMENTS = [(i * P, P) for i in range(4)] + [(SMP0, N_SAMPLE), (TAIL0, TAIL)]
FFN_OF_STAGE = {0: 0, 2: 1, 3: 2, 5: 3}
UNIT0 = {0: 0, 1: FFN_UNITS, 2: FFN_UNITS + IN_UNITS + OUT_UNITS}
UNIT0[3] = UNIT0[2] + FFN_UNITS
UNIT0[5] = UNIT0[3] + FFN_UNITS


def build(nc, d):
    with ExitStack() as ctx:
        def sb(name, shape, dt=F32):
            return ctx.enter_context(nc.sbuf_tensor(name, shape, dt))

        def sem(name):
            return ctx.enter_context(nc.semaphore(name))

        resid = sb("resid", [P, DC, NT])
        normed = sb("normed", [P, DC, NT])
        normed16 = normed[:, :, :].rearrange("p c n -> p (c n)").bitcast(F16) \
            .rearrange("p (a c n) -> p a c n", a=2, c=DC)
        wslot = sb("wslot", [P, 2, WSLOT])
        scales = sb("scales", [P, 160])
        gmax, gall, gexp, inv_x = (scales[:, 6 * i:6 * i + 6] for i in range(4))
        gains16 = scales[:, 24:72].rearrange("p (s c) -> p s c", s=6)
        wmax, wall, wexp, wdown, wscale, wback = (scales[:, 72 + 2 * i:74 + 2 * i] for i in range(6))
        hmax = scales[:, 84:84 + FC]
        gscale = scales[:, 106:112]
        hmax1 = scales[:, 112:113]
        hall, hexp, hdown, hscale, inv_h = (scales[:, 113 + 2 * i:115 + 2 * i] for i in range(5))
        wback_last = scales[:, 123:125]
        square = sb("square", [P, 2, NT])
        LOAD0 = {i: u - (OUT_UNITS if i >= 2 else 0) for i, u in UNIT0.items()}
        square_sum = sb("square_sum", [P, TILES * P])
        norm_work = sb("norm_work", [P, 2 * NT])
        root, rnorm = norm_work[:, 0:NT], norm_work[:, NT:2 * NT]
        o_diag = (norm_work[:, 0:TILES * P], square[:, :, :].rearrange("p b n -> p (b n)")[:, 0:TILES * P])
        diag = norm_work[:, 0:TILES * P].rearrange("p (t n) -> p t n", t=TILES)
        act_out = sb("act_out", [P, 2, NT])
        ones = sb("ones", [P, P])
        ident = sb("ident", [P, P])
        eps = sb("eps", [P, 1])
        gains = sb("gains", [P, 6, DC])
        ARENA = 31900
        arena = sb("arena", [P, ARENA])
        HN = FC * NT
        hidden16 = arena[:, 0:HN].bitcast(F16).rearrange("p (a f n) -> p a f n", a=2, f=FC)
        hidden = arena[:, HN:2 * HN].rearrange("p (f n) -> p f n", f=FC)
        w16 = arena[:, 2 * HN:2 * HN + 2 * WSLOT].bitcast(F16).rearrange("p (b a n) -> p b a n", b=2, a=2)
        top = [0]

        def take(n):
            top[0] += n
            assert top[0] <= ARENA, top[0]
            return arena[:, top[0] - n:top[0]]

        def heads4(ap):
            return ap.rearrange("p (h n) -> p h n", h=HEADS)

        zf = heads4(take(HEADS * NT))
        qa = heads4(take(HEADS * NT))
        ag = heads4(take(HEADS * NT))
        ka = heads4(take(HEADS * NT))
        w_out = arena[:, 0:OUT_UNITS * DC * P].rearrange("p (u n) -> p u n", u=OUT_UNITS)
        va = take(TILES * MAIN).rearrange("p (t n) -> p t n", t=TILES)
        kt = take(NT)
        assert top[0] <= FC * NT
        top[0] = FC * NT
        eg = take(8 * NT)
        decay = eg[:, 0:4 * NT].rearrange("p (b h n) -> p b h n", b=2, h=2)
        decayed = eg[:, 4 * NT:8 * NT].rearrange("p (b h n) -> p b h n", b=2, h=2)
        gate_a = heads4(eg[:, 0:4 * NT])
        gate_b = heads4(eg[:, 4 * NT:8 * NT])
        w_ai = eg[:, 0:DC * MAIN].rearrange("p (c n) -> p c n", c=DC)
        kd_tok = eg[:, 0:TILES * MAIN].rearrange("p (t n) -> p t n", t=TILES)
        past_w_out = OUT_UNITS * DC * P
        probs = [x.rearrange("p (h n) -> p h n", h=HEADS)
                 for x in (eg[:, 0:HEADS * 528], arena[:, past_w_out:past_w_out + HEADS * 528])]
        probs_t = eg[:, HEADS * 528:HEADS * 528 + 5 * MAIN].rearrange("p (c h n) -> p c h n", c=5, h=HEADS)
        qt = heads4(take(HEADS * NT))
        small = take(3 * NT)
        kit = small[:, 0:NT]
        qit = small[:, NT:3 * NT].rearrange("p (c n) -> p c n", c=2)
        states_lo = small[:, 0:3 * MAIN].rearrange("p (s n) -> p s n", s=3)
        states_hi = take(4 * MAIN).rearrange("p (s n) -> p s n", s=4)
        att = take(TILES * MAIN).rearrange("p (t h n) -> p t h n", t=TILES, h=HEADS)
        relu_sc = att.rearrange("p t h n -> p (t h n)")[:, 0:2 * 528].rearrange("p (b n) -> p b n", b=2)
        score = take(TILES * 528).rearrange("p (t n) -> p t n", t=TILES)
        w_vw = score.rearrange("p t n -> p (t n)")[:, 0:DC * VW].rearrange("p (c n) -> p c n", c=DC)
        ropes = take(2 * NT).rearrange("p (b n) -> p b n", b=2)
        adm = take(144)
        vb = take(TILES * DH).rearrange("p (t n) -> p t n", t=TILES)
        v_tail = take(DH)
        cache = take(3 * P).rearrange("p (c n) -> p c n", c=3)
        perms = take(2 * P).rearrange("p (c n) -> p c n", c=2)
        mask_bits = sb("mask_bits", [P, 8, P])
        masks = mask_bits[:].bitcast(mybir.dt.uint32)
        smalls = sb("smalls", [P, 256])
        wi = smalls[:, 0:20].rearrange("p (t h) -> p t h", t=TILES)
        rq = smalls[:, 20:40].rearrange("p (t h) -> p t h", t=TILES)
        lb_in, lb, lb_free, lb_ln, lb_on, lb_shift, lb_e = (smalls[:, 40 + 4 * i:44 + 4 * i] for i in range(7))
        cgain = smalls[:, 68:76]
        e_last = smalls[:, 76:100].rearrange("p (h s) -> p h s", h=HEADS)
        max8 = smalls[:, 100:108]
        mx, nbias, psumv, pinv = ([smalls[:, i:i + 4], smalls[:, j:j + 4]]
                                  for i, j in ((108, 202), (112, 206), (116, 210), (120, 214)))
        rqs = smalls[:, 124:144].rearrange("p (t h) -> p t h", t=TILES)
        pscale = smalls[:, 144:152]
        o_root, o_rnorm = smalls[:, 162:182], smalls[:, 182:202]
        root_tok, rnorm_tok = smalls[:, 152:157], smalls[:, 157:162]
        top[0] = 0
        UE = 2 * POOL_HIST + NT
        PP0, PS0 = POOL_HIST, 2 * POOL_HIST + N_PROMPT
        ue = take(DC * UE).rearrange("p (c n) -> p c n", c=DC)
        sums = take(DC * UE).rearrange("p (c n) -> p c n", c=DC)
        sums2 = take(DC * UE).rearrange("p (c n) -> p c n", c=DC)
        pooled = take(DC * NT).rearrange("p (c n) -> p c n", c=DC)
        POOL_SHARE = (1, 2)
        w_pool = take(2048).rearrange("p (g k m n) -> p g k m n", g=4, k=2, m=2)
        inv_cnt = take(64).rearrange("p (g n) -> p g n", g=4)

        ps = ctx.enter_context(nc.psum_tensor("ps", [P, 8, 512], F32))
        psf = ps[:, :, :].rearrange("p b n -> p (b n)")
        rnorm_all = psf[:, 6 * 512:6 * 512 + NT]

        def state(i):
            return states_lo[:, i] if i < 3 else states_hi[:, i - 3]

        consts_in, ident_in = sem("consts_in"), sem("ident_in")
        resid_in = [sem("resid_in%d" % i) for i in range(4)]
        gains_in = sem("gains_in")
        weights_in = [sem("weights_in0"), sem("weights_in1")]
        unit_done = sem("unit_done")
        gmax_done, gall_done, gscale_done = sem("gmax_done"), sem("gall_done"), sem("gscale_done")
        wmax_done = sem("wmax_done")
        wall_done = sem("wall_done")
        wexp_done, wdown_done = sem("wexp_done"), sem("wdown_done")
        wscale_done = sem("wscale_done")
        wback_done = sem("wback_done")
        whigh_done = sem("whigh_done")
        wlow_done = sem("wlow_done")
        hpart_done, hmax_done, hall_done, hscale_done = sem("hpart_done"), sem("hmax_done"), sem("hall_done"), sem("hscale_done")
        rpart_done = sem("rpart_done")
        part_mm = sem("part_mm")
        hhigh_done, hlow_done = sem("hhigh_done"), sem("hlow_done")
        scaled_done, nhigh_done = sem("scaled_done"), sem("nhigh_done")
        ones_set = sem("ones_set")
        hid_done = sem("hid_done")
        silu_done = sem("silu_done")
        resid_done = sem("resid_done")
        square_done = sem("square_done")
        sumsq_zero = sem("sumsq_zero")
        sumsq_done = sem("sumsq_done")
        sumall_done = sem("sumall_done")
        root_done = sem("root_done")
        rnorm_done = sem("rnorm_done")
        diag_done, spread_done = sem("diag_done"), sem("spread_done")
        normed_done = sem("normed_done")
        dve_step = sem("dve_step")
        act_step = sem("act_step")
        pool_step = sem("pool_step")
        names = """vw_in ai_in rope_in state_in vw_mm vw_evac ai_mm ai_evac raw_evac perm_mm rope_done
            isc_mm relu_done isc_acc qk_sq qsum_mm ksum_mm kroot_done k_normed qroot_done 
            gate_l1 gate_min gate_ka gate_ln gate_logf scan_done lb_done
            diff_done dexp_done mult_done level_mm att_zero att_evac elast_done kdt_mm kdt_evac delta_mm
            state_done sample_state head_mm head_evac osq_done osum_mm o_root_set odiag_done ospread_mm oroot_done oa_done
            logit_mm masked_done exp_done p_done pt_mm pt_evac pv_mm pv_evac
            pool_in hist_zero ue_done psum_done pwin_done pool_mm out_sem y_out w_out_in kperm_mm""".split()
        s = {n: sem(n) for n in names}

        block = ctx.enter_context(nc.Block())

        @block.sync
        def _(sync):
            sync.dma_start(gains[:], d["gains"]).then_inc(gains_in, 16)
            for i in range(4):
                sync.dma_start(resid[:, 2 * i:2 * i + 2], d["x"][:, 2 * i:2 * i + 2]).then_inc(resid_in[i], 16)

            def load(src, u, b, width):
                sync.dma_start(wslot[:, b, 0:width], src[bass.ds(u, 1)].rearrange("u p n -> (u p) n")) \
                    .then_inc(weights_in[b], 16)

            def load_units(src, unit0, n, width, first=0):
                with sync.Fori(first // 2, n // 2) as i:
                    for b in range(2):
                        sync.wait_ge(unit_done, 2 * i + unit0 + b + 1)
                        load(src, 2 * i + b, b, width)

            def load_split(src, ffn_unit0, n, width, first=0):
                with sync.Fori(first // 2, n // 2) as i:
                    for b in range(2):
                        sync.wait_ge(wlow_done, 2 * i + ffn_unit0 + b + 1)
                        load(src, 2 * i + b, b, width)

            def load_ffn(f, first=0):
                load_split(d["w_up"][f], f * FFN_UNITS, FC, 2 * DC * P, first)
                load_split(d["w_dn"][f], f * FFN_UNITS + FC, DC, FC * P)

            load_ffn(0)
            for b in range(2):
                sync.wait_ge(wlow_done, FFN_UNITS + b + 1)
                load(d["w_in"], b, b, DC * P)
            load_units(d["w_in"], UNIT0[1], IN_UNITS, DC * P, first=2)
            for b in range(2):
                sync.wait_ge(unit_done, UNIT0[1] + IN_UNITS + b + 1)
                load(d["w_up"][1], b, b, 2 * DC * P)
            sync.wait_ge(s["oa_done"], HEADS)
            sync.dma_start(w_out, d["w_out"]).then_inc(s["w_out_in"], 16)
            load_ffn(1, first=2)
            load_ffn(2)
            load_ffn(3)
            with sync.Fori(0, DC) as i:
                sync.wait_ge(resid_done, i + 2 + 5 * DC + 1)
                sync.dma_start(d["y"][:, bass.ds(i, 1), :], resid[:, bass.ds(i, 1), :]).then_inc(s["y_out"], 16)
            sync.wait_ge(s["y_out"], 16 * DC)

        @block.gpsimd
        def _(pool):
            g = nc.gpsimd

            def link(ins):
                nonlocal_step[0] += 1
                ins.then_inc(pool_step, 1)
                pool.wait_ge(pool_step, nonlocal_step[0])

            nonlocal_step = [0]
            pool.dma_start(ident[:], d["ident"]).then_inc(ident_in, 16)
            pool.dma_start(mask_bits[:], d["masks"]).then_inc(consts_in, 16)
            pool.dma_start(smalls[:, 40:44], d["lb_logits"]).then_inc(consts_in, 16)
            pool.dma_start(cgain, d["cgain"]).then_inc(consts_in, 16)
            pool.dma_start(pscale, d["pool_scale"]).then_inc(consts_in, 16)

            def all_max(n, done):
                b = done
                pool.wait_ge(wmax_done, n + 1)
                g.partition_all_reduce(wall[:, b:b + 1], wmax[:, b:b + 1], P, ALL_MAX).then_inc(wall_done, 1)

            def unit_low(n, b):
                pool.wait_ge(whigh_done, n + 1)
                g.tensor_tensor(w16[:, b, 1, 0:DN_W], wslot[:, b, 0:DN_W], w16[:, b, 0, 0:DN_W], ALU.subtract)                     .then_inc(wlow_done, 1)

            def ffn(f, ahead):
                n0 = f * FFN_UNITS
                for u in range(2, FC + 2):
                    all_max(n0 + u, u % 2)
                pool.wait_ge(hmax_done, f + 1)
                g.partition_all_reduce(hall[:, 0:1], hmax1, P, ALL_MAX).then_inc(hall_done, 1)
                unit_low(n0 + FC, 0)
                pool.wait_ge(hpart_done, FC * (f + 1))
                g.partition_all_reduce(hall[:, 1:2], hmax[:, FC - 1:FC], P, ALL_MAX).then_inc(hall_done, 1)
                unit_low(n0 + FC + 1, 1)
                for u in range(FC + 2, FFN_UNITS + 2 * ahead):
                    all_max(n0 + u, u % 2)

            def first_two(f):
                for b in range(2):
                    all_max(f * FFN_UNITS + b, b)

            pool.wait_ge(gmax_done, 1)
            g.partition_all_reduce(gall, gmax, P, ALL_MAX).then_inc(gall_done, 1)
            first_two(0)
            ffn(0, 0)
            pool.wait_ge(unit_done, FFN_UNITS + 2)
            pool.dma_start(adm, d["adm"]).then_inc(consts_in, 16)
            pool.dma_start(cache, d["cache"]).then_inc(consts_in, 16)
            pool.dma_start(perms, d["perms"]).then_inc(consts_in, 16)
            pool.dma_start(ropes, d["rope_idx"]).then_inc(s["rope_in"], 16)
            pool.dma_start(w_vw, d["w_vw"]).then_inc(s["vw_in"], 16)
            pool.dma_start(w_ai, d["w_ai"]).then_inc(s["ai_in"], 16)
            pool.wait_ge(s["vw_evac"], TILES)
            pool.dma_start(d["v"][:, 0:4], vb[:, 0:4]).then_inc(s["out_sem"], 16)
            pool.dma_start(d["v"][0:ROWS[4], 4], vb[0:ROWS[4], 4]).then_inc(s["out_sem"], 16)
            pool.wait_ge(s["rope_done"], 3)
            pool.dma_start(ropes, d["rope_head"]).then_inc(s["rope_in"], 16)
            pool.dma_start(d["ki"], kit[0:IDX_DIM]).then_inc(s["out_sem"], 16)
            pool.wait_ge(s["gate_l1"], 1)
            link(g.tensor_scalar(gate_b, zf, 0.0, None, ALU.min))
            g.tensor_tensor(gate_b, gate_b, gate_a, ALU.subtract).then_inc(s["gate_min"], 1)
            pool.wait_ge(s["gate_min"], 1)
            g.tensor_tensor(ka, gate_b, zf, ALU.subtract).then_inc(s["gate_min"], 1)
            pool.wait_ge(s["gate_ln"], 1)
            link(g.tensor_tensor(gate_a, gate_a, gate_b, ALU.subtract))
            pool.wait_ge(s["lb_done"], 1)
            for h in range(HEADS):
                last = g.tensor_scalar(gate_a[:, h], gate_a[:, h], lb_on[:, h:h + 1], None, ALU.mult)
            link(last)
            pool.wait_ge(s["gate_min"], 2)
            g.tensor_tensor(zf, gate_a, gate_b, ALU.add).then_inc(s["gate_logf"], 1)
            pool.wait_ge(s["isc_acc"], 4 * TILES)
            g.memset(att, 0.0).then_inc(s["att_zero"], 1)
            pool.dma_start(states_hi[:, 2], d["state"]).then_inc(s["state_in"], 16)
            pool.wait_ge(s["scan_done"], 1)
            for n, (kind, hp, h) in enumerate(DECAYS):
                if n >= 2:
                    pool.wait_ge(s["mult_done"], n - 1)
                e = decay[:, n % 2]
                b = zf[:, 2 * hp:2 * hp + 2]
                if kind == "level":
                    cols = MAIN if h == 64 else TAIL0 if h >= 16 else NT
                    ev = e[:, :, 0:cols].rearrange("p a (n x) -> p a n x", x=2 * h)
                    bv = b[:, :, 0:cols].rearrange("p a (n x) -> p a n x", x=2 * h)
                    ref = bv[:, :, :, h - 1:h].to_broadcast([P, 2, cols // (2 * h), h])
                    g.tensor_tensor(ev[:, :, :, 0:h], ref, bv[:, :, :, 0:h], ALU.subtract)
                    g.tensor_tensor(ev[:, :, :, h:2 * h], bv[:, :, :, h:2 * h], ref, ALU.subtract) \
                        .then_inc(s["diff_done"], 1)
                elif kind == "k":
                    for lo, w in ((0, P), (SMP0, N_SAMPLE), (TAIL0, TAIL)):
                        cols = MAIN if lo == 0 else w
                        ev = e[:, :, lo:lo + cols].rearrange("p a (n x) -> p a n x", x=w)
                        bv = b[:, :, lo:lo + cols].rearrange("p a (n x) -> p a n x", x=w)
                        last = g.tensor_tensor(ev, bv[:, :, :, w - 1:w].to_broadcast([P, 2, cols // w, w]), bv,
                                               ALU.subtract)
                    last.then_inc(s["diff_done"], 1)
            pool.wait_ge(s["rope_done"], 4)
            pool.dma_start(d["k"], kt).then_inc(s["out_sem"], 16)
            pool.wait_ge(s["state_done"], 5)
            pool.dma_start(d["hgrn_p"], states_hi[:, 1]).then_inc(s["out_sem"], 16)
            pool.wait_ge(s["sample_state"], 1)
            pool.dma_start(d["hgrn_s"], states_hi[:, 3]).then_inc(s["out_sem"], 16)
            first_two(1)
            ffn(1, 1)
            ffn(2, 1)
            pool.wait_ge(unit_done, UNIT0[3] + FFN_UNITS + 2)
            pool.dma_start(w_pool, d["w_pool"]).then_inc(s["pool_in"], 16)
            pool.dma_start(inv_cnt, d["inv_cnt"]).then_inc(s["pool_in"], 16)
            pool.dma_start(ue[:, :, N_PROMPT + POOL_HIST:PS0], d["state_pool"]).then_inc(s["pool_in"], 16)
            g.memset(ue[:, :, 0:POOL_HIST], 0.0).then_inc(s["hist_zero"], 1)
            pool.wait_ge(s["ue_done"], 3 * DC)
            pool.wait_ge(s["pool_in"], 48)
            pool.wait_ge(s["hist_zero"], 1)
            for gi in POOL_SHARE:
                cs, step, k = slice(2 * gi, 2 * gi + 2), 1, 0
                src = ue[:, cs]
                while step < POOL_WINDOWS[gi]:
                    dst = (sums, sums2)[k % 2][:, cs]
                    lo = 2 * step - 1
                    ins = g.tensor_tensor(dst[:, :, lo:UE], src[:, :, lo:UE], src[:, :, lo - step:UE - step], ALU.add)
                    src, step, k = dst, 2 * step, k + 1
                    if step < POOL_WINDOWS[gi]:
                        link(ins)
                    else:
                        ins.then_inc(s["psum_done"], 1)
            pool.dma_start(d["pool_p"], ue[:, :, N_PROMPT:N_PROMPT + POOL_HIST]).then_inc(s["out_sem"], 16)
            pool.dma_start(d["pool_s"], ue[:, :, UE - POOL_HIST:UE]).then_inc(s["out_sem"], 16)
            ffn(3, 0)
            pool.wait_ge(s["out_sem"], 16 * 8)

        @block.scalar
        def _(act):
            a = nc.scalar
            steps = [0]

            def link(ins):
                steps[0] += 1
                ins.then_inc(act_step, 1)
                act.wait_ge(act_step, steps[0])

            def halves(bank):
                return ps[:, bank:bank + 2, 0:HALF]

            def split(ap):
                return ap.rearrange("p (b n) -> p b n", b=2)

            def root_of(stage):
                act.wait_ge(sumall_done, stage + 1)
                a.activation(root_tok, ps[:, 2, 0:TILES], ACT.Sqrt, bias=eps[:, 0:1], scale=1.0 / D_MODEL) \
                    .then_inc(root_done, 1)

            def square_chunk(stage, c, b):
                act.wait_ge(resid_done, c + 2 + DC * stage + 1)
                act.wait_ge(sumsq_done, c + DC * (stage + 1) - 1)
                a.activation(square[:, b, :], resid[:, bass.ds(c, 1), :].rearrange("p a n -> p (a n)"),
                             ACT.Square).then_inc(square_done, 1)

            def squares(stage):
                with act.Fori(0, DC // 2) as i:
                    for b in range(2):
                        square_chunk(stage, 2 * i + b, b)
                root_of(stage + 1)

            def weight_high(stage, u, b, width, after_units=True, in_place=False):
                act.wait_ge(wscale_done, u + FFN_OF_STAGE[stage] * FFN_UNITS + 1)
                if after_units:
                    act.wait_ge(unit_done, u + UNIT0[stage] + 1)
                if in_place:
                    link(a.activation(wslot[:, b, 0:width], wslot[:, b, 0:width], ACT.Copy, scale=wscale[:, b:b + 1]))
                a.activation(w16[:, b, 0, 0:width], wslot[:, b, 0:width], ACT.Copy,
                             scale=1.0 if in_place else wscale[:, b:b + 1]).then_inc(whigh_done, 1)

            def silu(stage, u, b):
                f = FFN_OF_STAGE[stage]
                act.wait_ge(unit_done, u + UNIT0[stage] + 2 + 1)
                act.wait_ge(hid_done, u + FC * f + 1)
                act.wait_ge(wback_done, u + f * FFN_UNITS + 1)
                a.activation(split(act_out[:, b, :]), halves(4 * b), ACT.Silu, scale=wback[:, b:b + 1]) \
                    .then_inc(silu_done, 1)

            def normed_high(stage, f):
                for c in range(DC):
                    act.wait_ge(scaled_done, DC * f + c + 1)
                    a.activation(normed16[:, 0, c, :], square[:, c % 2, :], ACT.Copy).then_inc(nhigh_done, 1)
                    if c == 2:
                        weight_high(stage, 1, 1, UP_W)

            def ffn(stage, next_stage=None, last=False):
                f = FFN_OF_STAGE[stage]
                normed_high(stage, f)
                with act.Fori(0, FC // 2 - 1) as i:
                    for b in range(2):
                        silu(stage, 2 * i + b, b)
                        weight_high(stage, 2 * i + b + 2, b, UP_W)
                silu(stage, FC - 2, 0)
                weight_high(stage, FC, 0, DN_W, in_place=True)

                def hidden_high(i, part):
                    a.activation(hidden16[:, 0, bass.ds(i, 1), :].rearrange("p a n -> p (a n)"),
                                 hidden[:, bass.ds(i, 1), :].rearrange("p a n -> p (a n)"), ACT.Copy,
                                 scale=hscale[:, part:part + 1]).then_inc(hhigh_done, 1)

                act.wait_ge(hscale_done, 2 * f + 1)
                with act.Fori(0, EARLY) as i:
                    hidden_high(i, 0)
                silu(stage, FC - 1, 1)
                weight_high(stage, FC + 1, 1, DN_W, in_place=True)
                with act.Fori(EARLY, FC - 1) as i:
                    hidden_high(i, 0)
                act.wait_ge(hscale_done, 2 * f + 2)
                hidden_high(FC - 1, 1)
                with act.Fori(0, DC // 2 - 1) as i:
                    for b in range(2):
                        weight_high(stage, 2 * i + b + FC + 2, b, DN_W)
                        if not last:
                            square_chunk(stage, 2 * i + b, b)
                if next_stage:
                    weight_high(next_stage, 0, 0, UP_W)
                if not last:
                    for c in range(DC - 2, DC):
                        square_chunk(stage, c, c % 2)
                    root_of(stage + 1)

            act.wait_ge(ones_set, 3)
            for c in range(DC):
                act.wait_ge(resid_in[c // 2], 16)
                if c >= 2:
                    act.wait_ge(sumsq_done, c - 1)
                a.activation(square[:, c % 2, :], resid[:, c, :], ACT.Square).then_inc(square_done, 1)
            root_of(0)
            weight_high(0, 0, 0, UP_W)
            ffn(0)

            U = UNIT0[1] + 2
            for t in range(TILES):
                act.wait_ge(s["vw_mm"], t + 1)
                r = ROWS[t]
                a.activation(vb[0:r, t], ps[0:r, 4 + t % 2, 0:DH], ACT.Copy)
                if t == 4:
                    a.activation(v_tail[0:TAIL], ps[N_SAMPLE:r, 4, 0:DH], ACT.Copy)
                a.activation(wi[0:r, t], ps[0:r, 4 + t % 2, DH:VW], ACT.Copy, scale=IDX_HEADS ** -0.5) \
                    .then_inc(s["vw_evac"], 1)
            for n, dst in enumerate((kit, qit[:, 0], qit[:, 1])):
                act.wait_ge(unit_done, U + n + 1)
                a.activation(split(dst), halves(2 * (n % 2)), ACT.Copy).then_inc(s["raw_evac"], 1)
            for t in range(TILES):
                act.wait_ge(s["ai_mm"], t + 1)
                a.activation(va[0:ROWS[t], t], ps[0:ROWS[t], 4 + t % 2, :], ACT.Copy).then_inc(s["ai_evac"], 1)
            n = 0
            for t in range(TILES):
                for h in range(IDX_HEADS):
                    act.wait_ge(s["isc_mm"], n + 1)
                    if n >= 2:
                        act.wait_ge(s["isc_acc"], n - 1)
                    bank = 4 + 2 * (n % 2)
                    a.activation(relu_sc[0:ROWS[t], n % 2, 0:WIDTH[t]],
                                 psf[0:ROWS[t], bank * 512:bank * 512 + WIDTH[t]], ACT.Relu,
                                 scale=IDX_DIM ** -0.5).then_inc(s["relu_done"], 1)
                    n += 1
            act.wait_ge(unit_done, U + 3 + 1)
            a.activation(split(kt), halves(2), ACT.Copy).then_inc(s["raw_evac"], 1)
            a.activation(split(square[:, 0, :]), halves(2), ACT.Square).then_inc(s["qk_sq"], 1)
            for h in range(HEADS):
                b = 2 * ((4 + h) % 2)
                act.wait_ge(unit_done, U + 4 + h + 1)
                a.activation(split(qt[:, h]), halves(b), ACT.Copy, scale=cgain[:, 0:1])
                if h >= 1:
                    act.wait_ge(s["ksum_mm" if h == 1 else "qsum_mm"], 1 if h == 1 else h - 1)
                a.activation(split(square[:, (h + 1) % 2, :]), halves(b), ACT.Square).then_inc(s["qk_sq"], 1)
            for h in range(HEADS):
                act.wait_ge(unit_done, U + 8 + h + 1)
                a.activation(split(zf[:, h]), halves(2 * (h % 2)), ACT.Copy).then_inc(s["raw_evac"], 1)
            act.wait_ge(s["raw_evac"], 8)
            act.wait_ge(s["ai_mm"], TILES)
            link(a.activation(gate_a, zf, ACT.Abs))
            link(a.activation(gate_a, gate_a, ACT.Exp, scale=-1.0))
            a.activation(gate_a, gate_a, ACT.Ln, bias=ones[:, 0:1]).then_inc(s["gate_l1"], 1)

            def proj(n, dst, h, func):
                act.wait_ge(unit_done, U + n + 1)
                a.activation(split(dst[:, h]), halves(2 * (n % 2)), func).then_inc(s["raw_evac"], 1)

            act.wait_ge(s["qsum_mm"], 4)
            a.activation(rqs[:, 0:4], ps[:, 4, 0:16].rearrange("p (t h) -> p t h", t=4), ACT.Sqrt, bias=eps[:, 0:1],
                         scale=1.0 / DH)
            a.activation(rqs[0:ROWS[4], 4], ps[0:ROWS[4], 4, 16:20], ACT.Sqrt, bias=eps[0:ROWS[4], 0:1],
                         scale=1.0 / DH).then_inc(s["qroot_done"], 1)
            act.wait_ge(s["ksum_mm"], 1)
            a.activation(split(root), halves(6), ACT.Sqrt, bias=eps[:, 0:1], scale=1.0 / DH) \
                .then_inc(s["kroot_done"], 1)
            for h in range(HEADS):
                proj(12 + h, qa, h, ACT.Silu)
            act.wait_ge(s["gate_min"], 2)
            act.wait_ge(s["lb_done"], 1)
            link(a.activation(lb_ln, lb_free, ACT.Ln))
            for h in range(HEADS):
                last = a.activation(gate_a[:, h], gate_b[:, h], ACT.Exp, bias=lb_ln[:, h:h + 1])
            link(last)
            for h in range(HEADS):
                last = a.activation(gate_a[:, h], gate_a[:, h], ACT.Ln, bias=lb_shift[:, h:h + 1])
            last.then_inc(s["gate_ln"], 1)
            for h in range(2):
                proj(16 + h, ag, h, ACT.Sigmoid)
            for h in range(HEADS):
                last = a.activation(ka[:, h], ka[:, h], ACT.Exp, bias=lb_ln[:, h:h + 1])
            last.then_inc(s["gate_ka"], 1)
            for h in range(2, HEADS):
                proj(16 + h, ag, h, ACT.Sigmoid)
            act.wait_ge(s["scan_done"], 1)
            diffs = 0
            for n, (kind, hp, h) in enumerate(DECAYS):
                cols = NT if kind != "level" else MAIN if h == 64 else TAIL0 if h >= 16 else NT
                e = decay[:, n % 2, :, 0:cols]
                if kind == "q":
                    act.wait_ge(s["mult_done"], n - 1)
                    a.activation(e, zf[:, 2 * hp:2 * hp + 2], ACT.Exp).then_inc(s["dexp_done"], 1)
                else:
                    diffs += 1
                    act.wait_ge(s["diff_done"], diffs)
                    a.activation(e, e, ACT.Exp).then_inc(s["dexp_done"], 1)
            a.activation(e_last[:, :, 0:4], zf[:, :, P - 1:MAIN:P], ACT.Exp)
            a.activation(e_last[:, :, 4:5], zf[:, :, TAIL0 - 1:TAIL0], ACT.Exp)
            a.activation(e_last[:, :, 5:6], zf[:, :, NT - 1:NT], ACT.Exp).then_inc(s["elast_done"], 1)
            act.wait_ge(s["mult_done"], len(DECAYS))
            for t in range(TILES):
                act.wait_ge(s["kdt_mm"], t + 1)
                if t == 0:
                    act.wait_ge(s["level_mm"], 16)
                a.activation(kd_tok[0:ROWS[t], t], ps[0:ROWS[t], 6 + t % 2, :], ACT.Copy).then_inc(s["kdt_evac"], 1)
            for t in range(TILES):
                act.wait_ge(s["head_mm"], t + 1)
                if t == 0:
                    act.wait_ge(s["elast_done"], 1)
                r = ROWS[t]
                a.activation(zf[:, :, t * P:t * P + r],
                             ps[:, 6 + t % 2, :].rearrange("p (h n) -> p h n", h=HEADS)[:, :, 0:r], ACT.Copy) \
                    .then_inc(s["head_evac"], 1)
            act.wait_ge(s["head_evac"], TILES)
            for h in range(HEADS):
                if h >= 2:
                    act.wait_ge(s["osum_mm"], h - 1)
                a.activation(square[:, h % 2, :], zf[:, h], ACT.Square).then_inc(s["osq_done"], 1)
            act.wait_ge(s["osum_mm"], HEADS)
            act.wait_ge(s["o_root_set"], 1)
            a.activation(o_root[:, 0:16], ps[:, 0, 0:16], ACT.Sqrt, bias=eps[:, 0:1], scale=1.0 / DH)
            a.activation(o_root[0:ROWS[4], 16:20], ps[0:ROWS[4], 0, 16:20], ACT.Sqrt, bias=eps[0:ROWS[4], 0:1],
                         scale=1.0 / DH).then_inc(s["oroot_done"], 1)
            def exps(t, heads):
                r, x = ROWS[t], t % 2
                for h in heads:
                    act.wait_ge(s["masked_done"], t * HEADS + h + 1)
                    a.activation(probs[x][0:r, h, 0:WIDTH[t]], probs[x][0:r, h, 0:WIDTH[t]], ACT.Exp,
                                 bias=nbias[x][0:r, h:h + 1], scale=rq[0:r, t, h:h + 1],
                                 accum_out=psumv[x][0:r, h:h + 1]).then_inc(s["exp_done"], 1)

            ev = 0
            exps(0, range(HEADS))
            for t in range(TILES):
                r = ROWS[t]
                if t + 1 < TILES:
                    exps(t + 1, (0, 1))
                for c, (kw, kc, parts) in enumerate(key_chunks(t)):
                    act.wait_ge(s["pt_mm"], ev + 1)
                    if c == 0 and t > 0:
                        act.wait_ge(s["pv_mm"], t)
                    for lo, n in parts:
                        last = a.activation(probs_t[0:kw, c, :, lo:lo + n],
                                            ps[0:kw, 4 + ev % 2, :].rearrange("p (h n) -> p h n", h=HEADS)[:, :, lo:lo + n],
                                            ACT.Copy)
                    last.then_inc(s["pt_evac"], 1)
                    ev += 1
                if t + 1 < TILES:
                    exps(t + 1, (2, 3))
                act.wait_ge(s["pv_mm"], t + 1)
                a.activation(normed[:, 4:8, t * P:t * P + r],
                             ps[:, 6 + t % 2, :].rearrange("p (h n) -> p h n", h=HEADS)[:, :, 0:r], ACT.Copy) \
                    .then_inc(s["pv_evac"], 1)
            act.wait_ge(s["pv_mm"], TILES)
            weight_high(2, 0, 0, UP_W, after_units=False)
            squares(1)
            ffn(2, next_stage=3)
            ffn(3, next_stage=5)
            squares(4)
            ffn(5, last=True)

        @block.vector
        def _(dve):
            v = nc.vector
            steps = [0]

            def link(ins):
                steps[0] += 1
                ins.then_inc(dve_step, 1)
                dve.wait_ge(dve_step, steps[0])

            def halves(bank):
                return ps[:, bank:bank + 2, 0:HALF]

            def split(ap):
                return ap.rearrange("p (b n) -> p b n", b=2)

            def norm(stage, write=None, ahead=None):
                dve.wait_ge(root_done, stage + 1)
                v.reciprocal(rnorm_tok, root_tok).then_inc(rnorm_done, 1)
                dve.wait_ge(rnorm_done, stage + 1)
                if stage == 0:
                    dve.wait_ge(ident_in, 16)
                v.tensor_tensor(diag, ident[:].rearrange("p (a n) -> p a n", a=1).to_broadcast([P, TILES, P]),
                                rnorm_tok.rearrange("p (t a) -> p t a", a=1).to_broadcast([P, TILES, P]),
                                ALU.mult).then_inc(diag_done, 1)
                v.memset(square_sum[:], 0.0).then_inc(sumsq_zero, 1)
                if ahead:
                    ahead()
                if stage in FFN_OF_STAGE:
                    weight_scale(stage, 1, 1)
                dve.wait_ge(spread_done, stage + 1)
                if stage in FFN_OF_STAGE:
                    f = FFN_OF_STAGE[stage]
                    for c in range(DC + 1):
                        if 2 <= c < DC:
                            dve.wait_ge(normed_done, DC * NORMED[stage] + c - 1)
                        if c < DC:
                            v.scalar_tensor_tensor(square[:, c % 2, :], resid[:, c, :], gains16[:, stage, c:c + 1],
                                                   rnorm_all, ALU.mult, ALU.mult).then_inc(scaled_done, 1)
                        if c:
                            dve.wait_ge(scaled_done, DC * f + c)
                            dve.wait_ge(nhigh_done, DC * f + c)
                            v.tensor_tensor(normed16[:, 1, c - 1, :], square[:, (c - 1) % 2, :],
                                            normed16[:, 0, c - 1, :], ALU.subtract).then_inc(normed_done, 1)
                    return
                for c in range(DC):
                    if write:
                        write(c)
                    else:
                        v.scalar_tensor_tensor(normed[:, c, :], resid[:, c, :], gains[:, stage, c:c + 1], rnorm_all,
                                               ALU.mult, ALU.mult).then_inc(normed_done, 1)

            def add_one(base, c, b):
                dve.wait_ge(square_done, c + base + 1)
                dve.wait_ge(sumsq_done, c + base)
                v.tensor_tensor(square_sum[:, 0:NT], square_sum[:, 0:NT], square[:, b, :], ALU.add).then_inc(sumsq_done, 1)

            def add_squares(base, i, b):
                add_one(base, i + b, b)

            def update_chunk(stage, unit, c, b, factor):
                dve.wait_ge(unit_done, unit + 2 + 1)
                r = split(resid[:, bass.ds(c, 1), :].rearrange("p a n -> p (a n)"))
                v.scalar_tensor_tensor(r, halves(4 * b), factor, r, ALU.mult, ALU.add).then_inc(resid_done, 1)

            def update_residual(stage, unit0, factor):
                dve.wait_ge(sumsq_zero, stage + 1)
                with dve.Fori(0, DC // 2) as i:
                    for b in range(2):
                        update_chunk(stage, 2 * i + b + unit0, 2 * i + b, b, factor)
                    for b in range(2):
                        add_squares(DC * (stage + 1), 2 * i, b)

            def weight_max(stage, u, b, width):
                n = u + LOAD0[stage]
                slot_loads = (n - b) // 2 if isinstance(n, int) else None
                dve.wait_ge(weights_in[b], 16 * (slot_loads + 1) if slot_loads is not None else n * 8 + 16 - 8 * b)
                v.tensor_reduce(wmax[:, b:b + 1], wslot[:, b, 0:width], AXIS_X, ALU.max, apply_absolute_value=True) \
                    .then_inc(wmax_done, 1)

            def weight_scale(stage, u, b):
                n = u + FFN_OF_STAGE[stage] * FFN_UNITS + 1
                dve.wait_ge(wall_done, n)
                v.tensor_scalar(wexp[:, b:b + 1].bitcast(U32), wall[:, b:b + 1].bitcast(U32), EXPONENT, None,
                                ALU.bitwise_and).then_inc(wexp_done, 1)
                dve.wait_ge(wexp_done, n)
                v.tensor_scalar(wdown[:, b:b + 1], wexp[:, b:b + 1], 2.0 ** -13, TINY, ALU.mult, ALU.max) \
                    .then_inc(wdown_done, 1)
                dve.wait_ge(wdown_done, n)
                v.reciprocal(wscale[:, b:b + 1], wdown[:, b:b + 1]).then_inc(wscale_done, 1)

            def weight_back(stage, u, b, inv=None):
                if inv is None:
                    v.tensor_scalar(wback_last[:, b:b + 1], wdown[:, b:b + 1], inv_h[:, 1:2], None, ALU.mult)
                    inv = inv_h[:, 0:1]
                v.tensor_scalar(wback[:, b:b + 1], wdown[:, b:b + 1], inv, None, ALU.mult).then_inc(wback_done, 1)

            def weight_low(stage, u, b, width):
                dve.wait_ge(whigh_done, u + FFN_OF_STAGE[stage] * FFN_UNITS + 1)
                v.scalar_tensor_tensor(w16[:, b, 1, 0:width], wslot[:, b, 0:width], wscale[:, b:b + 1],
                                       w16[:, b, 0, 0:width], ALU.mult, ALU.subtract).then_inc(wlow_done, 1)

            def first_unit(stage):
                weight_max(stage, 0, 0, UP_W)
                weight_scale(stage, 0, 0)
                weight_back(stage, 0, 0, inv_x[:, stage:stage + 1])
                weight_low(stage, 0, 0, UP_W)
                weight_max(stage, 1, 1, UP_W)

            def hidden_chunk(stage, u, b):
                f = FFN_OF_STAGE[stage]
                dve.wait_ge(silu_done, u + FC * f + 1)
                dve.wait_ge(wback_done, u + f * FFN_UNITS + 1)
                h = hidden[:, bass.ds(u, 1), :].rearrange("p a n -> p (a n)")
                v.scalar_tensor_tensor(split(h), halves(4 * b + 2), wback[:, b:b + 1], split(act_out[:, b, :]),
                                       ALU.mult, ALU.mult).then_inc(hid_done, 1)
                dve.wait_ge(hid_done, u + FC * f + 2 + 1)
                v.tensor_reduce(hmax[:, bass.ds(u, 1)], h, AXIS_X, ALU.max, apply_absolute_value=True) \
                    .then_inc(hpart_done, 1)

            def ffn(stage, next_stage=None, last=False):
                f = FFN_OF_STAGE[stage]
                ix = inv_x[:, stage:stage + 1]
                weight_back(stage, 1, 1, ix)
                weight_low(stage, 1, 1, UP_W)
                weight_max(stage, 2, 0, UP_W)

                def up_turn(u, b, next_w, after_w):
                    weight_scale(stage, u + 1, 1 - b)
                    hidden_chunk(stage, u - 1, 1 - b)
                    if next_w == UP_W:
                        weight_back(stage, u + 1, 1 - b, ix)
                    weight_low(stage, u + 1, 1 - b, next_w)
                    weight_max(stage, u + 2, b, after_w)

                with dve.Fori(0, FC // 2 - 2) as i:
                    up_turn(2 * i + 1, 1, UP_W, UP_W)
                    up_turn(2 * i + 2, 0, UP_W, UP_W)
                up_turn(FC - 3, 1, UP_W, UP_W)
                up_turn(FC - 2, 0, UP_W, DN_W)

                def hidden_scale(part):
                    c = slice(part, part + 1)
                    dve.wait_ge(hall_done, 2 * f + part + 1)
                    link(v.tensor_scalar(hexp[:, c].bitcast(U32), hall[:, c].bitcast(U32), EXPONENT, None,
                                         ALU.bitwise_and))
                    link(v.tensor_scalar(hdown[:, c], hexp[:, c], 2.0 ** -13, TINY, ALU.mult, ALU.max))
                    v.reciprocal(hscale[:, c], hdown[:, c]).then_inc(hscale_done, 1)
                    link(v.tensor_scalar(inv_h[:, c], hdown[:, c], 0.5, None, ALU.mult))
                    dve.wait_ge(hscale_done, 2 * f + part + 1)

                def hidden_low(i, part):
                    dve.wait_ge(hhigh_done, i + FC * f + 1)
                    v.scalar_tensor_tensor(hidden16[:, 1, bass.ds(i, 1), :].rearrange("p a n -> p (a n)"),
                                           hidden[:, bass.ds(i, 1), :].rearrange("p a n -> p (a n)"),
                                           hscale[:, part:part + 1],
                                           hidden16[:, 0, bass.ds(i, 1), :].rearrange("p a n -> p (a n)"),
                                           ALU.mult, ALU.subtract).then_inc(hlow_done, 1)

                weight_scale(stage, FC, 0)
                weight_max(stage, FC + 1, 1, DN_W)
                hidden_chunk(stage, FC - 2, 0)
                dve.wait_ge(hpart_done, FC * (f + 1) - 1)
                v.tensor_reduce(hmax1, hmax[:, 0:FC - 1], AXIS_X, ALU.max).then_inc(hmax_done, 1)
                hidden_scale(0)
                weight_scale(stage, FC + 1, 1)
                with dve.Fori(0, EARLY) as i:
                    hidden_low(i, 0)
                hidden_chunk(stage, FC - 1, 1)
                hidden_scale(1)
                weight_back(stage, FC, 0)
                weight_back(stage, FC + 1, 1)
                with dve.Fori(EARLY, FC - 1) as i:
                    hidden_low(i, 0)
                hidden_low(FC - 1, 1)
                weight_max(stage, FC + 2, 0, DN_W)
                dve.wait_ge(sumsq_zero, stage + 1)

                def down_update(unit, c, b):
                    dve.wait_ge(wback_done, unit - UNIT0[stage] + f * FFN_UNITS + 1)
                    dve.wait_ge(part_mm, c + DC * f + 1)
                    r = split(resid[:, bass.ds(c, 1), :].rearrange("p a n -> p (a n)"))
                    v.scalar_tensor_tensor(r, halves(4 * b), wback[:, b:b + 1], r, ALU.mult, ALU.add) \
                        .then_inc(rpart_done, 1)
                    dve.wait_ge(rpart_done, c + DC * f + 1)
                    dve.wait_ge(unit_done, unit + 2 + 1)
                    v.scalar_tensor_tensor(r, halves(4 * b + 2), wback_last[:, b:b + 1], r, ALU.mult, ALU.add) \
                        .then_inc(resid_done, 1)

                def down_turn(u, c, b, split_next=True, after=None, add=True):
                    if split_next:
                        weight_scale(stage, u + 1, 1 - b)
                    down_update(u - 1 + UNIT0[stage], c, 1 - b)
                    if split_next:
                        dve.wait_ge(resid_done, c + 2 + DC * stage + 1)
                        weight_back(stage, u + 1, 1 - b)
                        weight_low(stage, u + 1, 1 - b, DN_W)
                    if after:
                        weight_max(stage, u + 2, b, after)
                    if add and not last:
                        add_one(DC * (stage + 1), c - 1, b)

                dve.wait_ge(wlow_done, f * FFN_UNITS + FC + 2 + 2)
                down_turn(FC + 1, 0, 1, after=DN_W, add=False)
                with dve.Fori(0, DC // 2 - 2) as i:
                    down_turn(2 * i + FC + 2, 2 * i + 1, 0, after=DN_W)
                    down_turn(2 * i + FC + 3, 2 * i + 2, 1, after=DN_W)
                down_turn(FFN_UNITS - 2, DC - 3, 0)
                if next_stage:
                    weight_max(next_stage, 0, 0, UP_W)
                    weight_scale(next_stage, 0, 0)
                down_turn(FFN_UNITS - 1, DC - 2, 1, split_next=False)
                if next_stage:
                    dve.wait_ge(resid_done, DC * stage + DC + 1)
                    weight_back(next_stage, 0, 0, inv_x[:, next_stage:next_stage + 1])
                    weight_low(next_stage, 0, 0, UP_W)
                    weight_max(next_stage, 1, 1, UP_W)
                down_update(UNIT0[stage] + FFN_UNITS - 1, DC - 1, 1)
                if not last:
                    for c in range(DC - 2, DC):
                        add_one(DC * (stage + 1), c, c % 2)

            v.memset(ones[:], 1.0).then_inc(ones_set, 1)
            v.memset(eps[:], RMS_EPS).then_inc(ones_set, 1)
            v.memset(square_sum[:], 0.0).then_inc(ones_set, 1)
            v.memset(act_out[:, 0, 0:1], 0.0).then_inc(hid_done, 2)
            v.memset(act_out[:, 0, 1:2], 0.0).then_inc(resid_done, 2)
            v.memset(act_out[:, 0, 2:3], 0.0).then_inc(wlow_done, 2)
            dve.wait_ge(gains_in, 16)
            v.tensor_reduce(gmax, gains[:], AXIS_X, ALU.max, apply_absolute_value=True).then_inc(gmax_done, 1)
            dve.wait_ge(ones_set, 3)
            for c in range(DC):
                dve.wait_ge(square_done, c + 1)
                if c:
                    dve.wait_ge(sumsq_done, c)
                v.tensor_tensor(square_sum[:, 0:NT], square_sum[:, 0:NT], square[:, c % 2, :], ALU.add).then_inc(sumsq_done, 1)
            dve.wait_ge(gall_done, 1)
            link(v.tensor_scalar(gexp.bitcast(U32), gall.bitcast(U32), EXPONENT, None, ALU.bitwise_and))
            link(v.tensor_scalar(inv_x, gexp, 2.0 ** -9, TINY, ALU.mult, ALU.max))
            link(v.reciprocal(gscale, inv_x))
            link(v.tensor_tensor(gains16, gains[:], gscale.rearrange("p (s a) -> p s a", a=1).to_broadcast([P, 6, DC]),
                                 ALU.mult))
            weight_max(0, 0, 0, UP_W)

            def split_first():
                weight_scale(0, 0, 0)
                weight_max(0, 1, 1, UP_W)
                weight_back(0, 0, 0, inv_x[:, 0:1])
                weight_low(0, 0, 0, UP_W)

            norm(0, ahead=split_first)
            ffn(0)
            norm(1)

            dve.wait_ge(consts_in, 16 * 7)
            link(v.tensor_tensor(lb_e, lb_in, lb_in, ALU.subtract))
            link(v.tensor_scalar(lb_e, lb_e, 1.0, None, ALU.add))
            link(v.reciprocal(lb_shift, lb_e))
            link(v.tensor_tensor(lb_e, lb_e, lb_shift, ALU.mult))
            link(v.tensor_tensor(lb, lb_e, lb_e, ALU.subtract))
            link(v.tensor_scalar(lb_free, lb, -1.0, 1.0, ALU.mult, ALU.add))
            link(v.tensor_scalar(lb_on, lb, 0.0, None, ALU.is_gt))
            link(v.tensor_scalar(lb_e, lb_on, -1.0, 1.0, ALU.mult, ALU.add))
            v.tensor_tensor(lb_shift, lb, lb_e, ALU.add).then_inc(s["lb_done"], 1)
            def rope(x, table, bank):
                link(v.tensor_tensor(x, x, ropes[:, 0], ALU.mult))
                link(v.tensor_tensor(split(act_out[:, 0, :]), halves(bank), split(ropes[:, 1]), ALU.mult))
                v.tensor_tensor(x, x, act_out[:, 0, :], ALU.add).then_inc(s["rope_done"], 1)

            dve.wait_ge(s["rope_in"], 16)
            for n, x in enumerate((kit, qit[:, 0], qit[:, 1])):
                dve.wait_ge(s["perm_mm"], n + 1)
                rope(x, 0, 6)
            n = 0
            for t in range(TILES):
                r, w = ROWS[t], WIDTH[t]
                for h in range(IDX_HEADS):
                    dve.wait_ge(s["relu_done"], n + 1)
                    if h == 0:
                        if t == 0:
                            dve.wait_ge(s["vw_evac"], TILES)
                        ins = v.tensor_scalar(score[0:r, t, 0:w], relu_sc[0:r, n % 2, 0:w], wi[0:r, t, 0:1], None,
                                              ALU.mult)
                    else:
                        ins = v.scalar_tensor_tensor(score[0:r, t, 0:w], relu_sc[0:r, n % 2, 0:w],
                                                     wi[0:r, t, h:h + 1], score[0:r, t, 0:w], ALU.mult, ALU.add)
                    ins.then_inc(s["isc_acc"], 1)
                    n += 1
                    dve.wait_ge(s["isc_acc"], n)
                if t < 4:
                    link(v.tensor_tensor(score[:, t, t * P:t * P + 144], score[:, t, t * P:t * P + 144], adm, ALU.add))
                else:
                    last = PAST + N_SAMPLE
                    link(v.memset(score[0:N_SAMPLE, t, last:last + TOPK - TOPK_SAMPLE], PAD_TOP))
                    link(v.memset(score[0:N_SAMPLE, t, last + TOPK - TOPK_SAMPLE:528], NEG_BIG))
            for t in range(TILES):
                sc = score[0:ROWS[t], t, 0:WIDTH[t]]
                for _ in range(TOPK // 8):
                    link(v.max(max8[0:ROWS[t]], sc))
                    link(v.match_replace(sc, max8[0:ROWS[t]], sc, TAKEN))
                link(v.tensor_scalar(sc, sc, -2e38, NEG_BIG, ALU.is_gt, ALU.mult))
                if t < 4:
                    link(v.tensor_tensor(score[:, t, t * P:t * P + 144], score[:, t, t * P:t * P + 144], adm, ALU.min))
                else:
                    link(v.memset(score[0:N_SAMPLE, t, PAST + N_SAMPLE:528], NEG_BIG))
            dve.wait_ge(s["kroot_done"], 1)
            link(v.reciprocal(rnorm, root))
            v.scalar_tensor_tensor(kt, kt, cgain[:, 1:2], rnorm, ALU.mult, ALU.mult).then_inc(s["k_normed"], 1)
            dve.wait_ge(s["k_normed"], 1)
            dve.wait_ge(s["rope_in"], 32)
            dve.wait_ge(s["qroot_done"], 1)
            link(v.reciprocal(rq[:, 0:4], rqs[:, 0:4]))
            link(v.reciprocal(rq[0:ROWS[4], 4], rqs[0:ROWS[4], 4]))
            link(v.tensor_scalar(rq[:, 0:4], rq[:, 0:4], DH ** -0.5, None, ALU.mult))
            link(v.tensor_scalar(rq[0:ROWS[4], 4], rq[0:ROWS[4], 4], DH ** -0.5, None, ALU.mult))
            for n in range(5):
                if n == 4:
                    dve.wait_ge(s["gate_logf"], 1)
                    for h in range(HEADS):
                        for lo, w in SEGMENTS:
                            last = v.tensor_tensor_scan(zf[:, h, lo:lo + w], ones[:, 0:w], zf[:, h, lo:lo + w], 0.0, ALU.mult,
                                                        ALU.add)
                    last.then_inc(s["scan_done"], 1)
                dve.wait_ge(s["kperm_mm"], n + 1)
                rope(kt if n == 0 else qt[:, n - 1], 1, 6)
                dve.wait_ge(s["rope_done"], 3 + n + 1)
            v.memset(o_root, 1.0).then_inc(s["o_root_set"], 1)
            dve.wait_ge(s["gate_ka"], 1)
            dve.wait_ge(s["raw_evac"], 16)
            dve.wait_ge(s["att_zero"], 1)
            nd = lv = 0

            def collect(n):
                kind, hp, h = LEVEL_PASSES[n]
                m = LEVELS.index(h) if kind == "level" else len(LEVELS)
                dve.wait_ge(s["level_mm"], n + 1)
                if n:
                    dve.wait_ge(s["att_evac"], n)
                for pair in range(2):
                    last = v.copy_predicated(
                        att[:, 2 * pair:2 * pair + 2, 2 * hp:2 * hp + 2, :],
                        masks[:, m:m + 1, :].rearrange("p (a b) n -> p a b n", b=1).to_broadcast([P, 2, 2, P]),
                        ps[:, 3 * (n % 2) + pair, :].rearrange("p (a b n) -> p a b n", a=2, b=2))
                if not (kind == "level" and h == 64):
                    r = N_SAMPLE if kind == "level" and h >= 16 else ROWS[4]
                    last = v.copy_predicated(
                        att[0:r, 4, 2 * hp:2 * hp + 2, 0:r],
                        masks[0:r, m:m + 1, 0:r].to_broadcast([r, 2, r]),
                        ps[0:r, 3 * (n % 2) + 2, 0:256].rearrange("p (b n) -> p b n", b=2)[:, :, 0:r])
                last.then_inc(s["att_evac"], 1)

            lv = 0
            for kind, hp, h in PASSES:
                if kind == "diag":
                    lv += 1
                    collect(lv - 2)
                    continue
                dve.wait_ge(s["dexp_done"], nd + 1)
                e, gd = decay[:, nd % 2], decayed[:, lv % 2]
                k2, q2 = ka[:, 2 * hp:2 * hp + 2], qa[:, 2 * hp:2 * hp + 2]
                if kind == "level":
                    if lv >= 2:
                        dve.wait_ge(s["level_mm"], lv - 1)
                    cols = MAIN if h == 64 else TAIL0 if h >= 16 else NT

                    def blocks(ap):
                        return ap[:, :, 0:cols].rearrange("p a (n x) -> p a n x", x=2 * h)
                    v.tensor_tensor(blocks(gd)[:, :, :, 0:h], blocks(e)[:, :, :, 0:h], blocks(k2)[:, :, :, 0:h], ALU.mult)
                    v.tensor_tensor(blocks(gd)[:, :, :, h:2 * h], blocks(e)[:, :, :, h:2 * h],
                                    blocks(q2)[:, :, :, h:2 * h], ALU.mult).then_inc(s["mult_done"], 1)
                    lv += 1
                    if lv >= 2:
                        collect(lv - 2)
                else:
                    if kind == "k" and hp == 0:
                        collect(lv - 1)
                    if kind == "q":
                        v.tensor_tensor(q2, q2, e, ALU.mult).then_inc(s["mult_done"], 1)
                    else:
                        v.tensor_tensor(k2, k2, e, ALU.mult).then_inc(s["mult_done"], 1)
                nd += 1
            dve.wait_ge(s["elast_done"], 1)
            dve.wait_ge(s["state_in"], 16)
            dve.wait_ge(s["out_sem"], 16 * 4)
            for i in range(6):
                dve.wait_ge(s["delta_mm"], i + 1)
                src = states_hi[:, 2] if i == 5 else state(max(i - 1, 0))
                dst = states_hi[:, 3] if i == 5 else state(i)
                seg = (0, 1, 2, 3, 5, 4)[i]
                if i == 0:
                    last = v.tensor_copy(dst, ps[:, 0, :])
                else:
                    if i < 5:
                        dve.wait_ge(s["state_done"], i)
                    for h in range(HEADS):
                        c = slice(h * DH, (h + 1) * DH)
                        last = v.scalar_tensor_tensor(dst[:, c], src[:, c], e_last[:, h, seg:seg + 1], ps[:, i, c],
                                                      ALU.mult, ALU.add)
                last.then_inc(s["state_done"] if i < 5 else s["sample_state"], 1)
            dve.wait_ge(s["oroot_done"], 1)
            link(v.reciprocal(o_rnorm, o_root))
            for h in range(HEADS + 1):
                if h < HEADS:
                    if h >= 2:
                        dve.wait_ge(s["ospread_mm"], h - 1)
                    v.tensor_tensor(o_diag[h % 2].rearrange("p (t n) -> p t n", t=TILES),
                                    ident[:].rearrange("p (a n) -> p a n", a=1).to_broadcast([P, TILES, P]),
                                    o_rnorm[:, h:20:HEADS].rearrange("p (t a) -> p t a", a=1)
                                    .to_broadcast([P, TILES, P]), ALU.mult).then_inc(s["odiag_done"], 1)
                if h:
                    g = act_out[:, (h - 1) % 2, :]
                    dve.wait_ge(s["ospread_mm"], h)
                    at = (4 + 2 * ((h - 1) % 2)) * 512
                    link(v.scalar_tensor_tensor(g, psf[:, at:at + NT], cgain[:, 3 + h:4 + h], ag[:, h - 1], ALU.mult,
                                                ALU.mult))
                    v.tensor_tensor(normed[:, h - 1, :], zf[:, h - 1], g, ALU.mult).then_inc(s["oa_done"], 1)
            dve.wait_ge(s["oa_done"], HEADS)
            for t in range(TILES + 1):
                if t:
                    r, w, x = ROWS[t - 1], WIDTH[t - 1], (t - 1) % 2
                    for h in range(HEADS):
                        dve.wait_ge(s["exp_done"], (t - 1) * HEADS + h + 1)
                        link(v.reciprocal(pinv[x][0:r, h:h + 1], psumv[x][0:r, h:h + 1]))
                        v.tensor_scalar(probs[x][0:r, h, 0:w], probs[x][0:r, h, 0:w], pinv[x][0:r, h:h + 1], None,
                                        ALU.mult).then_inc(s["p_done"], 1)
                if t == TILES:
                    break
                r, w, x = ROWS[t], WIDTH[t], t % 2
                for h in range(HEADS):
                    dve.wait_ge(s["logit_mm"], t * HEADS + h + 1)
                    if h == 0 and t >= 2:
                        dve.wait_ge(s["pt_mm"], sum(len(key_chunks(i)) for i in range(t - 1)))
                    bank = 2 * (h % 2)
                    link(v.tensor_tensor_reduce(out=probs[x][0:r, h, 0:w], in0=psf[0:r, bank * 512:bank * 512 + w],
                                                in1=score[0:r, t, 0:w], scale=1.0, scalar=TAKEN, op0=ALU.add,
                                                op1=ALU.max, accum_out=mx[x][0:r, h:h + 1]))
                    v.tensor_scalar(nbias[x][0:r, h:h + 1], mx[x][0:r, h:h + 1], rq[0:r, t, h:h + 1], -1.0, ALU.mult,
                                    ALU.mult).then_inc(s["masked_done"], 1)
                    dve.wait_ge(s["masked_done"], t * HEADS + h + 1)
            dve.wait_ge(s["out_sem"], 16 * 6)
            first_unit(2)
            update_residual(1, UNIT0[1] + IN_UNITS, 1.0)
            norm(2)
            ffn(2, next_stage=3)
            norm(3)
            ffn(3, next_stage=5)

            def to_ue(c):
                if c == 0:
                    dve.wait_ge(unit_done, UNIT0[3] + FFN_UNITS + 2)
                    dve.wait_ge(resid_done, 2 + DC * 4)
                for lo, n, dst in ((0, MAIN, PP0), (TAIL0, TAIL, PP0 + MAIN), (SMP0, N_SAMPLE, PS0)):
                    v.scalar_tensor_tensor(ue[:, c, dst:dst + n], resid[:, c, lo:lo + n], gains[:, 4, c:c + 1],
                                           rnorm_all[:, lo:lo + n], ALU.mult, ALU.mult).then_inc(s["ue_done"], 1)
            norm(4, to_ue)
            dve.wait_ge(s["ue_done"], 3 * DC)
            dve.wait_ge(s["pool_in"], 48)
            dve.wait_ge(s["hist_zero"], 1)
            bufs = (sums, sums2)

            def window_sums(gi):
                cs, step, k = slice(2 * gi, 2 * gi + 2), 1, 0
                src = ue[:, cs]
                while step < POOL_WINDOWS[gi]:
                    dst = bufs[k % 2][:, cs]
                    lo = 2 * step - 1
                    link(v.tensor_tensor(dst[:, :, lo:UE], src[:, :, lo:UE], src[:, :, lo - step:UE - step], ALU.add))
                    src, step, k = dst, 2 * step, k + 1

            def means(gi):
                cs, w = slice(2 * gi, 2 * gi + 2), POOL_WINDOWS[gi]
                src, dst = bufs[gi % 2][:, cs], bufs[(gi + 1) % 2][:, cs]
                for lo, n, at in ((16, MAIN - 16, PP0 + 16), (TAIL0, TAIL, PP0 + MAIN), (SMP0, N_SAMPLE, PS0)):
                    v.scalar_tensor_tensor(pooled[:, cs, lo:lo + n], src[:, :, at:at + n], 1.0 / w,
                                           ue[:, cs, at:at + n], ALU.mult, ALU.subtract)
                link(v.tensor_tensor(dst[:, :, PP0:PP0 + 16], src[:, :, PP0:PP0 + 16],
                                     inv_cnt[:, gi:gi + 1, :].to_broadcast([P, 2, 16]), ALU.mult))
                v.tensor_tensor(pooled[:, cs, 0:16], dst[:, :, PP0:PP0 + 16], ue[:, cs, PP0:PP0 + 16],
                                ALU.subtract).then_inc(s["pwin_done"], 1)

            def pool_update(gi):
                for c in (2 * gi, 2 * gi + 1):
                    dve.wait_ge(s["pool_mm"], c + 1)
                    r = split(resid[:, c, :])
                    v.scalar_tensor_tensor(r, halves(POOL_BANKS[c % 3]), pscale[:, c:c + 1], r, ALU.mult, ALU.add) \
                        .then_inc(resid_done, 1)

            window_sums(0)
            means(0)
            window_sums(3)
            dve.wait_ge(s["psum_done"], 1)
            means(1)
            pool_update(0)
            dve.wait_ge(s["psum_done"], 2)
            means(2)
            pool_update(1)
            means(3)
            pool_update(2)
            pool_update(3)
            norm(5)
            dve.wait_ge(s["out_sem"], 16 * 8)
            ffn(5, last=True)

        @block.tensor
        def _(pe):
            mm = nc.tensor.matmul

            def arrived(unit, b, i=0):
                pe.wait_ge(weights_in[b], 16 * (i + unit // 2 + 1))

            def sum_squares(stage):
                pe.wait_ge(sumsq_done, DC * (stage + 1))
                for t in range(TILES):
                    last = mm(ps[:, 2, t:t + 1], square_sum[:, t * P:(t + 1) * P], ones[:, 0:1], start=True, stop=True)
                last.then_inc(sumall_done, 1)
                spread(stage)

            def spread(stage):
                pe.wait_ge(diag_done, stage + 1)
                for lo, n in ((0, MAIN), (MAIN, NT - MAIN)):
                    last = mm(rnorm_all[:, lo:lo + n], ones[:], norm_work[:, lo:lo + n], start=True, stop=True)
                last.then_inc(spread_done, 1)

            def product(bank, w, x, k, n):
                for hf in range(2):
                    last = mm(ps[:, bank + hf, 0:HALF], w, x[:, hf * HALF:(hf + 1) * HALF], start=(k == 0),
                              stop=(k == n - 1))
                return last

            def product_part(bank, w, x, start, stop):
                for hf in range(2):
                    last = mm(ps[:, bank + hf, 0:HALF], w, x[:, hf * HALF:(hf + 1) * HALF], start=start, stop=stop)
                return last

            def product16(bank, w_high, w_low, x_high, x_low, k, n):
                product_part(bank, w_high, x_high, k == 0, False)
                product_part(bank, w_high, x_low, False, False)
                return product_part(bank, w_low, x_high, False, k == n - 1)

            def ffn(stage, last_stage=False):
                f = FFN_OF_STAGE[stage]
                n0 = f * FFN_UNITS
                with pe.Fori(0, FC // 2) as i:
                    for b in range(2):
                        pe.wait_ge(wlow_done, 2 * i + b + n0 + 2 + 1)
                        pe.wait_ge(hid_done, 2 * i + b + FC * f + 1)
                        w = w16[:, b, :, 0:UP_W].rearrange("p a (g c n) -> p a g c n", g=2, c=DC)
                        for c in range(DC):
                            if b == 0:
                                pe.wait_ge(nhigh_done, DC * f + c + 1)
                            for gu in range(2):
                                for a in range(2):
                                    product_part(4 * b + 2 * gu, w[:, a, gu, c, :], normed16[:, 0, c, :],
                                                 c == 0 and a == 0, False)
                            if b == 0:
                                pe.wait_ge(normed_done, DC * NORMED[stage] + c + 1)
                            for gu in range(2):
                                last = product_part(4 * b + 2 * gu, w[:, 0, gu, c, :], normed16[:, 1, c, :], False,
                                                    c == DC - 1)
                        last.then_inc(unit_done, 1)

                def down(i, b, follow):
                    pe.wait_ge(wlow_done, 2 * i + b + n0 + FC + 2 + 1)
                    pe.wait_ge(resid_done, 2 * i + b + DC * stage + 1)
                    w = w16[:, b, :, 0:DN_W].rearrange("p a (c n) -> p a c n", c=FC)
                    for c in range(FC):
                        if follow:
                            pe.wait_ge(hlow_done, FC * f + c + 1)
                        bank, k, n = (4 * b, c, FC - 1) if c < FC - 1 else (4 * b + 2, 0, 1)
                        last = product16(bank, w[:, 0, c, :], w[:, 1, c, :], hidden16[:, 0, c, :],
                                         hidden16[:, 1, c, :], k, n)
                        if c == FC - 2:
                            last.then_inc(part_mm, 1)
                    last.then_inc(unit_done, 1)

                down(0, 0, True)
                down(0, 1, False)
                with pe.Fori(1, DC // 2) as i:
                    for b in range(2):
                        down(i, b, False)
                if not last_stage:
                    sum_squares(stage + 1)

            pe.wait_ge(ones_set, 3)
            pe.wait_ge(ident_in, 16)
            mm(ps[:, 7, 0:2], ones[:], ones[:, 0:2], start=True, stop=True).then_inc(unit_done, 2)
            sum_squares(0)
            ffn(0)

            U = UNIT0[1]
            x = normed

            def cols(t):
                return slice(t * P, t * P + ROWS[t])

            def in_unit(n):
                arrived(U + n, n % 2)
                if 2 <= n < 8:
                    pe.wait_ge(s["qk_sq" if 5 <= n else "raw_evac"], n - 4 if 5 <= n else n - 1 if n < 5 else 0)
                w = wslot[:, n % 2, 0:DC * P].rearrange("p (c n) -> p c n", c=DC)
                for c in range(DC):
                    if n == 0:
                        pe.wait_ge(normed_done, DC + c + 1)
                    last = product(2 * (n % 2), w[:, c, :], x[:, c, :], c, DC)
                last.then_inc(unit_done, 1)

            def exchange(table, src, bank, signal):
                last = product(bank, perms[:, table, :], src, 0, 1)
                last.then_inc(signal, 1)

            in_unit(0)
            pe.wait_ge(s["vw_in"], 16)
            for t in range(TILES):
                if t >= 2:
                    pe.wait_ge(s["vw_evac"], t - 1)
                for c in range(DC):
                    last = mm(ps[0:ROWS[t], 4 + t % 2, 0:VW], x[:, c, cols(t)], w_vw[:, c, :], start=(c == 0),
                              stop=(c == DC - 1))
                last.then_inc(s["vw_mm"], 1)
            pe.wait_ge(consts_in, 16 * 7)
            for n, src in enumerate((kit, qit[:, 0], qit[:, 1])):
                if n:
                    in_unit(n)
                    pe.wait_ge(s["raw_evac"], n)
                    if n >= 2:
                        pe.wait_ge(s["rope_done"], n - 1)
                    exchange(0, (kit, qit[:, 0])[n - 1], 6, s["perm_mm"])
            pe.wait_ge(s["ai_in"], 16)
            for t in range(TILES):
                pe.wait_ge(s["vw_evac"], TILES)
                if t >= 2:
                    pe.wait_ge(s["ai_evac"], t - 1)
                for c in range(DC):
                    last = mm(ps[0:ROWS[t], 4 + t % 2, :], x[:, c, cols(t)], w_ai[:, c, :], start=(c == 0),
                              stop=(c == DC - 1))
                last.then_inc(s["ai_mm"], 1)
                if t == 0:
                    pe.wait_ge(s["raw_evac"], 3)
                    pe.wait_ge(s["rope_done"], 2)
                    exchange(0, qit[:, 1], 6, s["perm_mm"])
            pe.wait_ge(s["rope_done"], 3)
            pe.wait_ge(s["ai_evac"], TILES)
            n = 0
            for t in range(TILES):
                for h in range(IDX_HEADS):
                    if n >= 2:
                        pe.wait_ge(s["relu_done"], n - 1)
                    bank = 4 + 2 * (n % 2)
                    rows = slice(IDX_DIM * (h % 2), IDX_DIM * (h % 2) + IDX_DIM)
                    w = min(WIDTH[t], MAIN)
                    q = qit[rows, h // 2, cols(t)]
                    last = mm(ps[0:ROWS[t], bank, 0:w], q, kit[rows, 0:w], start=True, stop=True)
                    if WIDTH[t] > MAIN:
                        last = mm(ps[0:ROWS[t], bank + 1, 0:TAIL], q, kit[rows, TAIL0:NT], start=True, stop=True)
                    if t == 4:
                        q = qit[rows, h // 2, SMP0:TAIL0]
                        mm(ps[0:N_SAMPLE, bank, 0:PAST], q, cache[rows, 1, :], start=True, stop=True)
                        last = mm(ps[0:N_SAMPLE, bank, PAST:PAST + N_SAMPLE], q, kit[rows, SMP0:TAIL0], start=True,
                                  stop=True)
                    last.then_inc(s["isc_mm"], 1)
                    n += 1
            in_unit(3)
            for n in range(4, 8):
                if n == 4:
                    pe.wait_ge(s["raw_evac"], 3)
                in_unit(n)
                pe.wait_ge(s["qk_sq"], n - 3)
                pe.wait_ge(s["relu_done"], 4 * TILES)
                if n == 4:
                    product(6, ones[:], square[:, 0, :], 0, 1).then_inc(s["ksum_mm"], 1)
                else:
                    head_square_sums(mm, ps, square, ones, n - 5, s)
            pe.wait_ge(s["qk_sq"], 5)
            for n in range(8, IN_UNITS):
                if n < 10:
                    pass
                else:
                    pe.wait_ge(s["raw_evac"], n - 5)
                in_unit(n)
                if n == 8:
                    head_square_sums(mm, ps, square, ones, 3, s)
                if n >= 15:
                    pe.wait_ge(s["k_normed"], 1)
                    if n > 15:
                        pe.wait_ge(s["rope_done"], 3 + n - 15)
                    exchange(1, kt if n == 15 else qt[:, n - 16], 6, s["kperm_mm"])
            pe.wait_ge(s["rope_done"], 8)
            pe.wait_ge(s["kroot_done"], 1)
            pe.wait_ge(s["qroot_done"], 1)
            for n, (kind, hp, h) in enumerate(LEVEL_PASSES):
                if n >= 2:
                    pe.wait_ge(s["att_evac"], n - 1)
                if kind == "level":
                    pe.wait_ge(s["mult_done"], n + 1 if hp == 0 else n)
                else:
                    pe.wait_ge(s["gate_ka"], 1)
                for t in range(TILES):
                    r = ROWS[t]
                    if t == 4 and kind == "level":
                        if h == 64:
                            continue
                        if h >= 16:
                            r = N_SAMPLE
                    for a in range(2):
                        if kind == "level":
                            left = right = decayed[:, n % 2, a, t * P:t * P + r]
                        else:
                            left, right = ka[:, 2 * hp + a, t * P:t * P + r], qa[:, 2 * hp + a, t * P:t * P + r]
                        at = (t % 2) * 256 + a * P if t < 4 else a * P
                        last = mm(ps[0:r, 3 * (n % 2) + t // 2, at:at + r], left, right, start=True, stop=True)
                last.then_inc(s["level_mm"], 1)
            pe.wait_ge(s["mult_done"], len(DECAYS) - 2)
            for t in range(TILES):
                if t >= 2:
                    pe.wait_ge(s["kdt_evac"], t - 1)
                for h in range(HEADS):
                    last = nc.tensor.transpose(ps[0:ROWS[t], 6 + t % 2, h * DH:(h + 1) * DH], ka[:, h, cols(t)],
                                               ident[:])
                last.then_inc(s["kdt_mm"], 1)
            pe.wait_ge(s["att_evac"], 16)
            pe.wait_ge(s["kdt_evac"], TILES)
            pe.wait_ge(s["ai_evac"], TILES)
            for i in range(6):
                t, rows = (i, slice(0, P)) if i < 4 else (4, slice(N_SAMPLE, ROWS[4])) if i == 4 else (4, slice(0, N_SAMPLE))
                for h in range(HEADS):
                    c = slice(h * DH, (h + 1) * DH)
                    last = mm(ps[:, i, c], kd_tok[rows, t, c], va[rows, t, c], start=True, stop=True)
                last.then_inc(s["delta_mm"], 1)
            for t in range(TILES):
                if t >= 2:
                    pe.wait_ge(s["head_evac"], t - 1)
                if t:
                    pe.wait_ge(s["mult_done"], len(DECAYS))
                    pe.wait_ge(s["state_done"], t)
                if t == 4:
                    pe.wait_ge(s["state_in"], 16)
                o = ps[:, 6 + t % 2, :].rearrange("p (h n) -> p h n", h=HEADS)
                for h in range(HEADS):
                    c = slice(h * DH, (h + 1) * DH)
                    if t < 4:
                        last = mm(o[:, h, :], va[:, t, c], att[:, t, h, :], start=True, stop=(t == 0))
                        if t:
                            last = mm(o[:, h, :], state(t - 1)[:, c], qa[:, h, cols(t)], start=False, stop=True)
                    else:
                        for rows, st, lo, n in ((slice(0, N_SAMPLE), states_hi[:, 2], SMP0, N_SAMPLE),
                                                (slice(N_SAMPLE, ROWS[4]), state(3), TAIL0, TAIL)):
                            mm(o[:, h, rows], va[rows, 4, c], att[rows, 4, h, rows], start=True, stop=False)
                            last = mm(o[:, h, rows], st[:, c], qa[:, h, lo:lo + n], start=False, stop=True)
                last.then_inc(s["head_mm"], 1)
            for h in range(HEADS):
                pe.wait_ge(s["osq_done"], h + 1)
                if h == 0:
                    pe.wait_ge(s["sample_state"], 1)
                    pe.wait_ge(s["state_done"], 5)
                for t in range(TILES):
                    last = mm(ps[0:ROWS[t], 0, 4 * t + h:4 * t + h + 1], square[:, h % 2, t * P:t * P + ROWS[t]],
                              ones[:, 0:1], start=True, stop=True)
                last.then_inc(s["osum_mm"], 1)
            for h in range(HEADS):
                pe.wait_ge(s["odiag_done"], h + 1)
                if h >= 2:
                    pe.wait_ge(s["oa_done"], h - 1)
                if h == 0:
                    pe.wait_ge(s["head_evac"], TILES)
                at = (4 + 2 * (h % 2)) * 512
                for lo, n in ((0, MAIN), (MAIN, NT - MAIN)):
                    last = mm(psf[:, at + lo:at + lo + n], ones[:], o_diag[h % 2][:, lo:lo + n], start=True, stop=True)
                last.then_inc(s["ospread_mm"], 1)
            def logits(t, heads):
                r = ROWS[t]
                for h in heads:
                    n = t * HEADS + h
                    if n >= 2:
                        pe.wait_ge(s["masked_done"], n - 1)
                    elif n == 0:
                        pe.wait_ge(s["oroot_done"], 1)
                    bank = 2 * (h % 2)
                    q = qt[:, h, cols(t)]
                    w = min(WIDTH[t], MAIN)
                    last = mm(ps[0:r, bank, 0:w], q, kt[:, 0:w], start=True, stop=True)
                    if WIDTH[t] > MAIN:
                        last = mm(ps[0:r, bank + 1, 0:TAIL], q, kt[:, TAIL0:NT], start=True, stop=True)
                    if t == 4:
                        q = qt[:, h, SMP0:TAIL0]
                        mm(ps[0:N_SAMPLE, bank, 0:PAST], q, cache[:, 0, :], start=True, stop=True)
                        last = mm(ps[0:N_SAMPLE, bank, PAST:PAST + N_SAMPLE], q, kt[:, SMP0:TAIL0], start=True,
                                  stop=True)
                    last.then_inc(s["logit_mm"], 1)

            ev = 0
            logits(0, range(HEADS))
            for t in range(TILES):
                r = ROWS[t]
                if t + 1 < TILES:
                    logits(t + 1, (0, 1))
                for kw, kc, parts in key_chunks(t):
                    if ev == 0:
                        pe.wait_ge(s["oa_done"], HEADS)
                    if ev >= 2:
                        pe.wait_ge(s["pt_evac"], ev - 1)
                    for h in range(HEADS):
                        pe.wait_ge(s["p_done"], t * HEADS + h + 1)
                        last = nc.tensor.transpose(ps[0:kw, 4 + ev % 2, h * P:h * P + r], probs[t % 2][0:r, h, kc:kc + kw],
                                                   ident[0:r, 0:r])
                    last.then_inc(s["pt_mm"], 1)
                    ev += 1
                if t + 1 < TILES:
                    logits(t + 1, (2, 3))
                pe.wait_ge(s["pt_evac"], ev)
                if t == 0:
                    pe.wait_ge(s["head_evac"], TILES)
                if t >= 2:
                    pe.wait_ge(s["pv_evac"], t - 1)
                out = ps[:, 6 + t % 2, :].rearrange("p (h n) -> p h n", h=HEADS)
                chunks = key_chunks(t)
                if t < 4:
                    for c, (kw, kc, parts) in enumerate(chunks):
                        vk = v_tail[0:TAIL] if kc == MAIN else vb[0:kw, c]
                        last = mm(out, vk, probs_t[0:kw, c], start=(c == 0), stop=(c == len(chunks) - 1))
                else:
                    tail = slice(N_SAMPLE, ROWS[4])
                    for c in range(5):
                        kw = P if c < 4 else TAIL
                        last = mm(out[:, :, tail], vb[0:kw, c] if c < 4 else v_tail[0:TAIL], probs_t[0:kw, c, :, tail],
                                  start=(c == 0), stop=(c == 4))
                    smp = slice(0, N_SAMPLE)
                    mm(out[:, :, smp], cache[:, 2, :], probs_t[:, 0, :, smp], start=True, stop=False)
                    last = mm(out[:, :, smp], vb[0:N_SAMPLE, 4], probs_t[0:N_SAMPLE, 1, :, smp], start=False, stop=True)
                last.then_inc(s["pv_mm"], 1)
            pe.wait_ge(s["pv_evac"], TILES)
            pe.wait_ge(s["oa_done"], HEADS)
            pe.wait_ge(s["masked_done"], TILES * HEADS)
            pe.wait_ge(s["pt_evac"], ev)
            pe.wait_ge(s["w_out_in"], 16)
            for u in range(OUT_UNITS):
                pe.wait_ge(resid_done, u + DC + 1)
                w = w_out[:, u, :].rearrange("p (c n) -> p c n", c=DC)
                for c in range(DC):
                    last = product(4 * (u % 2), w[:, c, :], normed[:, c, :], c, DC)
                last.then_inc(unit_done, 1)
            sum_squares(2)
            ffn(2)
            ffn(3)
            pe.wait_ge(sumsq_zero, 5)
            for t in range(TILES):
                mm(ps[:, 2, t:t + 1], square_sum[:, t * P:(t + 1) * P], ones[:, 0:1], start=(t == 0), stop=False)

            def add_column_sums(c):
                pe.wait_ge(square_done, c + 5 * DC + 1)
                for t in reversed(range(TILES)):
                    last = mm(ps[0:ROWS[t], 2, t:t + 1], square[:, c % 2, t * P:t * P + ROWS[t]], ones[:, 0:1],
                              start=False, stop=(c == DC - 1 and t == 0))
                last.then_inc(sumsq_done, 1)
                if c == DC - 1:
                    last = mm(ps[0:1, 3, 0:1], ones[:, 0:1], ones[:, 0:1], start=True, stop=True)
                    last.then_inc(sumall_done, 1)

            pe.wait_ge(s["pool_in"], 48)
            for c in range(DC):
                gi, m = c // 2, c % 2
                pe.wait_ge(s["pwin_done"], gi + 1)
                if c >= 3:
                    pe.wait_ge(resid_done, DC * 4 + c)
                for k in range(2):
                    last = product(POOL_BANKS[c % 3], w_pool[:, gi, k, m, :], pooled[:, 2 * gi + k, :], k, 2)
                last.then_inc(s["pool_mm"], 1)
                if c >= 3:
                    add_column_sums(c - 3)
            for c in range(DC - 3, DC):
                add_column_sums(c)
            spread(5)
            ffn(5, last_stage=True)



POOL_BANKS = (0, 4, 6)


NORMED = {0: 0, 1: 1, 2: 2, 3: 3, 5: 4}
LEVEL_PASSES = [x for x in PASSES if x[0] in ("level", "diag")]


def key_chunks(t):
    if t < 4:
        w = WIDTH[t]
        return [(min(P, w - k), k, [(0, P)]) for k in range(0, w, P)]
    return [(P, k, [(0, ROWS[4])]) for k in range(0, MAIN, P)] + [(TAIL, MAIN, [(0, ROWS[4])])]


def head_square_sums(mm, ps, square, ones, h, s):
    for t in range(TILES):
        last = mm(ps[0:ROWS[t], 4, 4 * t + h:4 * t + h + 1], square[:, (h + 1) % 2, t * P:t * P + ROWS[t]],
                  ones[:, 0:1], start=True, stop=True)
    last.then_inc(s["qsum_mm"], 1)


def token_order():
    return np.r_[0:MAIN, TAIL0:NT], np.arange(SMP0, TAIL0)


def rope_tables(dim, heads_in_chunk):
    half = dim // 8
    inv = (np.float32(ROPE_THETA) ** (-np.arange(half, dtype=np.float32) / np.float32(half))).astype(np.float32)
    pos = np.zeros(NT, np.float32)
    prompt, sample = token_order()
    pos[prompt] = np.arange(N_PROMPT)
    pos[sample] = PAST + np.arange(N_SAMPLE)
    ang = (pos[None, :] * inv[:, None]).astype(np.float32).astype(np.float64)
    cos, sin = np.ones((dim, NT)), np.zeros((dim, NT))
    cos[:half] = cos[half:2 * half] = np.cos(ang)
    sin[:half], sin[half:2 * half] = -np.sin(ang), np.sin(ang)
    table = np.stack([np.tile(cos, (heads_in_chunk, 1)), np.tile(sin, (heads_in_chunk, 1))], 1)
    perm = np.arange(P)
    for k in range(heads_in_chunk):
        o = k * dim
        perm[o:o + 2 * half] = o + np.r_[half:2 * half, 0:half]
    return table.astype(np.float32), np.eye(P, dtype=np.float32)[perm]


def shape_constants():
    rope_idx, perm_idx = rope_tables(IDX_DIM, 2)
    rope_head, perm_head = rope_tables(DH, 1)
    i = np.arange(P)
    src, dst = i[:, None], i[None, :]
    masks = [(src // (2 * h) == dst // (2 * h)) & (src % (2 * h) < h) & (dst % (2 * h) >= h) for h in LEVELS]
    masks.append(src == dst)
    bound = np.where(i < 16, 16, np.where(i < 80, 80, 144))
    adm = np.where(np.arange(144)[None, :] < bound[:, None], 0.0, NEG_BIG).astype(np.float32)
    pos = np.arange(16)
    inv_cnt = np.stack([1.0 / np.minimum(w, pos + 1) for w in POOL_WINDOWS]).astype(np.float32)
    return {
        "ident": np.eye(P, dtype=np.float32), "masks": np.stack(masks, 1).astype(np.float32), "adm": adm,
        "rope_idx": rope_idx, "rope_head": rope_head, "perms": np.stack([perm_idx, perm_head], 1),
        "inv_cnt": np.ascontiguousarray(np.broadcast_to(inv_cnt, (P, 4, 16))),
    }


def chunked(a):
    return a.reshape(-1, P, *a.shape[1:]).swapaxes(0, 1)


def units(w):
    k, n = w.shape
    return w.reshape(k // P, P, n // P, P).transpose(2, 1, 0, 3).reshape(n // P, P, k)


_OUTS = {"y": (P, DC, NT), "k": (P, NT), "v": (P, TILES, DH), "ki": (IDX_DIM, NT), "hgrn_p": (P, HEADS * DH),
         "hgrn_s": (P, HEADS * DH), "pool_p": (P, DC, POOL_HIST), "pool_s": (P, DC, POOL_HIST)}


def kernel(**inputs):
    import concourse.bacc as _bacc
    from concourse.bass_utils import run_bass_kernel_spmd as _run

    i = {k: np.asarray(v) for k, v in inputs.items()}
    prompt, sample = token_order()
    x = np.empty((NT, D_MODEL), np.float32)
    x[prompt] = np.concatenate([i["meta_tokens"], i["x_prompt"][0]])
    x[sample] = i["x_sample"][0]
    w_in = i["ab_w_in"][0]
    c = np.cumsum((0, 512, 512, 512, 512, 512, 128, 128, 256, 64, 4))
    aq, af, ai, ag, bq, bk, bv, bqi, bki, bw = (w_in[:, c[n]:c[n + 1]] for n in range(10))
    gains = np.stack([i["norm_ffn1"][0], i["norm_mix"][0], i["norm_ffn2"][0],
                      i["norm_ffn1"][1], i["norm_mix"][1], i["norm_ffn2"][1]])
    cki = i["cache_ki"][0, 0].T
    arrays = {
        "x": chunked(x.T), "gains": gains.reshape(6, DC, P).transpose(2, 0, 1),
        "w_up": np.stack([np.stack([units(i[n + "_wg"][l]), units(i[n + "_wu"][l])], 2).reshape(FC, P, 2 * DC * P)
                          for l in range(2) for n in ("ffn1", "ffn2")]),
        "w_dn": np.stack([units(i[n + "_wd"][l]) for l in range(2) for n in ("ffn1", "ffn2")]),
        "w_in": units(np.concatenate([bki, bki, bqi, bk, bq, af, aq, ag], 1)),
        "w_vw": chunked(np.concatenate([bv, bw], 1)), "w_ai": chunked(ai), "w_out": units(i["ab_w_out"][0]).swapaxes(0, 1),
        "lb_logits": i["hgrn_lb_logits"].reshape(HEADS, P).T,
        "cgain": np.concatenate([i["attn_q_norm"], i["attn_k_norm"], i["attn_q_norm"], i["attn_k_norm"],
                                 i["hgrn_out_norm"].reshape(HEADS, P)]).T,
        "pool_scale": i["pool_scale"].reshape(DC, P).T,
        "cache": np.stack([i["cache_k"][0, 0].T, np.concatenate([cki, cki]), i["cache_v"][0, 0]], 1),
        "state": i["state_hgrn"][0, 0].transpose(1, 0, 2).reshape(P, HEADS * DH),
        "state_pool": chunked(i["state_pool"][0, 0].T),
        "w_pool": i["pool_w"][0].reshape(4, 2, P, 2, P).transpose(2, 0, 1, 3, 4).reshape(P, 4, 2, 2, P),
        **shape_constants(),
    }
    arrays = {k: np.ascontiguousarray(v) for k, v in arrays.items()}
    nc = _bacc.Bacc("TRN2", target_bir_lowering=False, num_devices=1)
    d = {k: nc.dram_tensor("in_" + k, v.shape, mybir.dt.from_np(v.dtype), kind="ExternalInput").ap()
         for k, v in arrays.items()}
    d |= {k: nc.dram_tensor("out_" + k, v, F32, kind="ExternalOutput").ap() for k, v in _OUTS.items()}
    build(nc, d)
    r = _run(nc, [{"in_" + k: v for k, v in arrays.items()}], core_ids=[0]).results[0]
    o = {k: r["out_" + k] for k in _OUTS}

    def tokens(a):
        a = a.transpose(2, 1, 0).reshape(NT, -1)
        return a[prompt], a[sample]

    y_p, y_s = tokens(o["y"])
    k_p, k_s = tokens(o["k"][:, None])
    ki_p, ki_s = tokens(o["ki"][:, None])
    v_rows = o["v"].transpose(1, 0, 2)
    v_all = np.concatenate([v_rows[:4].reshape(MAIN, DH), v_rows[4, :ROWS[4]]])
    v_p, v_s = v_all[prompt], v_all[sample]

    def states(a):
        return a.reshape(P, HEADS, DH).transpose(1, 0, 2)[None, None]

    def hist(a):
        return a.transpose(2, 1, 0).reshape(POOL_HIST, D_MODEL)[None, None]

    out = (y_p[N_META:][None], y_s[None], k_p[None, None], v_p[None, None], ki_p[None, None], states(o["hgrn_p"]),
           hist(o["pool_p"]), k_s[None, None], v_s[None, None], ki_s[None, None], states(o["hgrn_s"]),
           hist(o["pool_s"]))
    return tuple(np.ascontiguousarray(a) for a in out)
```
